# Optimizing a Trainium2 kernel written in Bass

```python
import jax, jax.numpy as jnp
from jax import lax
import numpy as np

D_MODEL = 1024
BATCH = 1
SEQ = 256
DEPTH = 2

MLA_HEADS = 6
MLA_NOPE = 64
MLA_ROPE = 32
MLA_V = 64
MLA_Q_RANK = 256
MLA_KV_RANK = 128
ATTN_Q_BLOCK = 128
RET_HEADS = 5
RET_DK = 64
RET_DV = 64
RET_CHUNK = 128
MOBA_HEADS = 5
MOBA_DH = 64
MOBA_BLOCK = 256
MOBA_TOPK = 3
MOBA_Q_CHUNK = 64
ROPE_THETA = 10000.0
LN_EPS = 1e-5
RMS_EPS = 1e-6
D_FF = 2816
N_EXPERTS = 8
TOP_K = 2
D_FF_EXPERT = 3584
DN_ALPHA = (2 * DEPTH) ** 0.25
DN_BETA = (8 * DEPTH) ** -0.25

W_MLA_OUT = MLA_HEADS * MLA_V
W_RET_OUT = RET_HEADS * RET_DV
W_MOBA_OUT = MOBA_HEADS * MOBA_DH
MIX_WIDTH = W_MLA_OUT + W_RET_OUT + W_MOBA_OUT
IN_SIZES = (MLA_Q_RANK, MLA_KV_RANK, MLA_ROPE,
            RET_HEADS * RET_DK, RET_HEADS * RET_DK, RET_HEADS * RET_DV, RET_HEADS * RET_DV,
            MOBA_HEADS * MOBA_DH, MOBA_HEADS * MOBA_DH, MOBA_HEADS * MOBA_DH)
D_IN = sum(IN_SIZES)
N_DENSE = (DEPTH + 1) // 2
N_MOE = DEPTH // 2


def layer_norm(x, g, b):
    xf = x.astype(jnp.float32)
    mu = jnp.mean(xf, -1, keepdims=True)
    var = jnp.mean(jnp.square(xf - mu), -1, keepdims=True)
    return ((xf - mu) * lax.rsqrt(var + LN_EPS) * g.astype(jnp.float32) + b.astype(jnp.float32)).astype(x.dtype)

def rms_norm(x, g):
    xf = x.astype(jnp.float32)
    y = xf * lax.rsqrt(jnp.mean(jnp.square(xf), -1, keepdims=True) + RMS_EPS)
    return (y * g.astype(jnp.float32)).astype(x.dtype)

def rope_tables(n_pos, dim):
    pos = jnp.arange(n_pos, dtype=jnp.float32)
    inv = ROPE_THETA ** (-jnp.arange(0, dim, 2, dtype=jnp.float32) / dim)
    ang = pos[:, None] * inv[None, :]
    return jnp.cos(ang), jnp.sin(ang)

def apply_rope(x, cos, sin):
    shp = (1, cos.shape[0]) + (1,) * (x.ndim - 3) + (cos.shape[1],)
    c = cos.reshape(shp).astype(x.dtype)
    s = sin.reshape(shp).astype(x.dtype)
    x1, x2 = jnp.split(x, 2, axis=-1)
    return jnp.concatenate([x1 * c - x2 * s, x1 * s + x2 * c], axis=-1)

def mla_attention(c_q, c_kv, k_rope, q_norm_g, kv_norm_g, w_uq, w_ukv, cos, sin):
    B, S, _ = c_q.shape
    H, QB = MLA_HEADS, ATTN_Q_BLOCK
    q = (rms_norm(c_q, q_norm_g) @ w_uq).reshape(B, S, H, MLA_NOPE + MLA_ROPE)
    q_nope = q[..., :MLA_NOPE]
    q_pe = apply_rope(q[..., MLA_NOPE:], cos, sin)
    kv = (rms_norm(c_kv, kv_norm_g) @ w_ukv).reshape(B, S, H, MLA_NOPE + MLA_V)
    k_nope, v = kv[..., :MLA_NOPE], kv[..., MLA_NOPE:]
    k_pe = apply_rope(k_rope, cos, sin)
    scale = (MLA_NOPE + MLA_ROPE) ** -0.5
    nq = S // QB
    qn_blocks = q_nope.reshape(B, nq, QB, H, MLA_NOPE).transpose(1, 0, 2, 3, 4)
    qp_blocks = q_pe.reshape(B, nq, QB, H, MLA_ROPE).transpose(1, 0, 2, 3, 4)
    k_pos = jnp.arange(S)

    def block(args):
        qn, qp, start = args
        s = (jnp.einsum('bqhd,bkhd->bhqk', qn, k_nope)
             + jnp.einsum('bqhd,bkd->bhqk', qp, k_pe)).astype(jnp.float32) * scale
        q_pos = start + jnp.arange(QB)
        s = jnp.where(k_pos[None, :] <= q_pos[:, None], s, -jnp.inf)
        p = jax.nn.softmax(s, axis=-1).astype(v.dtype)
        return jnp.einsum('bhqk,bkhd->bqhd', p, v)

    o = lax.map(block, (qn_blocks, qp_blocks, jnp.arange(nq) * QB))
    return o.transpose(1, 0, 2, 3, 4).reshape(B, S, W_MLA_OUT)

def retention(q, k, v, g, cos, sin):
    B, S, _ = q.shape
    H, C = RET_HEADS, RET_CHUNK
    nc = S // C
    f32 = jnp.float32
    q = apply_rope(q.reshape(B, S, H, RET_DK), cos, sin)
    k = apply_rope(k.reshape(B, S, H, RET_DK), cos, sin) * (RET_DK ** -0.5)
    v = v.reshape(B, S, H, RET_DV)
    log_gamma = jnp.log(1.0 - 2.0 ** (-5.0 - jnp.arange(H, dtype=f32)))
    qc = q.reshape(B, nc, C, H, RET_DK)
    kc = k.reshape(B, nc, C, H, RET_DK)
    vc = v.reshape(B, nc, C, H, RET_DV)
    idx = jnp.arange(C, dtype=f32)
    diff = idx[:, None] - idx[None, :]
    decay_in = jnp.where(diff >= 0, jnp.exp(log_gamma[:, None, None] * jnp.maximum(diff, 0.0)), 0.0)
    intra = jnp.einsum('bnihd,bnjhd->bnhij', qc, kc).astype(f32) * decay_in
    o_intra = jnp.einsum('bnhij,bnjhe->bnihe', intra.astype(v.dtype), vc).astype(f32)
    k_decay = jnp.exp(log_gamma[:, None] * (C - 1.0 - idx))
    kv = jnp.einsum('bnjhd,hj,bnjhe->nbhde', kc.astype(f32), k_decay, vc.astype(f32))
    chunk_decay = jnp.exp(log_gamma * C)[None, :, None, None]

    def step(R, kv_n):
        return R * chunk_decay + kv_n, R

    _, R_prev = lax.scan(step, jnp.zeros((B, H, RET_DK, RET_DV), f32), kv)
    q_decay = jnp.exp(log_gamma[:, None] * (idx + 1.0))
    o_cross = jnp.einsum('bnihd,nbhde,hi->bnihe', qc.astype(f32), R_prev, q_decay)
    o = (o_intra + o_cross).reshape(B, S, H, RET_DV)
    mu = jnp.mean(o, -1, keepdims=True)
    var = jnp.mean(jnp.square(o - mu), -1, keepdims=True)
    o = ((o - mu) * lax.rsqrt(var + RMS_EPS)).reshape(B, S, W_RET_OUT)
    return (jax.nn.silu(g.astype(f32)) * o).astype(q.dtype)

def moba_attention(q, k, v):
    B, S, _ = q.shape
    H, dh, BLK, QC = MOBA_HEADS, MOBA_DH, MOBA_BLOCK, MOBA_Q_CHUNK
    f32 = jnp.float32
    nb = -(-S // BLK)
    Sp = nb * BLK
    pad = Sp - S

    def heads(t):
        t = jnp.pad(t.reshape(B, S, H, dh), ((0, 0), (0, pad), (0, 0), (0, 0)))
        return t.transpose(0, 2, 1, 3)

    q, k, v = heads(q), heads(k), heads(v)
    k_blk = k.reshape(B, H, nb, BLK, dh)
    v_blk = v.reshape(B, H, nb, BLK, dh)
    k_mean = jnp.mean(k_blk.astype(f32), axis=3)
    slopes = 2.0 ** (-8.0 * (jnp.arange(H, dtype=f32) + 1.0) / H)
    n_sel = min(MOBA_TOPK, nb - 1)
    scale = dh ** -0.5
    nqc = Sp // QC
    q_chunks = q.reshape(B, H, nqc, QC, dh).transpose(2, 0, 1, 3, 4)
    bi = jnp.arange(B)[:, None, None, None]
    hi = jnp.arange(H)[None, :, None, None]
    blk_off = jnp.arange(BLK)

    def chunk(args):
        qc, start = args
        blk = start // BLK
        q_pos = start + jnp.arange(QC)
        k_own = lax.dynamic_index_in_dim(k_blk, blk, axis=2, keepdims=False)
        v_own = lax.dynamic_index_in_dim(v_blk, blk, axis=2, keepdims=False)
        own_pos = blk * BLK + blk_off
        s_own = (jnp.einsum('bhqd,bhkd->bhqk', qc, k_own).astype(f32) * scale
                 - slopes[:, None, None] * (q_pos[:, None] - own_pos[None, :]).astype(f32))
        s_own = jnp.where(own_pos[None, :] <= q_pos[:, None], s_own, -jnp.inf)
        if n_sel == 0:
            p = jax.nn.softmax(s_own, axis=-1).astype(v.dtype)
            return jnp.einsum('bhqk,bhkd->bhqd', p, v_own)
        gate = jnp.einsum('bhqd,bhnd->bhqn', qc.astype(f32), k_mean)
        gate = jnp.where(jnp.arange(nb) < blk, gate, -jnp.inf)
        _, sel = lax.top_k(gate, n_sel)
        k_sel = k_blk[bi, hi, sel]
        v_sel = v_blk[bi, hi, sel]
        sel_pos = sel[..., None] * BLK + blk_off
        s_sel = (jnp.einsum('bhqd,bhqnkd->bhqnk', qc, k_sel).astype(f32) * scale
                 - slopes[:, None, None, None] * (q_pos[:, None, None] - sel_pos).astype(f32))
        slot_ok = jnp.arange(n_sel) < blk
        s_sel = jnp.where(slot_ok[:, None], s_sel, -jnp.inf)
        s_all = jnp.concatenate([s_sel.reshape(B, H, QC, n_sel * BLK), s_own], axis=-1)
        p = jax.nn.softmax(s_all, axis=-1).astype(v.dtype)
        p_sel = p[..., :n_sel * BLK].reshape(B, H, QC, n_sel, BLK)
        return (jnp.einsum('bhqnk,bhqnkd->bhqd', p_sel, v_sel)
                + jnp.einsum('bhqk,bhkd->bhqd', p[..., n_sel * BLK:], v_own))

    o = lax.map(chunk, (q_chunks, jnp.arange(nqc) * QC))
    o = o.transpose(1, 0, 3, 2, 4).reshape(B, Sp, W_MOBA_OUT)
    return o[:, :S]

def hybrid_mixer(x, w_in, q_norm_g, kv_norm_g, w_uq, w_ukv, beta_mla, beta_moba, w_o,
                 cos_a, sin_a, cos_b, sin_b):
    h = x @ w_in
    splits = [int(s) for s in np.cumsum(IN_SIZES)[:-1]]
    c_q, c_kv, k_rope, rq, rk, rv, rg, mq, mk, mv = jnp.split(h, splits, axis=-1)
    o_a = rms_norm(mla_attention(c_q, c_kv, k_rope, q_norm_g, kv_norm_g, w_uq, w_ukv, cos_a, sin_a), beta_mla)
    o_b = retention(rq, rk, rv, rg, cos_b, sin_b)
    o_c = rms_norm(moba_attention(mq, mk, mv), beta_moba)
    return jnp.concatenate([o_a, o_b, o_c], axis=-1) @ w_o

def swiglu(x, w_gate, w_up, w_down):
    return (jax.nn.silu(x @ w_gate) * (x @ w_up)) @ w_down

def moe_swiglu(x, w_router, w_gate, w_up, w_down):
    B, S, D = x.shape
    xt = x.reshape(B * S, D)
    logits = (xt @ w_router).astype(jnp.float32)
    top_v, top_i = lax.top_k(logits, TOP_K)
    top_w = jax.nn.softmax(top_v, axis=-1)
    gates = jnp.sum(jax.nn.one_hot(top_i, N_EXPERTS, dtype=jnp.float32) * top_w[..., None], axis=1)
    y = jnp.zeros((B * S, D), jnp.float32)
    for e in range(N_EXPERTS):
        y = y + gates[:, e:e + 1] * swiglu(xt, w_gate[e], w_up[e], w_down[e]).astype(jnp.float32)
    return y.astype(x.dtype).reshape(B, S, D)

def first_inputs(seed: int = 0) -> dict:
    key = jax.random.key(seed)
    ks = jax.random.split(key, 24)
    f32 = jnp.float32
    nrm = lambda k, shp, s: jax.random.normal(k, shp, f32) * s
    x = jax.random.normal(ks[0], (BATCH, SEQ, D_MODEL), f32)
    col_scale = jnp.concatenate([
        jnp.full((s,), DN_BETA if i in (5, 9) else 1.0, f32) for i, s in enumerate(IN_SIZES)])
    w_in = nrm(ks[1], (DEPTH, D_MODEL, D_IN), D_MODEL ** -0.5) * col_scale
    ukv_scale = jnp.tile(jnp.concatenate([jnp.ones((MLA_NOPE,), f32), jnp.full((MLA_V,), DN_BETA, f32)]), MLA_HEADS)
    return {
        "x": x,
        "ln_emb_g": 1.0 + nrm(ks[2], (D_MODEL,), 0.02),
        "ln_emb_b": nrm(ks[3], (D_MODEL,), 0.02),
        "w_in": w_in,
        "q_norm_g": 1.0 + nrm(ks[4], (DEPTH, MLA_Q_RANK), 0.02),
        "kv_norm_g": 1.0 + nrm(ks[5], (DEPTH, MLA_KV_RANK), 0.02),
        "w_uq": nrm(ks[6], (DEPTH, MLA_Q_RANK, MLA_HEADS * (MLA_NOPE + MLA_ROPE)), MLA_Q_RANK ** -0.5),
        "w_ukv": nrm(ks[7], (DEPTH, MLA_KV_RANK, MLA_HEADS * (MLA_NOPE + MLA_V)), MLA_KV_RANK ** -0.5) * ukv_scale,
        "beta_mla": 1.0 + nrm(ks[8], (DEPTH, W_MLA_OUT), 0.02),
        "beta_moba": 1.0 + nrm(ks[9], (DEPTH, W_MOBA_OUT), 0.02),
        "w_o": nrm(ks[10], (DEPTH, MIX_WIDTH, D_MODEL), MIX_WIDTH ** -0.5 * DN_BETA),
        "ln1_g": 1.0 + nrm(ks[11], (DEPTH, D_MODEL), 0.02),
        "ln1_b": nrm(ks[12], (DEPTH, D_MODEL), 0.02),
        "ffn_w_gate": nrm(ks[13], (N_DENSE, D_MODEL, D_FF), D_MODEL ** -0.5 * DN_BETA),
        "ffn_w_up": nrm(ks[14], (N_DENSE, D_MODEL, D_FF), D_MODEL ** -0.5 * DN_BETA),
        "ffn_w_down": nrm(ks[15], (N_DENSE, D_FF, D_MODEL), D_FF ** -0.5 * DN_BETA),
        "router": nrm(ks[16], (N_MOE, D_MODEL, N_EXPERTS), D_MODEL ** -0.5),
        "exp_w_gate": nrm(ks[17], (N_MOE, N_EXPERTS, D_MODEL, D_FF_EXPERT), D_MODEL ** -0.5 * DN_BETA),
        "exp_w_up": nrm(ks[18], (N_MOE, N_EXPERTS, D_MODEL, D_FF_EXPERT), D_MODEL ** -0.5 * DN_BETA),
        "exp_w_down": nrm(ks[19], (N_MOE, N_EXPERTS, D_FF_EXPERT, D_MODEL), D_FF_EXPERT ** -0.5 * DN_BETA),
        "ln2_g": 1.0 + nrm(ks[20], (DEPTH, D_MODEL), 0.02),
        "ln2_b": nrm(ks[21], (DEPTH, D_MODEL), 0.02),
    }

def first_block(x, ln_emb_g, ln_emb_b, w_in, q_norm_g, kv_norm_g, w_uq, w_ukv, beta_mla, beta_moba,
              w_o, ln1_g, ln1_b, ffn_w_gate, ffn_w_up, ffn_w_down, router, exp_w_gate, exp_w_up,
              exp_w_down, ln2_g, ln2_b):
    S = x.shape[1]
    cos_a, sin_a = rope_tables(S, MLA_ROPE)
    cos_b, sin_b = rope_tables(S, RET_DK)
    x = layer_norm(x, ln_emb_g, ln_emb_b)
    for l in range(DEPTH):
        mix = hybrid_mixer(x, w_in[l], q_norm_g[l], kv_norm_g[l], w_uq[l], w_ukv[l],
                           beta_mla[l], beta_moba[l], w_o[l], cos_a, sin_a, cos_b, sin_b)
        x = layer_norm(DN_ALPHA * x + mix, ln1_g[l], ln1_b[l])
        if l % 2 == 0:
            j = l // 2
            f = swiglu(x, ffn_w_gate[j], ffn_w_up[j], ffn_w_down[j])
        else:
            j = l // 2
            f = moe_swiglu(x, router[j], exp_w_gate[j], exp_w_up[j], exp_w_down[j])
        x = layer_norm(DN_ALPHA * x + f, ln2_g[l], ln2_b[l])
    return x


DEPTH_2 = 1

N_MEM = 256
D_MIX = D_MODEL
D_SGU = D_MIX // 2
D_ATT = D_MIX - D_SGU
SGU_GROUPS = 8
SGU_GROUP_DIM = D_SGU // SGU_GROUPS
CHUNK = 128
N_HEADS = 8
HEAD_DIM = D_ATT // N_HEADS
DILATED_CONFIGS = ((128, 1), (512, 4), (2048, 16))
ROPE_THETA_2 = 500000.0
ROPE_DIM = HEAD_DIM // 4
X_HEADS = 4
X_HEAD_DIM = D_MODEL // X_HEADS
D_IN_2 = 2 * D_SGU + 3 * D_ATT
NORM_EPS = 1e-6
MAX_POS_OFFSET = 4096


F32 = jnp.float32

def rmsnorm(t, g):
    tf = t.astype(F32)
    y = tf * lax.rsqrt(jnp.mean(tf * tf, axis=-1, keepdims=True) + NORM_EPS)
    return (y * g.astype(F32)).astype(t.dtype)

def group_layernorm(t, g, b):
    G, C = t.shape[-2], t.shape[-1]
    tf = t.astype(F32)
    mu = jnp.mean(tf, axis=-1, keepdims=True)
    d = tf - mu
    y = d * lax.rsqrt(jnp.mean(d * d, axis=-1, keepdims=True) + LN_EPS)
    return (y * g.astype(F32).reshape(G, C) + b.astype(F32).reshape(G, C)).astype(t.dtype)

def swiglu_2(h, w_gate, w_up, w_down):
    return (jax.nn.silu(h @ w_gate) * (h @ w_up)) @ w_down

def partial_rotary(t, positions):
    half = ROPE_DIM // 2
    inv_freq = ROPE_THETA_2 ** (-2.0 * jnp.arange(half, dtype=F32) / ROPE_DIM)
    ang = positions.astype(F32)[..., None] * inv_freq
    cos = jnp.cos(ang)[:, :, None, :]
    sin = jnp.sin(ang)[:, :, None, :]
    tf = t.astype(F32)
    x1 = tf[..., :half]
    x2 = tf[..., half:ROPE_DIM]
    out = jnp.concatenate([x1 * cos - x2 * sin, x2 * cos + x1 * sin, tf[..., ROPE_DIM:]], axis=-1)
    return out.astype(t.dtype)

def chunked_spatial_gating(z, ln_g, ln_b, w_s, b_s):
    b, s, _ = z.shape
    u, v = z[..., :D_SGU], z[..., D_SGU:]
    v = group_layernorm(v.reshape(b, s, SGU_GROUPS, SGU_GROUP_DIM), ln_g, ln_b)
    v = v.reshape(b, s // CHUNK, CHUNK, SGU_GROUPS, SGU_GROUP_DIM)
    causal = jnp.tril(jnp.ones((CHUNK, CHUNK), dtype=bool))
    ws = w_s * causal.astype(w_s.dtype)
    mixed = jnp.einsum('gij,bnjgc->bnigc', ws, v) + b_s.T[:, :, None]
    return u * mixed.reshape(b, s, D_SGU)

def dilated_window_attention(q, k, v, window, dilation):
    b, s, h, e = q.shape
    band = window // dilation
    L = s // dilation
    nb = -(-L // band)
    Lp = nb * band
    qs = q.reshape(b, L, dilation, h, e)
    ks = k.reshape(b, L, dilation, h, e)
    vs = v.reshape(b, L, dilation, h, e)
    qb = jnp.pad(qs, ((0, 0), (0, Lp - L), (0, 0), (0, 0), (0, 0))).reshape(b, nb, band, dilation, h, e)

    def kv_blocks(t):
        t = jnp.pad(t, ((0, 0), (band, Lp - L), (0, 0), (0, 0), (0, 0))).reshape(b, nb + 1, band, dilation, h, e)
        return jnp.concatenate([t[:, :-1], t[:, 1:]], axis=2)

    kb, vb = kv_blocks(ks), kv_blocks(vs)
    scores = jnp.einsum('bnqrhe,bnkrhe->bnrhqk', qb.astype(F32), kb.astype(F32)) * (e ** -0.5)
    qi = jnp.arange(band)[:, None]
    kj = jnp.arange(2 * band)[None, :]
    dist = band + qi - kj
    key_pos = (jnp.arange(nb)[:, None, None] - 1) * band + kj[None]
    mask = ((dist >= 0) & (dist <= band))[None] & (key_pos >= 0)
    scores = jnp.where(mask[None, :, None, None], scores, -jnp.inf)
    lse = jax.nn.logsumexp(scores, axis=-1)
    p = jnp.exp(scores - lse[..., None])
    o = jnp.einsum('bnrhqk,bnkrhe->bnqrhe', p.astype(v.dtype), vb)
    o = o.reshape(b, Lp, dilation, h, e)[:, :L].reshape(b, s, h, e)
    lse = jnp.transpose(lse, (0, 1, 4, 2, 3)).reshape(b, Lp, dilation, h)[:, :L].reshape(b, s, h)
    return o, lse

def dilated_mixture_attention(q, k, v):
    outs, lses = [], []
    for window, dilation in DILATED_CONFIGS:
        o, l = dilated_window_attention(q, k, v, window, dilation)
        outs.append(o)
        lses.append(l)
    wts = jax.nn.softmax(jnp.stack(lses, axis=0), axis=0)
    return jnp.einsum('gbsh,gbshe->bshe', wts.astype(q.dtype), jnp.stack(outs, axis=0))

def memory_cross_attention(h, m, wq, wk, wv, wo):
    b, s, _ = h.shape
    nm = m.shape[1]
    q = (h @ wq).reshape(b, s, X_HEADS, X_HEAD_DIM)
    k = (m @ wk).reshape(b, nm, X_HEADS, X_HEAD_DIM)
    v = (m @ wv).reshape(b, nm, X_HEADS, X_HEAD_DIM)
    scores = jnp.einsum('bshe,bmhe->bhsm', q.astype(F32), k.astype(F32)) * (X_HEAD_DIM ** -0.5)
    p = jax.nn.softmax(scores, axis=-1)
    o = jnp.einsum('bhsm,bmhe->bshe', p.astype(v.dtype), v)
    return o.reshape(b, s, D_MODEL) @ wo

def second_inputs(seed: int = 0) -> dict:
    key = jax.random.key(seed)
    ks = jax.random.split(key, 32)

    def w(k, shape, fan_in):
        return jax.random.normal(k, shape, F32) * (fan_in ** -0.5)

    def gain(k, shape):
        return 1.0 + 0.02 * jax.random.normal(k, shape, F32)

    L = DEPTH_2
    x = jax.random.normal(ks[0], (BATCH, SEQ, D_MODEL), F32)
    mem = jax.random.normal(ks[1], (BATCH, N_MEM, D_MODEL), F32)
    start = jax.random.randint(ks[2], (BATCH, 1), 0, MAX_POS_OFFSET, dtype=jnp.int32)
    positions = (start + jnp.arange(SEQ, dtype=jnp.int32)[None, :]).astype(jnp.int32)
    return {
        "x": x,
        "mem": mem,
        "positions": positions,
        "ffn1_norm": gain(ks[3], (L, D_MODEL)),
        "ffn1_w_gate": w(ks[4], (L, D_MODEL, D_FF), D_MODEL),
        "ffn1_w_up": w(ks[5], (L, D_MODEL, D_FF), D_MODEL),
        "ffn1_w_down": w(ks[6], (L, D_FF, D_MODEL), D_FF),
        "mix_norm": gain(ks[7], (L, D_MODEL)),
        "w_in": w(ks[8], (L, D_MODEL, D_IN_2), D_MODEL),
        "sgu_ln_g": gain(ks[9], (L, D_SGU)),
        "sgu_ln_b": 0.02 * jax.random.normal(ks[10], (L, D_SGU), F32),
        "sgu_w_s": w(ks[11], (L, SGU_GROUPS, CHUNK, CHUNK), CHUNK),
        "sgu_b_s": 1.0 + 0.1 * jax.random.normal(ks[12], (L, SGU_GROUPS, CHUNK), F32),
        "out_norm_a": gain(ks[13], (L, D_SGU)),
        "out_norm_b": gain(ks[14], (L, D_ATT)),
        "w_out": w(ks[15], (L, D_MIX, D_MODEL), D_MIX),
        "cross_norm": gain(ks[16], (L, D_MODEL)),
        "mem_norm": gain(ks[17], (L, D_MODEL)),
        "cross_wq": w(ks[18], (L, D_MODEL, D_MODEL), D_MODEL),
        "cross_wk": w(ks[19], (L, D_MODEL, D_MODEL), D_MODEL),
        "cross_wv": w(ks[20], (L, D_MODEL, D_MODEL), D_MODEL),
        "cross_wo": w(ks[21], (L, D_MODEL, D_MODEL), D_MODEL),
        "ffn2_norm": gain(ks[22], (L, D_MODEL)),
        "ffn2_w_gate": w(ks[23], (L, D_MODEL, D_FF), D_MODEL),
        "ffn2_w_up": w(ks[24], (L, D_MODEL, D_FF), D_MODEL),
        "ffn2_w_down": w(ks[25], (L, D_FF, D_MODEL), D_FF),
        "final_norm": gain(ks[26], (D_MODEL,)),
    }

def second_block(x, mem, positions, ffn1_norm, ffn1_w_gate, ffn1_w_up, ffn1_w_down,
              mix_norm, w_in, sgu_ln_g, sgu_ln_b, sgu_w_s, sgu_b_s,
              out_norm_a, out_norm_b, w_out, cross_norm, mem_norm,
              cross_wq, cross_wk, cross_wv, cross_wo,
              ffn2_norm, ffn2_w_gate, ffn2_w_up, ffn2_w_down, final_norm):
    b, s, _ = x.shape
    for l in range(DEPTH_2):
        h = rmsnorm(x, ffn1_norm[l])
        x = x + 0.5 * swiglu_2(h, ffn1_w_gate[l], ffn1_w_up[l], ffn1_w_down[l])

        h = rmsnorm(x, mix_norm[l])
        z = h @ w_in[l]
        z_sgu = jax.nn.gelu(z[..., :2 * D_SGU], approximate=False)
        o0 = 2 * D_SGU
        q = z[..., o0:o0 + D_ATT].reshape(b, s, N_HEADS, HEAD_DIM)
        k = z[..., o0 + D_ATT:o0 + 2 * D_ATT].reshape(b, s, N_HEADS, HEAD_DIM)
        v = z[..., o0 + 2 * D_ATT:o0 + 3 * D_ATT].reshape(b, s, N_HEADS, HEAD_DIM)
        q = partial_rotary(q, positions)
        k = partial_rotary(k, positions)

        y_a = chunked_spatial_gating(z_sgu, sgu_ln_g[l], sgu_ln_b[l], sgu_w_s[l], sgu_b_s[l])
        y_b = dilated_mixture_attention(q, k, v).reshape(b, s, D_ATT)
        y = jnp.concatenate([rmsnorm(y_a, out_norm_a[l]), rmsnorm(y_b, out_norm_b[l])], axis=-1)
        x = x + y @ w_out[l]

        h = rmsnorm(x, cross_norm[l])
        m = rmsnorm(mem, mem_norm[l])
        x = x + memory_cross_attention(h, m, cross_wq[l], cross_wk[l], cross_wv[l], cross_wo[l])

        h = rmsnorm(x, ffn2_norm[l])
        x = x + 0.5 * swiglu_2(h, ffn2_w_gate[l], ffn2_w_up[l], ffn2_w_down[l])
    return rmsnorm(x, final_norm)


def setup_inputs(seed=0):
    out = dict(first_inputs(seed))
    for name, value in second_inputs(seed + 1).items():
        if name != "x":
            out[name + "_2"] = value
    return out


def reference(
    x, ln_emb_g, ln_emb_b, w_in, q_norm_g, kv_norm_g, w_uq, w_ukv, beta_mla, beta_moba, w_o,
    ln1_g, ln1_b, ffn_w_gate, ffn_w_up, ffn_w_down, router, exp_w_gate, exp_w_up, exp_w_down,
    ln2_g, ln2_b, mem_2, positions_2, ffn1_norm_2, ffn1_w_gate_2, ffn1_w_up_2, ffn1_w_down_2,
    mix_norm_2, w_in_2, sgu_ln_g_2, sgu_ln_b_2, sgu_w_s_2, sgu_b_s_2, out_norm_a_2,
    out_norm_b_2, w_out_2, cross_norm_2, mem_norm_2, cross_wq_2, cross_wk_2, cross_wv_2,
    cross_wo_2, ffn2_norm_2, ffn2_w_gate_2, ffn2_w_up_2, ffn2_w_down_2, final_norm_2,
):
    x = first_block(
        x, ln_emb_g, ln_emb_b, w_in, q_norm_g, kv_norm_g, w_uq, w_ukv, beta_mla, beta_moba, w_o,
        ln1_g, ln1_b, ffn_w_gate, ffn_w_up, ffn_w_down, router, exp_w_gate, exp_w_up,
        exp_w_down, ln2_g, ln2_b,
    )
    return second_block(
        x, mem_2, positions_2, ffn1_norm_2, ffn1_w_gate_2, ffn1_w_up_2, ffn1_w_down_2,
        mix_norm_2, w_in_2, sgu_ln_g_2, sgu_ln_b_2, sgu_w_s_2, sgu_b_s_2, out_norm_a_2,
        out_norm_b_2, w_out_2, cross_norm_2, mem_norm_2, cross_wq_2, cross_wk_2, cross_wv_2,
        cross_wo_2, ffn2_norm_2, ffn2_w_gate_2, ffn2_w_up_2, ffn2_w_down_2, final_norm_2,
    )


_drawn_inputs = setup_inputs


def setup_inputs(seed=0):
    import zlib

    import numpy as np

    out = dict(_drawn_inputs(seed))
    spreads = {}
    factors = {'q_norm_g': 8.0,
     'kv_norm_g': 4.52,
     'beta_mla': 5.297,
     'beta_moba': 7.538,
     'ffn1_norm_2': 6.266,
     'mix_norm_2': 3.067,
     'sgu_ln_g_2': 8.0,
     'sgu_ln_b_2': 8.0,
     'out_norm_a_2': 5.529,
     'out_norm_b_2': 5.196,
     'cross_norm_2': 8.0,
     'mem_norm_2': 8.0,
     'ffn2_norm_2': 8.0,
     'final_norm_2': 2.755}
    for name, (base, spread) in spreads.items():
        noise = np.random.default_rng([zlib.crc32(name.encode()), seed]).standard_normal(out[name].shape)
        drawn = base * np.exp(spread * noise) if base else spread * noise
        out[name] = __import__('jax').numpy.asarray(drawn.astype(out[name].dtype))
    for name, factor in factors.items():
        out[name] = (out[name] * factor).astype(out[name].dtype)
    return out
```

```python
from contextlib import ExitStack
from math import lcm

import numpy as np

import concourse.bass as bass
from concourse import mybir

ALU = mybir.AluOpType
ACT = mybir.ActivationFunctionType
F32 = mybir.dt.float32
F32R = mybir.dt.float32r
I32 = mybir.dt.int32
AX = mybir.AxisListType.X

P = 128
T = 2
S = T * P
D = 1024
KD = D // P
CW = 2048
RAW = 6
SPLIT = 3
LEAD = SPLIT - 1
FU = 256
UNROLL = lcm(RAW, SPLIT, 3) // 3
LB = 3 * UNROLL

DEPTH = 2
ALPHA = (2 * DEPTH) ** 0.25
LN_EPS = 1e-5
RMS_EPS = 1e-6
MLA_H, NOPE, ROPE = 6, 64, 32
QD = NOPE + ROPE
RET_H = MOBA_H = 5
HD = 64
DIL_H = 8
X_H, X_D = 4, 256
D_IN = 2656
D_IN2 = 2560
C_ROPE, C_RQ, C_RK, C_RV, C_RG, C_MQ, C_MK, C_MV = 384, 416, 736, 1056, 1376, 1696, 2016, 2336
O_RET, O_MOBA = 384, 704
D_FF, D_FFE, NE = 2816, 3584, 8
U_FF = D_FF // FU
U_MOE = NE * D_FFE // FU
NEG = -1e30

CONST_PARTS = [("ret", RET_H * S), ("moba", MOBA_H * 384), ("mla", 384), ("dil", 384), ("cos_a", T * 16),
               ("sin_a", T * 16), ("cos_b", T * 32), ("sin_b", T * 32), ("inv_freq", 8), ("ident", P),
               ("tril", P), ("tri8", 64)]
CONST_AT, CONST_W = {}, 0
for _name, _w in CONST_PARTS:
    CONST_AT[_name] = (CONST_W, CONST_W + _w)
    CONST_W += _w

COLS = {}
_n = 0
for _name, _w in [("q0", 2), ("kv0", 1), ("mix0", 8), ("q1", 2), ("kv1", 1), ("mix1", 8), ("ffn1", 8),
                  ("in2", 8), ("out2", 8), ("cross", 8), ("mem", 8), ("ffn2", 8), ("b_s", 8)]:
    COLS[_name] = _n
    _n += _w
NCOL = _n

PROJ = [CW] * 2


def ffn_widths(units):
    return [CW] * (3 * units)


STREAM = []
for _l in range(DEPTH):
    STREAM += [(f"in{_l}", PROJ * 5 + [KD * 96]), (f"uq{_l}", [2 * 576]), (f"ukv{_l}", [768]), (f"o{_l}", PROJ * 2)]
    STREAM += [("f0", ffn_widths(U_FF))] if _l == 0 else [("router", [KD * NE]), ("f1", ffn_widths(U_MOE))]
STREAM += [("f2", ffn_widths(U_FF)), ("in2", PROJ * 5), ("out2", PROJ * 2), ("wk", PROJ * 2), ("wv", PROJ * 2),
           ("wq", PROJ * 2), ("xo", PROJ * 2), ("f3", ffn_widths(U_FF))]
AT, WIDTH = {}, []
for _name, _ws in STREAM:
    AT[_name] = len(WIDTH)
    WIDTH += _ws
NCHUNK = len(WIDTH)
STREAM_LENGTH = [(_name, len(_ws)) for _name, _ws in STREAM]


LAYERS = range(DEPTH)
N_HEADS = RET_H + MOBA_H + MLA_H
N_SOFT = MOBA_H + MLA_H


def _by_layer(*parts, skip=()):
    return [(f"{n}{l}", c) for l in LAYERS for n, c in parts if f"{n}{l}" not in skip]


_ffns = [("f0", U_FF), ("f1", U_MOE), ("f2", U_FF), ("f3", U_FF)]
RAISED = {
    "tr": [("emb", 4)] + _by_layer(("lat", 2), ("mix", 4), ("ln1_", 4), ("ln2_", 4), skip=("ln2_1",))
    + [(n, 4) for n in ("n1", "nmix", "mix2", "nmem", "ncross", "xo", "n2")],
    "xh": [("emb", 4)] + _by_layer(("lat", 3), ("mix", KD), ("ln1_", 4), ("ln2_", 4), skip=("ln2_1",))
    + [(n, 4 if n == "xo" else KD) for n in ("n1", "nmix", "mix2", "nmem", "ncross", "xo", "n2")],
    "xt": [("emb", 4)] + _by_layer(("lat", 2), ("mix", KD), ("ln1_", 4), ("ln2_", 4), skip=("ln2_1",))
    + [(n, 4 if n == "xo" else KD) for n in ("n1", "nmix", "mix2", "nmem", "ncross", "xo", "n2")],
    "sd": [("emb", 1)] + _by_layer(("lat", 1), ("mix", 1), ("ret", 1), ("ln1_", 1), ("ln2_", 1))
    + [(n, 1) for n in ("n1", "nmix", "sgu", "mix2", "nmem", "ncross", "n2", "fin")],
    "x": [("emb", T)] + _by_layer(("lat", T), ("mix", T), ("ln1_", T), ("ln2_", T))
    + [(n, T) for n in ("n1", "nmix", "mix2", "nmem", "ncross", "xo", "n2")],
    "mv": [("emb", T)] + _by_layer(("ln1_", T), ("ln2_", T)),
    "pj": _by_layer(("in", 6), ("o", 2)) + [("in2", 5), ("out2", 2), ("wk", 6), ("wv", 2), ("wq", 6), ("xo", 2)],
    "ev0": _by_layer(("in", 6)) + [("in2", 7), ("wv", 2)],
    "ev1": _by_layer(("in", 6)) + [("in2", 3), ("wv", 2)],
    "ev": _by_layer(("uq", 4)) + [("wk", KD), ("wq", KD)],
    "resid": [(n, 4) for n in ("o0", "f0", "o1", "f1", "f2", "out2", "xo", "f3")],
}
for _k in ("tq", "qk", "s", "pt", "od", "o"):
    RAISED[_k] = [("at0", N_HEADS), ("at1", N_HEADS), ("dil", DIL_H)]
for _k in ("sf", "mx", "p", "tp"):
    RAISED[_k] = [("at0", N_SOFT), ("at1", N_SOFT), ("dil", DIL_H)]
for _k, _c in (("sg", T), ("hu", T), ("ut", 1), ("hh", 1), ("ht", 1)):
    RAISED[_k] = [(n, _c * u) for n, u in _ffns]


def before(stage, kind):
    total = 0
    for name, count in RAISED[kind]:
        if name == stage:
            return total
        total += count
    raise KeyError((stage, kind))


class Chunk:

    def __init__(self, base, it=0):
        self.raw = base % RAW
        self.split = base % SPLIT
        self.width = WIDTH[base]
        self.base = base
        self.n = base + LB * it
        self.landed = 16 * (base // RAW + 1) + (16 * (LB // RAW)) * it


def heads_of_layer():
    return ([("ret", n) for n in range(RET_H)] + [("moba", n) for n in range(MOBA_H)]
            + [("mla", n) for n in range(MLA_H)])


def program(nc, stream, x_in, mem_in, pos_in, consts, cols_in, rows_in, ws_in, out):
    with ExitStack() as ctx:
        def sb(name, shape, dt=F32):
            return ctx.enter_context(nc.sbuf_tensor(name, shape, dt))

        sems = {}

        def sem(name):
            if name not in sems:
                sems[name] = ctx.enter_context(nc.semaphore(name))
            return sems[name]

        def at(stage, kind, count):
            return sem(kind), count + before(stage, kind)

        def group_done(name, g, t):
            if t < T - 1:
                return at(name, "pj", g + 1)
            return used, AT[name] + min(2 * g + 2, dict(STREAM_LENGTH)[name])

        def tile_done(name, j):
            if j % 4 < 3:
                return at(name, "pj", 3 * (j // 4) + j % 4 + 1)
            return used, AT[name] + 2 * (j // 4) + 2

        raw = sb("raw", [P, RAW, CW])
        whi = sb("whi", [P, SPLIT, CW], F32R)
        wlo = sb("wlo", [P, SPLIT, CW], F32R)
        x = sb("resid", [P, T, D])
        r = sb("r", [P, T, D])
        xth = sb("xth", [P, KD, S], F32R)
        xtl = sb("xtl", [P, KD, S], F32R)
        h = sb("h", [P, T, D_IN])
        qc = sb("qc", [P, T, MLA_H, QD])
        kc = sb("kc", [P, T, MLA_H, QD])
        vc = sb("vc", [P, T, MLA_H, NOPE])
        qkt = sb("qkt", [P, 2, 512])
        prob = sb("prob", [P, 2, 512])
        probt = sb("probt", [P, 2, 512])
        hth = sb("hth", [P, 3, S], F32R)
        htl = sb("htl", [P, 3, S], F32R)
        bc = sb("bc", [P, 2, D])
        cst = sb("cst", [P, CONST_W])
        cols = sb("cols", [P, NCOL])
        bn = sb("bn", [P, T, 2, 6])
        mv = sb("mv", [P, T, 2])
        nmax = sb("nmax", [P, 16, T])
        rsum = sb("rsum", [P, 16, T])
        rinv = sb("rinv", [P, 16, T])
        ss = sb("ss", [P, 4])
        sd = sb("sd", [P, 4])
        rstd = sb("rstd", [P, 4])
        gs = sb("gs", [P, 4, 16])
        eps = sb("eps", [P, 2])
        small = sb("small", [P, 8, 16])
        lg = sb("lg", [P, 8, T, NE])
        posi = sb("posi", [P, T], I32)
        rot = sb("rot", [P, 6, T, 8])
        ps = [ctx.enter_context(nc.psum_tensor(f"ps{b}", [P, 512], F32)) for b in range(8)]

        def const(name):
            a, b = CONST_AT[name]
            return cst[:, a:b]

        ident = const("ident")
        c_ret = const("ret").rearrange("p (h i) -> p h i", h=RET_H)
        c_moba = const("moba").rearrange("p (h i) -> p h i", h=MOBA_H)
        sg = prob[:, :, 0:FU]
        hs = probt[:, :, 0:FU]
        gexp = qkt[:, 0, 0:U_MOE].rearrange("p (n t) -> p n t", t=T)
        lg3 = qkt[:, 1, 0:4 * NE * NE].rearrange("p (a t e f) -> p a t e f", a=2, t=T, e=NE)
        hflat = h[:, :, :].rearrange("p t n -> p (t n)")
        kt = hflat[:, 0:KD * S].rearrange("p (k s) -> p k s", k=KD)
        xv = hflat[:, KD * S:2 * KD * S].rearrange("p (t n) -> p t n", t=T)
        qt = r[:, :, :].rearrange("p t n -> p (t n)").rearrange("p (k s) -> p k s", k=KD)
        ws = kc[:, :, :, :].rearrange("p t h d -> p (t h d)")[:, 0:8 * P].rearrange("p (g j) -> p g j", g=8)
        wst = qc[:, :, :, :].rearrange("p t h d -> p (t h d)")[:, 0:8 * P].rearrange("p (g j) -> p g j", g=8)

        landed = [sem(f"landed{n}") for n in range(RAW)]
        hi_done = sem("hi_done")
        lo_done = sem("lo_done")
        used = sem("used")

        def f32(ap):
            return ap.bitcast(F32)

        block = ctx.enter_context(nc.Block())

        @block.sync
        def _(sp):
            def load(c):
                if not (isinstance(c.n, int) and c.n < RAW):
                    sp.wait_ge(lo_done, c.n - RAW + 1)
                sp.dma_start(raw[:, c.raw, 0:c.width], stream[c.n, :, 0:c.width]).then_inc(landed[c.raw], 16)

            n = 0
            while n < NCHUNK:
                if any(n == AT[f] for f in ("f0", "f1", "f2", "f3")):
                    name = next(f for f in ("f0", "f1", "f2", "f3") if n == AT[f])
                    loops = 3 * (U_MOE if name == "f1" else U_FF) // LB
                    with sp.Fori(0, loops) as it:
                        for j in range(LB):
                            load(Chunk(n + j, it))
                    n += loops * LB
                else:
                    load(Chunk(n))
                    n += 1

        @block.gpsimd
        def _(pool):
            pool.memset(eps[:, 0:1], LN_EPS).then_inc(sem("eps_set"), 1)
            pool.memset(eps[:, 1:2], RMS_EPS).then_inc(sem("eps_set"), 1)
            pool.dma_start(r[:, :, :], x_in.rearrange("(t p) d -> p t d", p=P)).then_inc(sem("x_in"), 16)
            pool.dma_start(cst[:, :], consts).then_inc(sem("const_in"), 16)
            pool.dma_start(cols[:, :], cols_in).then_inc(sem("cols_in"), 16)
            pool.dma_start(posi[:, :], pos_in).then_inc(sem("pos_in"), 16)

            def rows(n, count, free, value):
                if free:
                    pool.wait_ge(*at(free[0], free[1], value))
                pool.dma_start(bc[:, 0:count, :], rows_in[n:n + count, :].partition_broadcast(P)).then_inc(
                    sem(f"rows{n}"), 16)

            rows(0, 2, None, 0)
            for l in range(DEPTH):
                rows(2 + 4 * l, 2, ("emb" if l == 0 else "ln2_0", "x"), T)
                rows(4 + 4 * l, 2, (f"ln1_{l}", "x"), T)
            rows(10, 1, ("ln2_1", "x"), T)
            pool.wait_ge(*at("ln2_1", "x", T))
            pool.dma_start(ws, ws_in.rearrange("g i j -> i g j")).then_inc(sem("ws_in"), 16)
            pool.wait_ge(*at("out2", "resid", 4))
            pool.dma_start(r[:, :, :], mem_in.rearrange("(t p) d -> p t d", p=P)).then_inc(sem("mem_in"), 16)
            rows(11, 1, ("xo", "tr"), 4)
            for t in range(T):
                pool.wait_ge(sem("final"), t + 1)
                pool.dma_start(out[t * P:(t + 1) * P, :], r[:, t, :]).then_inc(sem("stored"), 16)
            pool.wait_ge(sem("stored"), 16 * T)

        @block.tensor
        def _(pe):
            def mm3(o, ah, al, bh, bl, start, stop):
                pe.matmul(o, ah, bh, start=start, stop=False, skip_group_check=True)
                pe.matmul(o, ah, bl, start=False, stop=False, skip_group_check=True)
                return pe.matmul(o, al, bh, start=False, stop=stop, skip_group_check=True)

            def chunk(c):
                pe.wait_ge(lo_done, c.n + 1)

            def transpose_x(stage, src, kn=KD, banks=(0, 1, 2, 3)):
                for t in range(T):
                    pe.wait_ge(*at(stage, "x", t + 1))
                    for k in range(kn):
                        m = pe.transpose(ps[banks[k // 2]][:, (k % 2) * S + t * P:(k % 2) * S + (t + 1) * P],
                                         src[:, t, k * P:(k + 1) * P], ident)
                        if t == T - 1 and (k % 2 == 1 or k == kn - 1):
                            m.then_inc(sem("tr"), 1)

            def project(name, stage, ah, al, groups, kn, bank, ready, free):
                pe.wait_ge(*at(ready[0], "xt", ready[1]))
                n = AT[name]
                for g, (width, chunks) in enumerate(groups):
                    per = kn // chunks
                    for j in range(chunks):
                        c = Chunk(n)
                        n += 1
                        chunk(c)
                        wh = whi[:, c.split, 0:per * width].rearrange("p (k n) -> p k n", k=per)
                        wl = wlo[:, c.split, 0:per * width].rearrange("p (k n) -> p k n", k=per)
                        for t in range(T):
                            if j == 0:
                                free(g, t)
                            for k in range(per):
                                kk = j * per + k
                                m = mm3(ps[bank(g, t)][:, 0:width], ah[:, kk, t * P:(t + 1) * P],
                                        al[:, kk, t * P:(t + 1) * P], wh[:, k, :], wl[:, k, :],
                                        start=(kk == 0), stop=(kk == kn - 1))
                            if j == chunks - 1 and t < T - 1:
                                m.then_inc(sem("pj"), 1)
                        m.then_inc(used, 1)

            def project_t(name, stage, ready, free):
                pe.wait_ge(*at(ready[0], "xt", ready[1]))
                for g in range(2):
                    for j in range(2):
                        c = Chunk(AT[name] + 2 * g + j)
                        chunk(c)
                        wh = whi[:, c.split, :].rearrange("p (k n) -> p k n", k=4)
                        wl = wlo[:, c.split, :].rearrange("p (k n) -> p k n", k=4)
                        for q in range(4):
                            if j == 0:
                                free(4 * g + q)
                            for k in range(4):
                                kk = 4 * j + k
                                m = mm3(ps[4 * g + q][:, 0:S], wh[:, k, q * P:(q + 1) * P], wl[:, k, q * P:(q + 1) * P],
                                        xth[:, kk, :], xtl[:, kk, :], start=(kk == 0), stop=(kk == 7))
                            if j == 1 and q < 3:
                                m.then_inc(sem("pj"), 1)
                        m.then_inc(used, 1)

            def ffn(name, units):
                first_chunk = AT[name]

                def gate_up(a, b):
                    for j, c in enumerate((a, b)):
                        chunk(c)
                        wh = whi[:, c.split, :].rearrange("p (k n) -> p k n", k=4)
                        wl = wlo[:, c.split, :].rearrange("p (k n) -> p k n", k=4)
                        for t in range(T):
                            for k in range(4):
                                kk = 4 * j + k
                                m = mm3(ps[t][:, :], xth[:, kk, t * P:(t + 1) * P], xtl[:, kk, t * P:(t + 1) * P],
                                        wh[:, k, :], wl[:, k, :], start=(kk == 0), stop=(kk == 7))
                        m.then_inc(used, 1)

                def down(c, u, first, last):
                    chunk(c)
                    pe.wait_ge(*at(name, "ht", u + 1))
                    wh = whi[:, c.split, :].rearrange("p (k n) -> p k n", k=2)
                    wl = wlo[:, c.split, :].rearrange("p (k n) -> p k n", k=2)
                    for t in range(T):
                        for n in range(2):
                            for k in range(2):
                                m = mm3(ps[4 + 2 * t + n][:, :], hth[:, k, t * P:(t + 1) * P], htl[:, k, t * P:(t + 1) * P],
                                        wh[:, k, n * 512:(n + 1) * 512], wl[:, k, n * 512:(n + 1) * 512],
                                        start=first and k == 0, stop=last and k == 1)
                    m.then_inc(used, 1)

                def turn(u):
                    pe.wait_ge(*at(name, "hu", 2 * u + 2))
                    for t in range(T):
                        for k in range(2):
                            m = pe.transpose(ps[2][:, k * S + t * P:k * S + (t + 1) * P], hs[:, t, k * P:(k + 1) * P], ident)
                    m.then_inc(sem("ut"), 1)

                def unit(u, base, it, first):
                    gate_up(Chunk(base, it), Chunk(base + 1, it))
                    down(Chunk(base + 2, it), u - 1, first, False)
                    turn(u)

                gate_up(Chunk(first_chunk), Chunk(first_chunk + 1))
                turn(0)
                unit(1, first_chunk + 2, 0, True)
                loops = (units - 3) // UNROLL
                with pe.Fori(0, loops) as it:
                    for j in range(UNROLL):
                        unit(it * UNROLL + 2 + j, first_chunk + 5 + 3 * j, it, False)
                for u in range(2 + loops * UNROLL, units):
                    unit(u, first_chunk + 3 * u - 1, 0, False)
                down(Chunk(first_chunk + 3 * units - 1), units - 1, False, True)

            def heads(stage, work, masked):
                soft = [kind != "ret" for kind, _ in work]

                def turn_qk(i):
                    kind, n = work[i]
                    if i >= 2:
                        pe.wait_ge(*at(stage, "qk", i - 1))
                    for s in range(2):
                        for t in range(T):
                            if kind == "mla":
                                src = (qc, kc)[s][:, t, n, :]
                            elif kind == "dil":
                                col = 1024 + 512 * s + HD * n
                                src = h[:, t, col:col + P]
                            else:
                                col = ((C_RQ, C_RK) if kind == "ret" else (C_MQ, C_MK))[s] + HD * n
                                src = h[:, t, col:col + P]
                            w = src.shape[-1]
                            m = pe.transpose(ps[i % 2][0:w, s * S + t * P:s * S + (t + 1) * P], src, ident)
                    m.then_inc(sem("tq"), 1)

                def scores(i):
                    kind, n = work[i]
                    d = QD if kind == "mla" else HD
                    q, k = qkt[0:d, i % 2, 0:S], qkt[0:d, i % 2, S:2 * S]
                    o = ps[2 + i % 2]
                    pe.wait_ge(*at(stage, "qk", i + 1))
                    if i >= 2 and soft[i - 2]:
                        pe.wait_ge(*at(stage, "sf", sum(soft[:i - 1])))
                    elif i >= 2:
                        pe.wait_ge(*at(stage, "pt", i - 1))
                    if kind == "ret":
                        pe.matmul(o[:, 0:S], k[:, 0:P], q, start=True, stop=True)
                        m = pe.matmul(o[:, S:S + P], k[:, P:S], q[:, P:S], start=True, stop=True)
                    else:
                        pe.matmul(o[:, 0:P], q[:, 0:P], k[:, 0:P], start=True, stop=True)
                        m = pe.matmul(o[:, P:P + S], q[:, P:S], k, start=True, stop=True)
                    m.then_inc(sem("s"), 1)

                def turn_p(i):
                    if not soft[i]:
                        return
                    pe.wait_ge(*at(stage, "p", sum(soft[:i + 1])))
                    for b in range(3):
                        m = pe.transpose(ps[4 + i % 2][:, b * P:(b + 1) * P], prob[:, i % 2, b * P:(b + 1) * P], ident)
                    m.then_inc(sem("tp"), 1)

                def outputs(i):
                    kind, n = work[i]
                    pt = probt[:, i % 2, :]
                    pe.wait_ge(*at(stage, "pt", i + 1))
                    if i >= 2:
                        pe.wait_ge(*at(stage, "o", i - 1))

                    def v(t):
                        if kind == "mla":
                            return vc[:, t, n, :]
                        col = {"ret": C_RV, "moba": C_MV, "dil": 2048}[kind] + HD * n
                        return h[:, t, col:col + HD]
                    o = ps[6 + i % 2]
                    pe.matmul(o[:, 0:HD], pt[:, 0:P], v(0), start=True, stop=True)
                    pe.matmul(o[:, HD:2 * HD], pt[:, P:2 * P], v(0), start=True, stop=False)
                    pe.matmul(o[:, HD:2 * HD], pt[:, 2 * P:3 * P], v(1), start=False, stop=True).then_inc(
                        sem("od"), 1)

                for i in range(len(work) + 3):
                    if i >= 3:
                        outputs(i - 3)
                    if 2 <= i < len(work) + 2:
                        turn_p(i - 2)
                    if 1 <= i < len(work) + 1:
                        scores(i - 1)
                    if i < len(work):
                        turn_qk(i)

            pe.wait_ge(sem("const_in"), 16)
            transpose_x("emb", x)
            xt_stage = "emb"
            for l in range(DEPTH):
                st = f"in{l}"

                def free_in(g, t):
                    if g >= 2:
                        pe.wait_ge(*at(st, f"ev{t}", g - 1))

                groups = [(512, 2)] * 5 + [(96, 1)]
                project(st, st, xth, xtl, groups, KD, lambda g, t: 2 * (g % 2) + t, (xt_stage, 4), free_in)
                transpose_x(f"lat{l}", h, kn=3, banks=(4, 5))
                for g, stage, ks in ((0, f"uq{l}", (0, 2)), (1, f"ukv{l}", (2, 3))):
                    width = 288 if g == 0 else 384
                    c = Chunk(AT[stage])
                    chunk(c)
                    pe.wait_ge(*at(f"lat{l}", "xt", 2))
                    if g == 0:
                        pe.wait_ge(*at(st, "ev0", 6))
                        pe.wait_ge(*at(st, "ev1", 6))
                    kn = ks[1] - ks[0]
                    wh = whi[:, c.split, 0:c.width].rearrange("p (k n) -> p k n", k=kn)
                    wl = wlo[:, c.split, 0:c.width].rearrange("p (k n) -> p k n", k=kn)
                    for t in range(T):
                        for half in range(2):
                            for k in range(kn):
                                m = mm3(ps[4 * g + 2 * t + half][:, 0:width], hth[:, ks[0] + k, t * P:(t + 1) * P],
                                        htl[:, ks[0] + k, t * P:(t + 1) * P], wh[:, k, half * width:(half + 1) * width],
                                        wl[:, k, half * width:(half + 1) * width], start=(k == 0), stop=(k == kn - 1))
                    m.then_inc(used, 1)
                pe.wait_ge(sem(f"rope{l}"), 1)
                heads(f"at{l}", heads_of_layer(), True)
                transpose_x(f"mix{l}", r)
                project(f"o{l}", f"o{l}", xth, xtl, [(512, 2)] * 2, KD, lambda g, t: 4 + 2 * t + g,
                        (f"mix{l}", KD), lambda g, t: None)
                transpose_x(f"ln1_{l}", x)
                pe.wait_ge(*at(f"ln1_{l}", "xt", 4))
                if l == 1:
                    c = Chunk(AT["router"])
                    chunk(c)
                    for t in range(T):
                        for k in range(KD):
                            m = mm3(ps[3][:, t * NE:(t + 1) * NE], xth[:, k, t * P:(t + 1) * P],
                                    xtl[:, k, t * P:(t + 1) * P], whi[:, c.split, k * NE:(k + 1) * NE],
                                    wlo[:, c.split, k * NE:(k + 1) * NE], start=(k == 0), stop=(k == KD - 1))
                    m.then_inc(used, 1)
                ffn(f"f{l}", U_MOE if l else U_FF)
                if l == 0:
                    transpose_x(f"ln2_{l}", x)
                xt_stage = f"ln2_{l}"

            transpose_x("n1", r)
            pe.wait_ge(*at("n1", "xt", KD))
            ffn("f2", U_FF)
            transpose_x("nmix", r)

            def free_in2(g, t):
                if g in (2, 3):
                    pe.wait_ge(*at("in2", "ev0", 2 * g - 3 + t))
                if g == 4:
                    pe.wait_ge(*at("in2", f"ev{t}", (5, 1)[t]))
            project("in2", "in2", xth, xtl, [(512, 2)] * 5, KD, lambda g, t: 2 * (g % 2) + t, ("nmix", KD), free_in2)
            pe.wait_ge(sem("ws_masked"), 1)
            for g in range(8):
                m = pe.transpose(ps[4 + g // 4][:, (g % 4) * P:(g % 4 + 1) * P], ws[:, g, :], ident)
            m.then_inc(sem("ws_tr"), 1)
            pe.wait_ge(sem("ws_t"), 2)
            pe.wait_ge(sem("v_norm"), 1)
            for g in range(8):
                m = pe.matmul(ps[6 + g // 4][:, (g % 4) * P:(g % 4 + 1) * P], wst[:, g, :],
                              h[:, :, 512 + HD * g:512 + HD * (g + 1)], start=True, stop=True)
            m.then_inc(sem("mixed"), 1)
            pe.wait_ge(sem("rot_done"), 1)
            pe.wait_ge(sem("ya"), 1)
            heads("dil", [("dil", n) for n in range(DIL_H)], True)
            transpose_x("mix2", r)
            project("out2", "out2", xth, xtl, [(512, 2)] * 2, KD, lambda g, t: 4 + 2 * t + g, ("mix2", KD),
                    lambda g, t: None)
            transpose_x("nmem", r)

            def free_k(b):
                if b == 4:
                    pe.wait_ge(*at("out2", "resid", 4))
            project_t("wk", "wk", ("nmem", KD), free_k)
            pe.wait_ge(*at("wk", "ev", KD))
            project("wv", "wv", xth, xtl, [(512, 2)] * 2, KD, lambda g, t: 2 * g + t, ("nmem", KD), lambda g, t: None)
            pe.wait_ge(*at("wv", "ev0", 2))
            pe.wait_ge(*at("wv", "ev1", 2))
            transpose_x("ncross", r)
            project_t("wq", "wq", ("ncross", KD), lambda b: None)
            pe.wait_ge(*at("wq", "ev", KD))
            for i in range(X_H + 2):
                if i >= 2:
                    n = i - 2
                    pe.wait_ge(sem("x_pt"), n + 1)
                    if n >= 2:
                        pe.wait_ge(sem("x_o"), n - 1)
                    for t in range(T):
                        for mt in range(T):
                            m = pe.matmul(ps[6 + n % 2][:, t * X_D:(t + 1) * X_D],
                                          probt[:, n % 2, (2 * t + mt) * P:(2 * t + mt + 1) * P],
                                          xv[:, mt, n * X_D:(n + 1) * X_D], start=(mt == 0), stop=(mt == 1))
                    m.then_inc(sem("x_od"), 1)
                if i < X_H:
                    if i >= 2:
                        pe.wait_ge(sem("x_p"), i - 1)
                    for t in range(T):
                        for k in range(2):
                            m = pe.matmul(ps[2 + i % 2][:, t * S:(t + 1) * S], qt[:, 2 * i + k, t * P:(t + 1) * P],
                                          kt[:, 2 * i + k, :], start=(k == 0), stop=(k == 1))
                    m.then_inc(sem("x_s"), 1)
                if 1 <= i < X_H + 1:
                    n = i - 1
                    pe.wait_ge(sem("x_p"), n + 1)
                    for b in range(4):
                        m = pe.transpose(ps[4 + n % 2][:, b * P:(b + 1) * P], prob[:, n % 2, b * P:(b + 1) * P], ident)
                    m.then_inc(sem("x_tp"), 1)
            transpose_x("xo", bc)
            project("xo", "xo", xth, xtl, [(512, 2)] * 2, KD, lambda g, t: 4 + 2 * t + g, ("xo", 4),
                    lambda g, t: None)
            transpose_x("n2", r)
            pe.wait_ge(*at("n2", "xt", KD))
            ffn("f3", U_FF)

        @block.scalar
        def _(act):
            cursor = [0]
            chained = [0]

            def link(ins):
                chained[0] += 1
                ins.then_inc(sem("act_chain"), 1)
                act.wait_ge(sem("act_chain"), chained[0])

            def hi(c):
                act.wait_ge(landed[c.raw], c.landed)
                if not (isinstance(c.n, int) and c.n < SPLIT):
                    act.wait_ge(used, c.n - SPLIT + 1)
                act.activation(whi[:, c.split, 0:c.width], raw[:, c.raw, 0:c.width], ACT.Copy).then_inc(hi_done, 1)

            def advance(upto):
                while cursor[0] <= min(upto, NCHUNK - 1):
                    hi(Chunk(cursor[0]))
                    cursor[0] += 1

            def split_x(stage, gain=None, kn=KD, dst=xth, banks=(0, 1, 2, 3)):
                for b in range((kn + 1) // 2):
                    act.wait_ge(*at(stage, "tr", b + 1))
                    ks = range(2 * b, min(2 * b + 2, kn))
                    if gain is None:
                        act.activation(dst[:, 2 * b:2 * b + 2, :], ps[banks[b]][:, :].rearrange("p (k s) -> p k s", k=2),
                                       ACT.Copy).then_inc(sem("xh"), 1)
                        continue
                    for k in ks:
                        act.activation(dst[:, k, :], ps[banks[b]][:, (k % 2) * S:(k % 2 + 1) * S], ACT.Copy,
                                       scale=cols[:, gain + k:gain + k + 1]).then_inc(sem("xh"), 1)

            def root(stage, src, n, scale, e):
                act.activation(sd[:, 0:n], src, ACT.Sqrt, bias=eps[:, e:e + 1], scale=scale).then_inc(sem("sd"), 1)

            def rms_stats(stage, parts):
                for n, (junk, src) in enumerate(parts):
                    link(act.activation(junk, src, ACT.Square, accum_out=ss[:, n:n + 1]))
                root(stage, ss[:, 0:len(parts)], len(parts), 1.0 / parts[0][1].shape[-1], 1)

            def evac(stage, g, t, dst, width, bank, func=ACT.Copy):
                act.wait_ge(*group_done(stage, g, t))
                act.activation(dst, ps[bank][:, 0:width], func).then_inc(sem("ev0"), 1)

            def ffn(name, units):
                first_chunk = AT[name]

                def unit(u, base, it, chunks):
                    n = base + LEAD
                    for j in range(chunks - 1):
                        if n + j < NCHUNK:
                            hi(Chunk(n + j, it))
                    act.wait_ge(used, base + LB * it + 2)
                    for t in range(T):
                        act.activation(sg[:, t, :], ps[t][:, 0:FU], ACT.Silu).then_inc(sem("sg"), 1)
                    if n + chunks - 1 < NCHUNK:
                        hi(Chunk(n + chunks - 1, it))
                    act.wait_ge(*at(name, "ut", u + 1))
                    act.activation(hth[:, 0:2, :], ps[2][:, :].rearrange("p (k s) -> p k s", k=2), ACT.Copy).then_inc(
                        sem("hh"), 1)

                advance(first_chunk + LEAD - 1)
                unit(0, first_chunk, 0, 2)
                unit(1, first_chunk + 2, 0, 3)
                loops = (units - 3) // UNROLL
                with act.Fori(0, loops) as it:
                    for j in range(UNROLL):
                        unit(it * UNROLL + 2 + j, first_chunk + 5 + 3 * j, it, 3)
                for u in range(2 + loops * UNROLL, units):
                    unit(u, first_chunk + 3 * u - 1, 0, 3)
                cursor[0] = first_chunk + 3 * units - 1 + LEAD

            def heads(stage, work, last):
                soft = [kind != "ret" for kind, _ in work]
                for i in range(len(work) + 1):
                    if i < len(work):
                        d = QD if work[i][0] == "mla" else HD
                        act.wait_ge(*at(stage, "tq", i + 1))
                        act.activation(qkt[0:d, i % 2, :], ps[i % 2][0:d, :], ACT.Copy).then_inc(sem("qk"), 1)
                    if i >= 1 and soft[i - 1]:
                        n = i - 1
                        act.wait_ge(*at(stage, "mx", sum(soft[:i])))
                        act.activation(prob[:, n % 2, 0:P], prob[:, n % 2, 0:P], ACT.Exp, bias=nmax[:, n, 0:1],
                                       accum_out=rsum[:, n, 0:1])
                        act.activation(prob[:, n % 2, P:3 * P], prob[:, n % 2, P:3 * P], ACT.Exp, bias=nmax[:, n, 1:2],
                                       accum_out=rsum[:, n, 1:2]).then_inc(sem("p"), 1)
                    if i == 1:
                        advance(last + LEAD)

            act.wait_ge(sem("eps_set"), 2)
            act.wait_ge(sem("cols_in"), 16)
            advance(LEAD - 1)
            act.wait_ge(*at("emb", "mv", T))
            root("emb", mv[:, :, 1], T, 1.0, 0)
            split_x("emb")
            for l in range(DEPTH):
                st = f"in{l}"
                for g in range(6):
                    last = AT[st] + 2 * g + (1 if g < 5 else 0)
                    advance(last + LEAD)
                    width = 512 if g < 5 else 96
                    evac(st, g, 0, h[:, 0, 512 * g:512 * g + width], width, 2 * (g % 2))
                    if g == 0:
                        act.wait_ge(*at(st, "ev1", 1))
                        act.wait_ge(*at(st, "ev0", 1))
                        for t in range(T):
                            link(act.activation(prob[:, t, 0:256], h[:, t, 0:256], ACT.Square, accum_out=ss[:, t:t + 1]))
                            link(act.activation(prob[:, t, 256:384], h[:, t, 256:384], ACT.Square,
                                                accum_out=ss[:, 2 + t:3 + t]))
                        link(act.activation(sd[:, 0:2], ss[:, 0:2], ACT.Sqrt, bias=eps[:, 1:2], scale=1.0 / 256))
                        act.activation(sd[:, 2:4], ss[:, 2:4], ACT.Sqrt, bias=eps[:, 1:2], scale=1.0 / 128).then_inc(
                            sem("sd"), 1)
                last = AT[f"ukv{l}"]
                act.wait_ge(*at(st, "ev0", 6))
                act.wait_ge(*at(st, "ev1", 6))
                act.activation(h[:, :, C_RG:C_RG + 320], h[:, :, C_RG:C_RG + 320], ACT.Silu).then_inc(sem(f"gate{l}"), 1)
                split_x(f"lat{l}", COLS[f"q{l}"], 3, hth, (4, 5))
                advance(last + LEAD)
                act.wait_ge(used, AT[f"uq{l}"] + 1)
                for t in range(T):
                    for half in range(2):
                        act.activation(qc[:, t, 3 * half:3 * half + 3, :],
                                       ps[2 * t + half][:, 0:288].rearrange("p (h d) -> p h d", h=3),
                                       ACT.Copy).then_inc(sem("ev"), 1)
                heads(f"at{l}", heads_of_layer(), last)
                act.wait_ge(*at(f"at{l}", "o", 16))
                for t in range(T):
                    link(act.activation(prob[:, t, 0:384], r[:, t, 0:384], ACT.Square, accum_out=ss[:, t:t + 1]))
                    link(act.activation(prob[:, t, 0:320], r[:, t, O_MOBA:D], ACT.Square, accum_out=ss[:, 2 + t:3 + t]))
                link(act.activation(sd[:, 0:2], ss[:, 0:2], ACT.Sqrt, bias=eps[:, 1:2], scale=1.0 / 384))
                act.activation(sd[:, 2:4], ss[:, 2:4], ACT.Sqrt, bias=eps[:, 1:2], scale=1.0 / 320).then_inc(
                    sem("sd"), 1)
                act.wait_ge(sem(f"ret{l}_var"), 1)
                act.activation(gs[:, 2, 0:10], gs[:, 1, 0:10], ACT.Sqrt, bias=eps[:, 1:2], scale=1.0 / HD).then_inc(
                    sem("sd"), 1)
                split_x(f"mix{l}", COLS[f"mix{l}"])
                advance(AT[f"o{l}"] + 3 + LEAD)
                act.wait_ge(*at(f"ln1_{l}", "mv", T))
                root(f"ln1_{l}", mv[:, :, 1], T, 1.0, 0)
                split_x(f"ln1_{l}")
                if l == 1:
                    advance(AT["router"] + LEAD)
                    act.wait_ge(sem("rt_max"), 1)
                    for t in range(T):
                        act.activation(lg[:, 1, t, :], lg[:, 0, t, :], ACT.Exp, bias=small[:, 0, t:t + 1]).then_inc(
                            sem("rt_exp"), 1)
                ffn(f"f{l}", U_MOE if l else U_FF)
                act.wait_ge(*at(f"ln2_{l}", "mv", T))
                root(f"ln2_{l}", mv[:, :, 1], T, 1.0, 0)
                if l == 0:
                    split_x(f"ln2_{l}")

            def rms_of_x(stage):
                rms_stats(stage, [(r[:, t, :], x[:, t, :]) for t in range(T)])

            act.wait_ge(*at("ln2_1", "x", T))
            rms_of_x("n1")
            split_x("n1", COLS["ffn1"])
            ffn("f2", U_FF)
            act.wait_ge(sem("angle"), 1)
            act.activation(rot[:, 4], rot[:, 2], ACT.Sin).then_inc(sem("sines"), 1)
            act.activation(rot[:, 5], rot[:, 2], ACT.Sin, scale=0.5).then_inc(sem("sines"), 1)
            act.wait_ge(*at("f2", "resid", 4))
            rms_of_x("nmix")
            split_x("nmix", COLS["in2"])
            for g in range(5):
                advance(AT["in2"] + 2 * g + 1 + LEAD)
                evac("in2", g, 0, h[:, 0, 512 * g:512 * g + 512], 512, 2 * (g % 2), ACT.Gelu if g < 2 else ACT.Copy)
                if g < 2:
                    evac("in2", g, 1, h[:, 1, 512 * g:512 * g + 512], 512, 2 * (g % 2) + 1, ACT.Gelu)
            last = AT["in2"] + 9
            act.wait_ge(sem("sgu_var"), 1)
            act.activation(gs[:, 2, :], gs[:, 1, :], ACT.Sqrt, bias=eps[:, 0:1], scale=1.0 / HD).then_inc(sem("sd"), 1)
            act.wait_ge(sem("ws_tr"), 1)
            for b in range(2):
                act.activation(wst[:, 4 * b:4 * b + 4, :], ps[4 + b][:, :].rearrange("p (g j) -> p g j", g=4),
                               ACT.Copy).then_inc(sem("ws_t"), 1)
            heads("dil", [("dil", n) for n in range(DIL_H)], last)
            act.wait_ge(*at("dil", "o", DIL_H))
            rms_stats("mix2", [(prob[:, t, :], r[:, t, 512 * a:512 * a + 512]) for a in range(2) for t in range(T)])
            split_x("mix2", COLS["out2"])
            advance(AT["out2"] + 3 + LEAD)
            act.wait_ge(sem("mem_in"), 16)
            for t in range(T):
                link(act.activation(bc[:, 1, :], r[:, t, :], ACT.Square, accum_out=ss[:, t:t + 1]))
            root("nmem", ss[:, 0:T], T, 1.0 / D, 1)
            split_x("nmem", COLS["mem"])
            for j in range(KD):
                advance(AT["wk"] + 2 * (j // 4) + 1 + LEAD)
                act.wait_ge(*tile_done("wk", j))
                act.activation(kt[:, j, :], ps[j][:, 0:S], ACT.Copy).then_inc(sem("ev"), 1)
            for g in range(2):
                advance(AT["wv"] + 2 * g + 1 + LEAD)
                evac("wv", g, 0, xv[:, 0, 512 * g:512 * g + 512], 512, 2 * g)
            act.wait_ge(*at("nmem", "tr", 4))
            rms_of_x("ncross")
            split_x("ncross", COLS["cross"])
            for j in range(KD):
                advance(AT["wq"] + 2 * (j // 4) + 1 + LEAD)
                act.wait_ge(*tile_done("wq", j))
                act.activation(qt[:, j, :], ps[j][:, 0:S], ACT.Copy).then_inc(sem("ev"), 1)
            last = AT["wq"] + 3
            for i in range(X_H):
                act.wait_ge(sem("x_mx"), i + 1)
                if i >= 2:
                    act.wait_ge(sem("x_tp"), i - 1)
                for t in range(T):
                    m = act.activation(prob[:, i % 2, t * S:(t + 1) * S], ps[2 + i % 2][:, t * S:(t + 1) * S], ACT.Exp,
                                       bias=nmax[:, i, t:t + 1], scale=X_D ** -0.5, accum_out=rsum[:, i, t:t + 1])
                m.then_inc(sem("x_p"), 1)
                advance(last + 1 + i if i < SPLIT else 0)
            split_x("xo")
            advance(AT["xo"] + 3 + LEAD)
            act.wait_ge(*at("xo", "resid", 4))
            rms_of_x("n2")
            split_x("n2", COLS["ffn2"])
            ffn("f3", U_FF)
            act.wait_ge(*at("f3", "resid", 4))
            rms_of_x("fin")

        @block.vector
        def _(dve):
            cursor = [0]
            chained = [0]

            def link(ins):
                chained[0] += 1
                ins.then_inc(sem("dve_chain"), 1)
                dve.wait_ge(sem("dve_chain"), chained[0])

            def lo(c):
                dve.wait_ge(hi_done, c.n + 1)
                dve.tensor_tensor(wlo[:, c.split, 0:c.width], raw[:, c.raw, 0:c.width], f32(whi[:, c.split, 0:c.width]),
                                  ALU.subtract).then_inc(lo_done, 1)

            def advance(upto):
                while cursor[0] <= min(upto, NCHUNK - 1):
                    lo(Chunk(cursor[0]))
                    cursor[0] += 1

            def split_x(stage, gain=None, kn=KD, dsth=xth, dstl=xtl, banks=(0, 1, 2, 3)):
                for b in range((kn + 1) // 2):
                    if gain is None:
                        dve.wait_ge(*at(stage, "xh", b + 1))
                        dve.tensor_tensor(dstl[:, 2 * b:2 * b + 2, :], ps[banks[b]][:, :].rearrange("p (k s) -> p k s", k=2),
                                          f32(dsth[:, 2 * b:2 * b + 2, :]), ALU.subtract).then_inc(sem("xt"), 1)
                        continue
                    n = min(2 * b + 2, kn)
                    dve.wait_ge(*at(stage, "xh", n))
                    for k in range(2 * b, n):
                        m = dve.scalar_tensor_tensor(out=dstl[:, k, :], in0=ps[banks[b]][:, (k % 2) * S:(k % 2 + 1) * S],
                                                     scalar=cols[:, gain + k:gain + k + 1], in1=f32(dsth[:, k, :]),
                                                     op0=ALU.mult, op1=ALU.subtract)
                        if kn == KD or k % 2 == 1 or k == kn - 1:
                            m.then_inc(sem("xt"), 1)

            def layer_norm(stage, row):
                for t in range(T):
                    for a in range(2):
                        m = dve.bn_stats(bn[:, t, a, :], r[:, t, 512 * a:512 * a + 512])
                    link(m)
                    dve.bn_aggr(mv[:, t, :], bn[:, t, :, :].rearrange("p a s -> p (a s)")).then_inc(sem("mv"), 1)
                dve.wait_ge(*at(stage, "mv", T))
                dve.wait_ge(sem(f"rows{row}"), 16)
                for t in range(T):
                    link(dve.scalar_tensor_tensor(out=r[:, t, :], in0=r[:, t, :], scalar=mv[:, t, 0:1], in1=bc[:, 0, :],
                                                  op0=ALU.subtract, op1=ALU.mult))
                dve.wait_ge(*at(stage, "sd", 1))
                link(dve.reciprocal(rstd[:, 0:T], sd[:, 0:T]))
                for t in range(T):
                    dve.scalar_tensor_tensor(out=x[:, t, :], in0=r[:, t, :], scalar=rstd[:, t:t + 1], in1=bc[:, 1, :],
                                             op0=ALU.mult, op1=ALU.add).then_inc(sem("x"), 1)

            def residual(stage, done, dst, a, b):
                dve.wait_ge(*done)
                for t in range(T):
                    for n in range(2):
                        cut = slice(512 * n, 512 * n + 512)
                        p = ps[4 + 2 * t + n][:, :]
                        if b == 1.0:
                            m = dve.scalar_tensor_tensor(out=dst[:, t, cut], in0=x[:, t, cut], scalar=float(a), in1=p,
                                                         op0=ALU.mult, op1=ALU.add)
                        else:
                            m = dve.scalar_tensor_tensor(out=dst[:, t, cut], in0=p, scalar=float(b), in1=x[:, t, cut],
                                                         op0=ALU.mult, op1=ALU.add)
                        m.then_inc(sem("resid"), 1)
                dve.wait_ge(*at(stage, "resid", 4))

            def rms_scale(stage, src, dst=None):
                dst = r if dst is None else dst
                dve.wait_ge(*at(stage, "sd", 1))
                link(dve.reciprocal(rstd[:, 0:T], sd[:, 0:T]))
                for t in range(T):
                    dve.tensor_scalar(dst[:, t, :], src[:, t, :], rstd[:, t:t + 1], None, ALU.mult).then_inc(
                        sem("x"), 1)

            def evac(stage, g, t, dst, width, bank):
                dve.wait_ge(*group_done(stage, g, t))
                dve.tensor_copy(dst, ps[bank][:, 0:width]).then_inc(sem("ev1"), 1)

            def ffn(name, units, gated=False):
                first_chunk = AT[name]

                def unit(u, base, it, chunks, pair):
                    n = base + LEAD
                    for j in range(chunks - 1):
                        if n + j < NCHUNK:
                            lo(Chunk(n + j, it))
                    for t in range(T):
                        dve.wait_ge(*at(name, "sg", 2 * u + t + 1))
                        if gated:
                            m = dve.scalar_tensor_tensor(out=hs[:, t, :], in0=sg[:, t, :], scalar=gexp[:, pair, t:t + 1],
                                                         in1=ps[t][:, FU:2 * FU], op0=ALU.mult, op1=ALU.mult)
                        else:
                            m = dve.tensor_tensor(hs[:, t, :], sg[:, t, :], ps[t][:, FU:2 * FU], ALU.mult)
                        m.then_inc(sem("hu"), 1)
                    if n + chunks - 1 < NCHUNK:
                        lo(Chunk(n + chunks - 1, it))
                    dve.wait_ge(*at(name, "hh", u + 1))
                    dve.tensor_tensor(htl[:, 0:2, :], ps[2][:, :].rearrange("p (k s) -> p k s", k=2),
                                      f32(hth[:, 0:2, :]), ALU.subtract).then_inc(sem("ht"), 1)

                advance(first_chunk + LEAD - 1)
                unit(0, first_chunk, 0, 2, 0)
                unit(1, first_chunk + 2, 0, 3, 0)
                loops = (units - 3) // UNROLL
                with dve.Fori(0, loops) as it:
                    for j in range(UNROLL):
                        unit(it * UNROLL + 2 + j, first_chunk + 5 + 3 * j, it, 3, it * (UNROLL // 2) + 1 + j // 2)
                for u in range(2 + loops * UNROLL, units):
                    unit(u, first_chunk + 3 * u - 1, 0, 3, u // 2)
                cursor[0] = first_chunk + 3 * units - 1 + LEAD

            def rotate(x1, x2, cos, sin, tmp):
                dve.tensor_tensor(tmp[0], x1, cos, ALU.mult)
                dve.tensor_tensor(tmp[1], x2, sin, ALU.mult)
                dve.tensor_tensor(tmp[2], x1, sin, ALU.mult)
                link(dve.tensor_tensor(tmp[3], x2, cos, ALU.mult))
                dve.tensor_tensor(x1, tmp[0], tmp[1], ALU.subtract)
                m = dve.tensor_tensor(x2, tmp[2], tmp[3], ALU.add)
                link(m)

            def heads(stage, work, last):
                soft = [kind != "ret" for kind, _ in work]
                for i in range(1, len(work) + 3 + 1):
                    if i - 1 < len(work):
                        n = i - 1
                        kind, hn = work[n]
                        dve.wait_ge(*at(stage, "s", n + 1))
                        if kind == "ret":
                            dve.tensor_tensor(probt[:, n % 2, 0:S], ps[2 + n % 2][:, 0:S], c_ret[:, hn, :], ALU.mult)
                            dve.tensor_tensor(probt[:, n % 2, S:S + P], ps[2 + n % 2][:, S:S + P], c_ret[:, hn, 0:P],
                                              ALU.mult).then_inc(sem("pt"), 1)
                        else:
                            mask = c_moba[:, hn, :] if kind == "moba" else const(kind)
                            scale = QD ** -0.5 if kind == "mla" else HD ** -0.5
                            dve.scalar_tensor_tensor(out=prob[:, n % 2, 0:3 * P], in0=ps[2 + n % 2][:, 0:3 * P], scalar=scale,
                                                     in1=mask, op0=ALU.mult, op1=ALU.add).then_inc(sem("sf"), 1)
                            dve.wait_ge(*at(stage, "sf", sum(soft[:n + 1])))
                            dve.tensor_reduce(nmax[:, n, 0:1], prob[:, n % 2, 0:P], AX, ALU.max, negate=True)
                            dve.tensor_reduce(nmax[:, n, 1:2], prob[:, n % 2, P:3 * P], AX, ALU.max, negate=True).then_inc(
                                sem("mx"), 1)
                    if 0 <= i - 2 < len(work) and soft[i - 2]:
                        n = i - 2
                        dve.wait_ge(*at(stage, "tp", sum(soft[:n + 1])))
                        dve.tensor_copy(probt[:, n % 2, 0:3 * P], ps[4 + n % 2][:, 0:3 * P]).then_inc(sem("pt"), 1)
                    if 0 <= i - 3 < len(work):
                        n = i - 3
                        kind, hn = work[n]
                        col = {"ret": O_RET, "moba": O_MOBA, "mla": 0, "dil": 512}[kind] + HD * hn
                        dve.wait_ge(*at(stage, "od", n + 1))
                        if kind == "ret":
                            dve.tensor_copy(r[:, :, col:col + HD], ps[6 + n % 2][:, 0:2 * HD].rearrange(
                                "p (t d) -> p t d", t=T)).then_inc(sem("o"), 1)
                        else:
                            link(dve.reciprocal(rinv[:, n, :], rsum[:, n, :]))
                            for t in range(T):
                                m = dve.tensor_scalar(r[:, t, col:col + HD], ps[6 + n % 2][:, t * HD:(t + 1) * HD],
                                                      rinv[:, n, t:t + 1], None, ALU.mult)
                            m.then_inc(sem("o"), 1)
                    if i == 2:
                        advance(last + LEAD)

            def group_var(stage, v, groups, scratch):
                link(dve.tensor_reduce(gs[:, 0, 0:groups], v, AX, ALU.add))
                link(dve.tensor_scalar(gs[:, 0, 0:groups], gs[:, 0, 0:groups], 1.0 / HD, None, ALU.mult))
                return None

            dve.wait_ge(sem("x_in"), 16)
            dve.wait_ge(sem("const_in"), 16)
            dve.wait_ge(sem("cols_in"), 16)
            advance(LEAD - 1)
            layer_norm("emb", 0)
            split_x("emb")
            for l in range(DEPTH):
                st = f"in{l}"
                for g in range(6):
                    last = AT[st] + 2 * g + (1 if g < 5 else 0)
                    advance(last + LEAD)
                    width = 512 if g < 5 else 96
                    evac(st, g, 1, h[:, 1, 512 * g:512 * g + width], width, 2 * (g % 2) + 1)
                    if g == 1:
                        dve.wait_ge(*at(f"lat{l}", "sd", 1))
                        link(dve.reciprocal(rstd[:, :], sd[:, :]))
                        for t in range(T):
                            dve.tensor_scalar(h[:, t, 0:256], h[:, t, 0:256], rstd[:, t:t + 1], None, ALU.mult)
                            dve.tensor_scalar(h[:, t, 256:384], h[:, t, 256:384], rstd[:, 2 + t:3 + t], None,
                                              ALU.mult).then_inc(sem("x"), 1)
                    if g == 3:
                        dve.wait_ge(*at(st, "ev0", 3))
                        dve.wait_ge(*at(st, "ev1", 3))
                        for t in range(T):
                            v = h[:, t, C_RQ:C_RV].rearrange("p (h d) -> p h d", d=HD)
                            tmp = [r[:, a // 2, 320 * (a % 2):320 * (a % 2) + 320].rearrange("p (h d) -> p h d", d=32)
                                   for a in range(4)]
                            cos, sin = (const(c)[:, 32 * t:32 * t + 32].unsqueeze(1).to_broadcast([P, 10, 32])
                                        for c in ("cos_b", "sin_b"))
                            rotate(v[:, :, 0:32], v[:, :, 32:64], cos, sin, tmp)
                        v = h[:, :, C_ROPE:C_RQ]
                        tmp = [small[:, 2 * a:2 * a + 2, :] for a in range(4)]
                        cos, sin = (const(c).rearrange("p (t d) -> p t d", t=T) for c in ("cos_a", "sin_a"))
                        rotate(v[:, :, 0:16], v[:, :, 16:32], cos, sin, tmp)
                last = AT[f"ukv{l}"]
                split_x(f"lat{l}", COLS[f"q{l}"], 3, hth, htl, (4, 5))
                advance(last + LEAD)
                dve.wait_ge(used, AT[f"ukv{l}"] + 1)
                for t in range(T):
                    for half in range(2):
                        kv = ps[4 + 2 * t + half][:, 0:384].rearrange("p (h d) -> p h d", h=3)
                        dve.tensor_copy(kc[:, t, 3 * half:3 * half + 3, 0:NOPE], kv[:, :, 0:NOPE])
                        dve.tensor_copy(vc[:, t, 3 * half:3 * half + 3, :], kv[:, :, NOPE:])
                    link(dve.tensor_copy(kc[:, t, :, NOPE:QD],
                                         h[:, t, C_ROPE:C_RQ].unsqueeze(1).to_broadcast([P, MLA_H, ROPE])))
                dve.wait_ge(*at(f"uq{l}", "ev", 4))
                for t in range(T):
                    tmp = [r[:, a // 2, 320 * (a % 2):320 * (a % 2) + 96].rearrange("p (h d) -> p h d", d=16)
                           for a in range(4)]
                    cos, sin = (const(c)[:, 16 * t:16 * t + 16].unsqueeze(1).to_broadcast([P, MLA_H, 16])
                                for c in ("cos_a", "sin_a"))
                    rotate(qc[:, t, :, NOPE:NOPE + 16], qc[:, t, :, NOPE + 16:QD], cos, sin, tmp)
                dve.wait_ge(*at(st, "ev0", 6))
                dve.wait_ge(sem(f"gate{l}"), 1)
                dve.sem_inc(sem(f"rope{l}"), 1)
                heads(f"at{l}", heads_of_layer(), last)
                ov = r[:, :, O_RET:O_MOBA].rearrange("p t (h d) -> p t h d", d=HD)
                gv = gs[:, :, 0:10].rearrange("p s (t h) -> p s t h", t=T)
                gg = h[:, :, C_RG:C_RG + 320].rearrange("p t (h d) -> p t h d", d=HD)
                dve.wait_ge(*at(f"at{l}", "o", 16))
                link(dve.tensor_reduce(gv[:, 0], ov, AX, ALU.add))
                link(dve.tensor_scalar(gs[:, 0, 0:10], gs[:, 0, 0:10], 1.0 / HD, None, ALU.mult))
                sq = h[:, :, C_RQ:C_RK].rearrange("p t (h d) -> p t h d", d=HD)
                for t in range(T):
                    link(dve.tensor_tensor(ov[:, t], ov[:, t], gv[:, 0, t].unsqueeze(2).to_broadcast([P, RET_H, HD]),
                                           ALU.subtract))
                link(dve.tensor_tensor(sq, ov, ov, ALU.mult))
                dve.tensor_reduce(gv[:, 1], sq, AX, ALU.add).then_inc(sem(f"ret{l}_var"), 1)
                dve.wait_ge(*at(f"ret{l}", "sd", 1))
                link(dve.reciprocal(gs[:, 3, 0:10], gs[:, 2, 0:10]))
                for t in range(T):
                    link(dve.tensor_tensor(ov[:, t], ov[:, t], gv[:, 3, t].unsqueeze(2).to_broadcast([P, RET_H, HD]), ALU.mult))
                link(dve.tensor_tensor(ov, ov, gg, ALU.mult))
                dve.wait_ge(*at(f"mix{l}", "sd", 1))
                link(dve.reciprocal(rstd[:, :], sd[:, :]))
                for t in range(T):
                    dve.tensor_scalar(r[:, t, 0:384], r[:, t, 0:384], rstd[:, t:t + 1], None, ALU.mult)
                    dve.tensor_scalar(r[:, t, O_MOBA:D], r[:, t, O_MOBA:D], rstd[:, 2 + t:3 + t], None, ALU.mult).then_inc(
                        sem("x"), 1)
                split_x(f"mix{l}", COLS[f"mix{l}"])
                advance(AT[f"o{l}"] + 3 + LEAD)
                residual(f"o{l}", (used, AT[f"o{l}"] + 4), r, ALPHA, 1.0)
                layer_norm(f"ln1_{l}", 2 + 4 * l)
                split_x(f"ln1_{l}")
                if l == 1:
                    advance(AT["router"] + LEAD)
                    dve.wait_ge(used, AT["router"] + 1)
                    link(dve.tensor_copy(lg[:, 0], ps[3][:, 0:T * NE].rearrange("p (t e) -> p t e", t=T)))
                    dve.tensor_reduce(small[:, 0, 0:T], lg[:, 0], AX, ALU.max, negate=True).then_inc(sem("rt_max"), 1)
                    tri8 = const("tri8").rearrange("p (e f) -> p e f", e=NE)
                    for t in range(T):
                        mine = lg[:, 0, t].unsqueeze(2).to_broadcast([P, NE, NE])
                        other = lg[:, 0, t].unsqueeze(1).to_broadcast([P, NE, NE])
                        dve.tensor_tensor(lg3[:, 0, t], other, mine, ALU.is_gt)
                        link(dve.tensor_tensor(lg3[:, 1, t], other, mine, ALU.is_equal))
                        link(dve.tensor_tensor(lg3[:, 1, t], lg3[:, 1, t], tri8, ALU.mult))
                        link(dve.tensor_tensor(lg3[:, 0, t], lg3[:, 0, t], lg3[:, 1, t], ALU.add))
                        link(dve.tensor_reduce(lg[:, 2, t], lg3[:, 0, t], AX, ALU.add))
                    link(dve.tensor_scalar(lg[:, 3], lg[:, 2], 2.0, None, ALU.is_lt))
                    dve.wait_ge(sem("rt_exp"), T)
                    link(dve.tensor_tensor(lg[:, 4], lg[:, 1], lg[:, 3], ALU.mult))
                    link(dve.tensor_reduce(small[:, 1, 0:T], lg[:, 4], AX, ALU.add))
                    link(dve.reciprocal(small[:, 2, 0:T], small[:, 1, 0:T]))
                    for t in range(T):
                        link(dve.tensor_scalar(lg[:, 5, t], lg[:, 4, t], small[:, 2, t:t + 1], None, ALU.mult))
                        link(dve.tensor_copy(gexp[:, :, t].rearrange("p (e n) -> p e n", e=NE),
                                             lg[:, 5, t].unsqueeze(2).to_broadcast([P, NE, U_MOE // 2 // NE])))
                ffn(f"f{l}", U_MOE if l else U_FF, gated=(l == 1))
                residual(f"f{l}", (used, AT[f"f{l}"] + 3 * (U_MOE if l else U_FF)), r, ALPHA, 1.0)
                layer_norm(f"ln2_{l}", 4 + 4 * l)
                if l == 0:
                    split_x(f"ln2_{l}")

            rms_scale("n1", x)
            split_x("n1", COLS["ffn1"])
            ffn("f2", U_FF)
            ang, turns, red = rot[:, 0], rot[:, 1], rot[:, 2]
            dve.wait_ge(sem("pos_in"), 16)
            link(dve.tensor_copy(small[:, 3, 0:T], posi[:, :]))
            for t in range(T):
                link(dve.tensor_scalar(ang[:, t], const("inv_freq"), small[:, 3, t:t + 1], None, ALU.mult))
            magic = 1.5 * 2.0 ** 23
            link(dve.tensor_scalar(turns, ang, float(1 / (2 * np.pi)), magic, ALU.mult, ALU.add))
            link(dve.tensor_scalar(turns, turns, magic, None, ALU.subtract))
            two_pi = 2 * np.pi
            p1 = 6.28125
            p2 = float(np.floor((two_pi - p1) * 2 ** 21) / 2 ** 21)
            p3 = float(np.float32(two_pi - p1 - p2))
            link(dve.scalar_tensor_tensor(out=red, in0=turns, scalar=-p1, in1=ang, op0=ALU.mult, op1=ALU.add))
            link(dve.scalar_tensor_tensor(out=red, in0=turns, scalar=-p2, in1=red, op0=ALU.mult, op1=ALU.add))
            link(dve.scalar_tensor_tensor(out=red, in0=turns, scalar=-p3, in1=red, op0=ALU.mult, op1=ALU.add))
            lim = 3.1415925
            dve.tensor_scalar(red, red, lim, -lim, ALU.min, ALU.max).then_inc(sem("angle"), 1)
            residual("f2", (used, AT["f2"] + 3 * U_FF), x, 1.0, 0.5)
            dve.wait_ge(sem("sines"), 2)
            cosr, sinr = rot[:, 3], rot[:, 4]
            link(dve.tensor_tensor(rot[:, 5], rot[:, 5], rot[:, 5], ALU.mult))
            link(dve.tensor_scalar(cosr, rot[:, 5], -2.0, 1.0, ALU.mult, ALU.add))
            rms_scale("nmix", x)
            split_x("nmix", COLS["in2"])
            for g in range(5):
                advance(AT["in2"] + 2 * g + 1 + LEAD)
                if g >= 2:
                    evac("in2", g, 1, h[:, 1, 512 * g:512 * g + 512], 512, 2 * (g % 2) + 1)
                if g == 0:
                    dve.wait_ge(sem("ws_in"), 16)
                    dve.tensor_tensor(ws, ws, const("tril").unsqueeze(1).to_broadcast([P, 8, P]), ALU.mult).then_inc(
                        sem("ws_masked"), 1)
                if g == 2:
                    dve.wait_ge(*at("in2", "ev0", 4))
                    dve.wait_ge(sem("rows10"), 16)
                    gv = gs[:, :, :].rearrange("p s (t h) -> p s t h", t=T)
                    for t in range(T):
                        v = h[:, t, 512:1024].rearrange("p (h d) -> p h d", d=HD)
                        sq = r[:, t, 0:512].rearrange("p (h d) -> p h d", d=HD)
                        link(dve.tensor_reduce(gv[:, 0, t], v, AX, ALU.add))
                        link(dve.tensor_scalar(gv[:, 0, t], gv[:, 0, t], 1.0 / HD, None, ALU.mult))
                        link(dve.tensor_tensor(v, v, gv[:, 0, t].unsqueeze(2).to_broadcast([P, 8, HD]), ALU.subtract))
                        link(dve.tensor_tensor(sq, v, v, ALU.mult))
                        m = dve.tensor_reduce(gv[:, 1, t], sq, AX, ALU.add)
                        if t == 0:
                            link(m)
                    m.then_inc(sem("sgu_var"), 1)
            last = AT["in2"] + 9
            dve.wait_ge(*at("sgu", "sd", 1))
            link(dve.reciprocal(gs[:, 3, :], gs[:, 2, :]))
            for t in range(T):
                v = h[:, t, 512:1024].rearrange("p (h d) -> p h d", d=HD)
                link(dve.tensor_tensor(v, v, gv[:, 3, t].unsqueeze(2).to_broadcast([P, 8, HD]), ALU.mult))
                link(dve.tensor_tensor(h[:, t, 512:1024], h[:, t, 512:1024], bc[:, 0, 0:512], ALU.mult))
                m = dve.tensor_tensor(h[:, t, 512:1024], h[:, t, 512:1024], bc[:, 0, 512:1024], ALU.add)
                if t == 0:
                    link(m)
            m.then_inc(sem("v_norm"), 1)
            dve.wait_ge(*at("in2", "ev0", 7))
            dve.wait_ge(*at("in2", "ev1", 3))
            for t in range(T):
                v = h[:, t, 1024:2048].rearrange("p (h d) -> p h d", d=HD)
                tmp = [r[:, 0, 512 + P * a:512 + P * (a + 1)].rearrange("p (h d) -> p h d", d=8) for a in range(4)]
                cos, sin = (c[:, t].unsqueeze(1).to_broadcast([P, 16, 8]) for c in (cosr, sinr))
                rotate(v[:, :, 0:8], v[:, :, 8:16], cos, sin, tmp)
            dve.sem_inc(sem("rot_done"), 1)
            dve.wait_ge(sem("mixed"), 1)
            for g in range(8):
                m = dve.scalar_tensor_tensor(
                    out=r[:, :, HD * g:HD * (g + 1)],
                    in0=ps[6 + g // 4][:, (g % 4) * P:(g % 4 + 1) * P].rearrange("p (t d) -> p t d", t=T),
                    scalar=cols[:, COLS["b_s"] + g:COLS["b_s"] + g + 1], in1=h[:, :, HD * g:HD * (g + 1)],
                    op0=ALU.add, op1=ALU.mult)
            m.then_inc(sem("ya"), 1)
            heads("dil", [("dil", n) for n in range(DIL_H)], last)
            dve.wait_ge(*at("mix2", "sd", 1))
            link(dve.reciprocal(rstd[:, :], sd[:, :]))
            for t in range(T):
                dve.tensor_scalar(r[:, t, 0:512], r[:, t, 0:512], rstd[:, t:t + 1], None, ALU.mult)
                dve.tensor_scalar(r[:, t, 512:D], r[:, t, 512:D], rstd[:, 2 + t:3 + t], None, ALU.mult).then_inc(
                    sem("x"), 1)
            split_x("mix2", COLS["out2"])
            advance(AT["out2"] + 3 + LEAD)
            residual("out2", (used, AT["out2"] + 4), x, 1.0, 1.0)
            rms_scale("nmem", r)
            split_x("nmem", COLS["mem"])
            advance(AT["wk"] + 3 + LEAD)
            for g in range(2):
                advance(AT["wv"] + 2 * g + 1 + LEAD)
                evac("wv", g, 1, xv[:, 1, 512 * g:512 * g + 512], 512, 2 * g + 1)
            rms_scale("ncross", x)
            split_x("ncross", COLS["cross"])
            last = AT["wq"] + 3
            advance(last + LEAD)
            for i in range(X_H + 2):
                if i < X_H:
                    dve.wait_ge(sem("x_s"), i + 1)
                    link(dve.tensor_reduce(nmax[:, i, :], ps[2 + i % 2][:, :].rearrange("p (t m) -> p t m", t=T), AX, ALU.max,
                                           negate=True))
                    dve.tensor_scalar(nmax[:, i, :], nmax[:, i, :], X_D ** -0.5, None, ALU.mult).then_inc(sem("x_mx"), 1)
                if 1 <= i < X_H + 1:
                    n = i - 1
                    dve.wait_ge(sem("x_tp"), n + 1)
                    if n >= 2:
                        dve.wait_ge(sem("x_od"), n - 1)
                    dve.tensor_copy(probt[:, n % 2, :], ps[4 + n % 2][:, :]).then_inc(sem("x_pt"), 1)
                if i >= 2:
                    n = i - 2
                    dve.wait_ge(sem("x_od"), n + 1)
                    link(dve.reciprocal(rinv[:, n, :], rsum[:, n, :]))
                    for t in range(T):
                        m = dve.tensor_scalar(bc[:, t, n * X_D:(n + 1) * X_D], ps[6 + n % 2][:, t * X_D:(t + 1) * X_D],
                                              rinv[:, n, t:t + 1], None, ALU.mult)
                        if n < X_H - 1 and t == T - 1:
                            m.then_inc(sem("x_o"), 1)
                        if n == X_H - 1:
                            m.then_inc(sem("x"), 1)
                advance(last + 1 + i if i < SPLIT else 0)
            split_x("xo")
            advance(AT["xo"] + 3 + LEAD)
            residual("xo", (used, AT["xo"] + 4), x, 1.0, 1.0)
            rms_scale("n2", x)
            split_x("n2", COLS["ffn2"])
            ffn("f3", U_FF)
            residual("f3", (used, AT["f3"] + 3 * U_FF), x, 1.0, 0.5)
            dve.wait_ge(*at("fin", "sd", 1))
            dve.wait_ge(sem("rows11"), 16)
            link(dve.reciprocal(rstd[:, 0:T], sd[:, 0:T]))
            for t in range(T):
                dve.scalar_tensor_tensor(out=r[:, t, :], in0=x[:, t, :], scalar=rstd[:, t:t + 1], in1=bc[:, 0, :],
                                         op0=ALU.mult, op1=ALU.mult).then_inc(sem("final"), 1)


def shape_constants():
    f = np.float32
    i = np.arange(S)[:, None]
    j = np.arange(S)[None, :]
    parts = {}
    log_gamma = np.log(f(1.0) - f(2.0) ** (-f(5.0) - np.arange(RET_H, dtype=f)))
    dist = np.maximum(i.T - np.arange(P)[:, None], 0).astype(f)
    decay = np.exp(log_gamma[:, None, None] * dist) * (i.T >= np.arange(P)[:, None]) * f(HD ** -0.5)
    parts["ret"] = decay.transpose(1, 0, 2)

    def tiles(m):
        return np.concatenate([m[0:P, 0:P], m[P:S, :]], axis=1)

    causal = np.where(j <= i, 0.0, NEG)
    parts["mla"] = tiles(causal)
    slopes = f(2.0) ** (f(-8.0) * (np.arange(MOBA_H, dtype=f) + 1) / f(MOBA_H))
    parts["moba"] = np.stack([tiles(np.where(j <= i, -s * (i - j).astype(f), NEG)) for s in slopes], axis=1)
    count = sum(((j <= i) & ((i - j) % d == 0) & (i - j <= w)).astype(f) for w, d in ((128, 1), (512, 4), (2048, 16)))
    parts["dil"] = tiles(np.where(count > 0, np.log(np.maximum(count, 1)), NEG))
    for name, dim in (("a", 32), ("b", 64)):
        inv = f(10000.0) ** (-np.arange(0, dim, 2, dtype=f) / f(dim))
        ang = np.arange(S, dtype=f)[:, None] * inv[None, :]
        for fn, g in (("cos", np.cos), ("sin", np.sin)):
            parts[f"{fn}_{name}"] = g(ang).reshape(T, P, dim // 2).transpose(1, 0, 2)
    inv = f(500000.0) ** (f(-2.0) * np.arange(8, dtype=f) / f(16))
    parts["inv_freq"] = np.broadcast_to(inv, (P, 8))
    parts["ident"] = np.eye(P)
    parts["tril"] = np.tril(np.ones((P, P)))
    parts["tri8"] = np.broadcast_to(np.tril(np.ones((NE, NE)), -1).reshape(1, 64), (P, 64))
    return np.concatenate([np.asarray(parts[n], f).reshape(P, -1) for n, _ in CONST_PARTS], axis=1)


def lay_out_stream(a):
    big = np.zeros((NCHUNK, P, CW), np.float32)

    def project(name, w):
        n = AT[name]
        for c in range(0, w.shape[1], 512):
            part = w[:, c:c + 512]
            wide = part.shape[1]
            v = part.reshape(KD, P, wide).transpose(1, 0, 2)
            if wide == 512:
                big[n] = v[:, 0:4].reshape(P, CW)
                big[n + 1] = v[:, 4:8].reshape(P, CW)
                n += 2
            else:
                big[n, :, 0:KD * wide] = v.reshape(P, KD * wide)
                n += 1

    def ffn(name, gate, up, down):
        units = gate.shape[0] * gate.shape[2] // FU
        per = units // gate.shape[0]
        first_chunk = AT[name]
        for u in range(units):
            e, c = u // per, (u % per) * FU
            gu = np.concatenate([gate[e, :, c:c + FU].reshape(KD, P, FU), up[e, :, c:c + FU].reshape(KD, P, FU)], axis=2)
            v = gu.transpose(1, 0, 2)
            first = first_chunk + max(3 * u - 1, 0)
            big[first] = v[:, 0:4].reshape(P, CW)
            big[first + 1] = v[:, 4:8].reshape(P, CW)
            last = first_chunk + (3 * u + 4 if u < units - 1 else 3 * u + 2)
            big[last] = down[e, c:c + FU].reshape(2, P, D).transpose(1, 0, 2).reshape(P, CW)

    for l in range(DEPTH):
        project(f"in{l}", a["w_in"][l])
        big[AT[f"uq{l}"], :, 0:1152] = a["w_uq"][l].reshape(2, P, 576).transpose(1, 0, 2).reshape(P, 1152)
        big[AT[f"ukv{l}"], :, 0:768] = a["w_ukv"][l]
        project(f"o{l}", a["w_o"][l])
    ffn("f0", a["ffn_w_gate"], a["ffn_w_up"], a["ffn_w_down"])
    big[AT["router"], :, 0:KD * NE] = a["router"][0].reshape(KD, P, NE).transpose(1, 0, 2).reshape(P, KD * NE)
    ffn("f1", a["exp_w_gate"][0], a["exp_w_up"][0], a["exp_w_down"][0])
    ffn("f2", a["ffn1_w_gate_2"], a["ffn1_w_up_2"], a["ffn1_w_down_2"])
    project("in2", a["w_in_2"][0])
    project("out2", a["w_out_2"][0])
    project("wk", a["cross_wk_2"][0])
    project("wv", a["cross_wv_2"][0])
    project("wq", a["cross_wq_2"][0])
    project("xo", a["cross_wo_2"][0])
    ffn("f3", a["ffn2_w_gate_2"], a["ffn2_w_up_2"], a["ffn2_w_down_2"])
    return big


def kernel(**inputs):
    import concourse.bacc as bacc
    from concourse.bass_utils import run_bass_kernel_spmd

    a = {k: np.asarray(v) for k, v in inputs.items()}
    one = np.ones(O_MOBA - O_RET, np.float32)
    gains = []
    for l in range(DEPTH):
        gains += [a["q_norm_g"][l], a["kv_norm_g"][l], a["beta_mla"][l], one, a["beta_moba"][l]]
    gains += [a["ffn1_norm_2"][0], a["mix_norm_2"][0], a["out_norm_a_2"][0], a["out_norm_b_2"][0], a["cross_norm_2"][0],
              a["mem_norm_2"][0], a["ffn2_norm_2"][0], a["sgu_b_s_2"][0].reshape(-1)]
    rows = [a["ln_emb_g"], a["ln_emb_b"]]
    for l in range(DEPTH):
        rows += [a["ln1_g"][l], a["ln1_b"][l], a["ln2_g"][l], a["ln2_b"][l]]
    rows += [np.concatenate([a["sgu_ln_g_2"][0], a["sgu_ln_b_2"][0]]), a["final_norm_2"]]
    arrays = {
        "stream": lay_out_stream(a),
        "x": a["x"][0],
        "mem": a["mem_2"][0],
        "positions": np.ascontiguousarray(a["positions_2"][0].reshape(T, P).T),
        "consts": shape_constants(),
        "cols": np.ascontiguousarray(np.concatenate(gains).reshape(NCOL, P).T),
        "rows": np.stack(rows),
        "spatial": a["sgu_w_s_2"][0],
    }
    nc = bacc.Bacc("TRN2", target_bir_lowering=False, num_devices=1)
    args = [nc.dram_tensor(f"in_{n}", v.shape, mybir.dt.from_np(v.dtype), kind="ExternalInput").ap() for n, v in arrays.items()]
    out = nc.dram_tensor("out", (S, D), F32, kind="ExternalOutput").ap()
    program(nc, *args, out)
    result = run_bass_kernel_spmd(nc, [{f"in_{n}": v for n, v in arrays.items()}], core_ids=[0])
    return result.results[0]["out"].reshape(1, S, D)
```

```python
from contextlib import ExitStack
from math import lcm

import numpy as np

import concourse.bass as bass
from concourse import mybir

ALU = mybir.AluOpType
ACT = mybir.ActivationFunctionType
F32 = mybir.dt.float32
F32R = mybir.dt.float32r
I32 = mybir.dt.int32
AX = mybir.AxisListType.X

P = 128
T = 2
S = T * P
D = 1024
KD = D // P
CW = 2048
RAW = 6
SPLIT = 3
LEAD = SPLIT - 1
FU = 256
UNROLL = lcm(RAW, SPLIT, 3) // 3
LB = 3 * UNROLL

DEPTH = 2
ALPHA = (2 * DEPTH) ** 0.25
LN_EPS = 1e-5
RMS_EPS = 1e-6
MLA_H, NOPE, ROPE = 6, 64, 32
QD = NOPE + ROPE
RET_H = MOBA_H = 5
HD = 64
DIL_H = 8
X_H, X_D = 4, 256
D_IN = 2656
D_IN2 = 2560
C_ROPE, C_RQ, C_RK, C_RV, C_RG, C_MQ, C_MK, C_MV = 384, 416, 736, 1056, 1376, 1696, 2016, 2336
O_RET, O_MOBA = 384, 704
D_FF, D_FFE, NE = 2816, 3584, 8
U_FF = D_FF // FU
U_E = D_FFE // FU
U_MOE = NE * U_E
ROUNDS_E = 3 * U_E // RAW
GATHER_AT = (6, 9)
NEG = -1e30

CONST_PARTS = [("ret", RET_H * S), ("moba", MOBA_H * 384), ("mla", 384), ("dil", 384), ("cos_a", T * 16),
               ("sin_a", T * 16), ("cos_b", T * 32), ("sin_b", T * 32), ("inv_freq", 8), ("ident", P),
               ("tril", P), ("tri8", 64)]
CONST_AT, CONST_W = {}, 0
for _name, _w in CONST_PARTS:
    CONST_AT[_name] = (CONST_W, CONST_W + _w)
    CONST_W += _w

COLS = {}
_n = 0
for _name, _w in [("q0", 2), ("kv0", 1), ("mix0", 8), ("q1", 2), ("kv1", 1), ("mix1", 8), ("ffn1", 8),
                  ("in2", 8), ("out2", 8), ("cross", 8), ("mem", 8), ("ffn2", 8), ("b_s", 8)]:
    COLS[_name] = _n
    _n += _w
NCOL = _n

PROJ = [CW] * 2


def ffn_widths(units):
    return [CW] * (3 * units)


STREAM = []
for _l in range(DEPTH):
    STREAM += [(f"in{_l}", PROJ * 5 + [KD * 96]), (f"uq{_l}", [2 * 576]), (f"ukv{_l}", [768]), (f"o{_l}", PROJ * 2)]
    STREAM += [("f0", ffn_widths(U_FF))] if _l == 0 else [("router", [KD * NE]), ("f1", ffn_widths(U_MOE))]
STREAM += [("f2", ffn_widths(U_FF)), ("in2", PROJ * 5), ("out2", PROJ * 2), ("wk", PROJ * 2), ("wv", PROJ * 2),
           ("wq", PROJ * 2), ("xo", PROJ * 2), ("f3", ffn_widths(U_FF))]
AT, WIDTH = {}, []
for _name, _ws in STREAM:
    AT[_name] = len(WIDTH)
    WIDTH += _ws
NCHUNK = len(WIDTH)
STREAM_LENGTH = [(_name, len(_ws)) for _name, _ws in STREAM]


LAYERS = range(DEPTH)
N_HEADS = RET_H + MOBA_H + MLA_H
N_SOFT = MOBA_H + MLA_H


def _by_layer(*parts, skip=()):
    return [(f"{n}{l}", c) for l in LAYERS for n, c in parts if f"{n}{l}" not in skip]


_ffns = [("f0", U_FF), ("f2", U_FF), ("f3", U_FF)]
RAISED = {
    "tr": [("emb", 4)] + _by_layer(("lat", 2), ("mix", 4), ("ln1_", 4), ("ln2_", 4), skip=("ln2_1",))
    + [(n, 4) for n in ("n1", "nmix", "mix2", "nmem", "ncross", "xo", "n2")],
    "xh": [("emb", 4)] + _by_layer(("lat", 3), ("mix", KD), ("ln1_", 4), ("ln2_", 4), skip=("ln2_1",))
    + [(n, 4 if n == "xo" else KD) for n in ("n1", "nmix", "mix2", "nmem", "ncross", "xo", "n2")],
    "xt": [("emb", 4)] + _by_layer(("lat", 2), ("mix", KD), ("ln1_", 4), ("ln2_", 4), skip=("ln2_1",))
    + [(n, 4 if n == "xo" else KD) for n in ("n1", "nmix", "mix2", "nmem", "ncross", "xo", "n2")],
    "sd": [("emb", 1)] + _by_layer(("lat", 1), ("mix", 1), ("ret", 1), ("ln1_", 1), ("ln2_", 1))
    + [(n, 1) for n in ("n1", "nmix", "sgu", "mix2", "nmem", "ncross", "n2", "fin")],
    "x": [("emb", T)] + _by_layer(("lat", T), ("mix", T), ("ln1_", T), ("ln2_", T))
    + [(n, T) for n in ("n1", "nmix", "mix2", "nmem", "ncross", "xo", "n2")],
    "mv": [("emb", T)] + _by_layer(("ln1_", T), ("ln2_", T)),
    "pj": _by_layer(("in", 6), ("o", 2)) + [("in2", 5), ("out2", 2), ("wk", 6), ("wv", 2), ("wq", 6), ("xo", 2)],
    "ev0": _by_layer(("in", 6)) + [("in2", 7), ("wv", 2)],
    "ev1": _by_layer(("in", 6)) + [("in2", 3), ("wv", 2)],
    "ev": _by_layer(("uq", 4)) + [("wk", KD), ("wq", KD)],
    "resid": [(n, 4) for n in ("o0", "f0", "o1", "f1", "f2", "out2", "xo", "f3")],
}
for _k in ("tq", "qk", "s", "pt", "od", "o"):
    RAISED[_k] = [("at0", N_HEADS), ("at1", N_HEADS), ("dil", DIL_H)]
for _k in ("sf", "mx", "p", "tp"):
    RAISED[_k] = [("at0", N_SOFT), ("at1", N_SOFT), ("dil", DIL_H)]
UNIT_KINDS = ("sg", "hu", "ut", "hh", "ht")
for _k, _c in (("sg", T), ("hu", T), ("ut", 1), ("hh", 1), ("ht", 1)):
    RAISED[_k] = [(n, _c * u) for n, u in _ffns]


def before(stage, kind):
    total = 0
    for name, count in RAISED[kind]:
        if name == stage:
            return total
        total += count
    raise KeyError((stage, kind))


class Chunk:

    def __init__(self, base, it=0):
        self.raw = base % RAW
        self.split = base % SPLIT
        self.width = WIDTH[base]
        self.base = base
        self.n = base + LB * it
        self.landed = 16 * (base // RAW + 1) + (16 * (LB // RAW)) * it


def heads_of_layer():
    return ([("ret", n) for n in range(RET_H)] + [("moba", n) for n in range(MOBA_H)]
            + [("mla", n) for n in range(MLA_H)])


def program(nc, stream, x_in, mem_in, pos_in, consts, route_in, cols_in, rows_in, ws_in, out):
    with ExitStack() as ctx:
        def sb(name, shape, dt=F32):
            return ctx.enter_context(nc.sbuf_tensor(name, shape, dt))

        sems = {}

        def sem(name):
            if name not in sems:
                sems[name] = ctx.enter_context(nc.semaphore(name))
            return sems[name]

        def at(stage, kind, count):
            if stage == "f1" and kind in UNIT_KINDS:
                return sem(f"f1_{kind}"), count
            return sem(kind), count + before(stage, kind)

        def unit_sem(stage, kind):
            return sem(f"f1_{kind}" if stage == "f1" else kind)

        def group_done(name, g, t):
            if t < T - 1:
                return at(name, "pj", g + 1)
            return used, AT[name] + min(2 * g + 2, dict(STREAM_LENGTH)[name])

        def tile_done(name, j):
            if j % 4 < 3:
                return at(name, "pj", 3 * (j // 4) + j % 4 + 1)
            return used, AT[name] + 2 * (j // 4) + 2

        raw = sb("raw", [P, RAW, CW])
        whi = sb("whi", [P, SPLIT, CW], F32R)
        wlo = sb("wlo", [P, SPLIT, CW], F32R)
        x = sb("resid", [P, T, D])
        r = sb("r", [P, T, D])
        xth = sb("xth", [P, KD, S], F32R)
        xtl = sb("xtl", [P, KD, S], F32R)
        h = sb("h", [P, T, D_IN])
        qc = sb("qc", [P, T, MLA_H, QD])
        kc = sb("kc", [P, T, MLA_H, QD])
        vc = sb("vc", [P, T, MLA_H, NOPE])
        qkt = sb("qkt", [P, 2, 512])
        prob = sb("prob", [P, 2, 512])
        probt = sb("probt", [P, 2, 512])
        hth = sb("hth", [P, 3, S], F32R)
        htl = sb("htl", [P, 3, S], F32R)
        bc = sb("bc", [P, 2, D])
        cst = sb("cst", [P, CONST_W])
        cols = sb("cols", [P, NCOL])
        bn = sb("bn", [P, T, 2, 6])
        mv = sb("mv", [P, T, 2])
        nmax = sb("nmax", [P, 16, T])
        rsum = sb("rsum", [P, 16, T])
        rinv = sb("rinv", [P, 16, T])
        ss = sb("ss", [P, 4])
        sd = sb("sd", [P, 4])
        rstd = sb("rstd", [P, 4])
        gs = sb("gs", [P, 4, 16])
        eps = sb("eps", [P, 2])
        flag = sb("flag", [P, 1], I32)
        small = sb("small", [P, 8, 16])
        lg = sb("lg", [P, 8, T, NE])
        posi = sb("posi", [P, T], I32)
        rot = sb("rot", [P, 6, T, 8])
        ps = [ctx.enter_context(nc.psum_tensor(f"ps{b}", [P, 512], F32)) for b in range(8)]

        def const(name):
            a, b = CONST_AT[name]
            return cst[:, a:b]

        ident = const("ident")
        c_ret = const("ret").rearrange("p (h i) -> p h i", h=RET_H)
        c_moba = const("moba").rearrange("p (h i) -> p h i", h=MOBA_H)
        sg = prob[:, :, 0:FU]
        hs = probt[:, :, 0:FU]
        hflat = h[:, :, :].rearrange("p t n -> p (t n)")
        onehot = hflat[:, 0:NE * S].rearrange("p (e t s) -> p e t s", e=NE, t=T)
        spread = hflat[:, NE * S:2 * NE * S].rearrange("p (e s) -> p e s", e=NE)
        spread_now = hflat[:, 2 * NE * S:2 * NE * S + S]
        route = hflat[:, 2 * NE * S + S:2 * NE * S + S + 4 * P].rearrange("p (n s) -> p n s", n=4)
        earlier, ones, slots, zeros = (route[:, n, :] for n in range(4))
        gated = r[:, :, :].rearrange("p t n -> p (t n)").rearrange("p (e t s) -> p e t s", e=NE, t=T)
        gexp = qkt[:, 0, 0:U_MOE].rearrange("p (n t) -> p n t", t=T)
        lg3 = qkt[:, 1, 0:4 * NE * NE].rearrange("p (a t e f) -> p a t e f", a=2, t=T, e=NE)
        kt = hflat[:, 0:KD * S].rearrange("p (k s) -> p k s", k=KD)
        xv = hflat[:, KD * S:2 * KD * S].rearrange("p (t n) -> p t n", t=T)
        qt = r[:, :, :].rearrange("p t n -> p (t n)").rearrange("p (k s) -> p k s", k=KD)
        ws = kc[:, :, :, :].rearrange("p t h d -> p (t h d)")[:, 0:8 * P].rearrange("p (g j) -> p g j", g=8)
        wst = qc[:, :, :, :].rearrange("p t h d -> p (t h d)")[:, 0:8 * P].rearrange("p (g j) -> p g j", g=8)

        landed = [sem(f"landed{n}") for n in range(RAW)]
        hi_done = sem("hi_done")
        lo_done = sem("lo_done")
        used = sem("used")

        def f32(ap):
            return ap.bitcast(F32)

        block = ctx.enter_context(nc.Block())

        @block.sync
        def _(sp):
            def load(c):
                if not (isinstance(c.n, int) and c.n < RAW):
                    sp.wait_ge(lo_done, c.n - RAW + 1)
                sp.dma_start(raw[:, c.raw, 0:c.width], stream[c.n, :, 0:c.width]).then_inc(landed[c.raw], 16)

            n = 0
            while n < NCHUNK:
                if any(n == AT[f] for f in ("f0", "f1", "f2", "f3")):
                    name = next(f for f in ("f0", "f1", "f2", "f3") if n == AT[f])
                    loops = 3 * (U_MOE if name == "f1" else U_FF) // LB
                    with sp.Fori(0, loops) as it:
                        for j in range(LB):
                            load(Chunk(n + j, it))
                    n += loops * LB
                else:
                    load(Chunk(n))
                    n += 1

        @block.gpsimd
        def _(pool):
            pool.memset(eps[:, 0:1], LN_EPS).then_inc(sem("eps_set"), 1)
            pool.memset(eps[:, 1:2], RMS_EPS).then_inc(sem("eps_set"), 1)
            pool.dma_start(r[:, :, :], x_in.rearrange("(t p) d -> p t d", p=P)).then_inc(sem("x_in"), 16)
            pool.dma_start(cst[:, :], consts).then_inc(sem("const_in"), 16)
            pool.dma_start(cols[:, :], cols_in).then_inc(sem("cols_in"), 16)
            pool.dma_start(posi[:, :], pos_in).then_inc(sem("pos_in"), 16)

            def rows(n, count, free, value):
                if free:
                    pool.wait_ge(*at(free[0], free[1], value))
                pool.dma_start(bc[:, 0:count, :], rows_in[n:n + count, :].partition_broadcast(P)).then_inc(
                    sem(f"rows{n}"), 16)

            rows(0, 2, None, 0)
            for l in range(DEPTH):
                rows(2 + 4 * l, 2, ("emb" if l == 0 else "ln2_0", "x"), T)
                rows(4 + 4 * l, 2, (f"ln1_{l}", "x"), T)
                if l == 1:
                    pool.wait_ge(*at("mix1", "x", T))
                    pool.dma_start(route, route_in.rearrange("p (n s) -> p n s", n=4)).then_inc(sem("route_in"), 16)
            rows(10, 1, ("ln2_1", "x"), T)
            pool.wait_ge(*at("ln2_1", "x", T))
            pool.dma_start(ws, ws_in.rearrange("g i j -> i g j")).then_inc(sem("ws_in"), 16)
            pool.wait_ge(*at("out2", "resid", 4))
            pool.dma_start(r[:, :, :], mem_in.rearrange("(t p) d -> p t d", p=P)).then_inc(sem("mem_in"), 16)
            rows(11, 1, ("xo", "tr"), 4)
            for t in range(T):
                pool.wait_ge(sem("final"), t + 1)
                pool.dma_start(out[t * P:(t + 1) * P, :], r[:, t, :]).then_inc(sem("stored"), 16)
            pool.wait_ge(sem("stored"), 16 * T)

        @block.tensor
        def _(pe):
            def mm3(o, ah, al, bh, bl, start, stop):
                pe.matmul(o, ah, bh, start=start, stop=False, skip_group_check=True)
                pe.matmul(o, ah, bl, start=False, stop=False, skip_group_check=True)
                return pe.matmul(o, al, bh, start=False, stop=stop, skip_group_check=True)

            def chunk(c):
                pe.wait_ge(lo_done, c.n + 1)

            def transpose_x(stage, src, kn=KD, banks=(0, 1, 2, 3)):
                for t in range(T):
                    pe.wait_ge(*at(stage, "x", t + 1))
                    for k in range(kn):
                        m = pe.transpose(ps[banks[k // 2]][:, (k % 2) * S + t * P:(k % 2) * S + (t + 1) * P],
                                         src[:, t, k * P:(k + 1) * P], ident)
                        if t == T - 1 and (k % 2 == 1 or k == kn - 1):
                            m.then_inc(sem("tr"), 1)

            def project(name, stage, ah, al, groups, kn, bank, ready, free):
                pe.wait_ge(*at(ready[0], "xt", ready[1]))
                n = AT[name]
                for g, (width, chunks) in enumerate(groups):
                    per = kn // chunks
                    for j in range(chunks):
                        c = Chunk(n)
                        n += 1
                        chunk(c)
                        wh = whi[:, c.split, 0:per * width].rearrange("p (k n) -> p k n", k=per)
                        wl = wlo[:, c.split, 0:per * width].rearrange("p (k n) -> p k n", k=per)
                        for t in range(T):
                            if j == 0:
                                free(g, t)
                            for k in range(per):
                                kk = j * per + k
                                m = mm3(ps[bank(g, t)][:, 0:width], ah[:, kk, t * P:(t + 1) * P],
                                        al[:, kk, t * P:(t + 1) * P], wh[:, k, :], wl[:, k, :],
                                        start=(kk == 0), stop=(kk == kn - 1))
                            if j == chunks - 1 and t < T - 1:
                                m.then_inc(sem("pj"), 1)
                        m.then_inc(used, 1)

            def project_t(name, stage, ready, free):
                pe.wait_ge(*at(ready[0], "xt", ready[1]))
                for g in range(2):
                    for j in range(2):
                        c = Chunk(AT[name] + 2 * g + j)
                        chunk(c)
                        wh = whi[:, c.split, :].rearrange("p (k n) -> p k n", k=4)
                        wl = wlo[:, c.split, :].rearrange("p (k n) -> p k n", k=4)
                        for q in range(4):
                            if j == 0:
                                free(4 * g + q)
                            for k in range(4):
                                kk = 4 * j + k
                                m = mm3(ps[4 * g + q][:, 0:S], wh[:, k, q * P:(q + 1) * P], wl[:, k, q * P:(q + 1) * P],
                                        xth[:, kk, :], xtl[:, kk, :], start=(kk == 0), stop=(kk == 7))
                            if j == 1 and q < 3:
                                m.then_inc(sem("pj"), 1)
                        m.then_inc(used, 1)

            def ffn(name, units):
                first_chunk = AT[name]

                def gate_up(a, b):
                    for j, c in enumerate((a, b)):
                        chunk(c)
                        wh = whi[:, c.split, :].rearrange("p (k n) -> p k n", k=4)
                        wl = wlo[:, c.split, :].rearrange("p (k n) -> p k n", k=4)
                        for t in range(T):
                            for k in range(4):
                                kk = 4 * j + k
                                m = mm3(ps[t][:, :], xth[:, kk, t * P:(t + 1) * P], xtl[:, kk, t * P:(t + 1) * P],
                                        wh[:, k, :], wl[:, k, :], start=(kk == 0), stop=(kk == 7))
                        m.then_inc(used, 1)

                def down(c, u, first, last):
                    chunk(c)
                    pe.wait_ge(*at(name, "ht", u + 1))
                    wh = whi[:, c.split, :].rearrange("p (k n) -> p k n", k=2)
                    wl = wlo[:, c.split, :].rearrange("p (k n) -> p k n", k=2)
                    for t in range(T):
                        for n in range(2):
                            for k in range(2):
                                m = mm3(ps[4 + 2 * t + n][:, :], hth[:, k, t * P:(t + 1) * P], htl[:, k, t * P:(t + 1) * P],
                                        wh[:, k, n * 512:(n + 1) * 512], wl[:, k, n * 512:(n + 1) * 512],
                                        start=first and k == 0, stop=last and k == 1)
                    m.then_inc(used, 1)

                def turn(u):
                    pe.wait_ge(*at(name, "hu", 2 * u + 2))
                    for t in range(T):
                        for k in range(2):
                            m = pe.transpose(ps[2][:, k * S + t * P:k * S + (t + 1) * P], hs[:, t, k * P:(k + 1) * P], ident)
                    m.then_inc(unit_sem(name, "ut"), 1)

                def unit(u, base, it, first):
                    gate_up(Chunk(base, it), Chunk(base + 1, it))
                    down(Chunk(base + 2, it), u - 1, first, False)
                    turn(u)

                gate_up(Chunk(first_chunk), Chunk(first_chunk + 1))
                turn(0)
                unit(1, first_chunk + 2, 0, True)
                loops = (units - 3) // UNROLL
                with pe.Fori(0, loops) as it:
                    for j in range(UNROLL):
                        unit(it * UNROLL + 2 + j, first_chunk + 5 + 3 * j, it, False)
                for u in range(2 + loops * UNROLL, units):
                    unit(u, first_chunk + 3 * u - 1, 0, False)
                down(Chunk(first_chunk + 3 * units - 1), units - 1, False, True)

            def experts():
                first_chunk = AT["f1"]

                def gather(e, q, g, bank):
                    for k in range(4):
                        for t in range(T):
                            m = pe.matmul(ps[bank][:, k * P:(k + 1) * P], x[:, t, (4 * g + k) * P:(4 * g + k + 1) * P],
                                          onehot[:, e, t, :], start=(t == 0), stop=(t == T - 1))
                    m.then_inc(sem("e_ga"), 1)

                def gate_up(q, a, b):
                    for j, c in enumerate((a, b)):
                        chunk(c)
                        wh = whi[:, c.split, :].rearrange("p (k n) -> p k n", k=4)
                        wl = wlo[:, c.split, :].rearrange("p (k n) -> p k n", k=4)
                        for k in range(4):
                            kk = 4 * j + k
                            m = mm3(ps[0][:, :], xth[:, kk, q * P:(q + 1) * P], xtl[:, kk, q * P:(q + 1) * P],
                                    wh[:, k, :], wl[:, k, :], start=(kk == 0), stop=(kk == 7))
                        m.then_inc(used, 1)

                def down(c, u, first, last):
                    chunk(c)
                    pe.wait_ge(sem("e_ht"), u + 1)
                    wh = whi[:, c.split, :].rearrange("p (k n) -> p k n", k=2)
                    wl = wlo[:, c.split, :].rearrange("p (k n) -> p k n", k=2)
                    for n in range(2):
                        for k in range(2):
                            m = mm3(ps[2 + n][:, :], hth[:, k, 0:P], htl[:, k, 0:P], wh[:, k, n * 512:(n + 1) * 512],
                                    wl[:, k, n * 512:(n + 1) * 512], start=first and k == 0, stop=last and k == 1)
                    m.then_inc(used, 1)

                def turn(u):
                    pe.wait_ge(sem("e_h"), u + 1)
                    for k in range(2):
                        m = pe.transpose(ps[1][:, k * P:(k + 1) * P], hs[:, 0, k * P:(k + 1) * P], ident)
                    m.then_inc(sem("e_ut"), 1)

                def scatter(q):
                    for t in range(T):
                        for n in range(2):
                            m = pe.matmul(ps[4 + 2 * t + n][:, :], spread_now[:, t * P:(t + 1) * P], r[:, q, n * 512:(n + 1) * 512],
                                          start=False, stop=False, skip_group_check=True)
                    m.then_inc(sem("e_sc"), 1)

                def unit(e, q, j, base, rounds, u):
                    gate_up(q, Chunk(base, rounds), Chunk(base + 1, rounds))
                    gathering = j in GATHER_AT and e is not None
                    if gathering:
                        pe.wait_ge(sem("e_ht"), u)
                        gather(e + 1, 1 - q, GATHER_AT.index(j), 1)
                    if j == 1 and not (isinstance(u, int) and u == 1):
                        pe.wait_ge(sem("e_oa"), e)
                        pe.wait_ge(sem("e_od"), e)
                    if not (isinstance(u, int) and u == 0):
                        down(Chunk(base + 2, rounds), u - 1, j == 1, j == 0)
                    if gathering:
                        pe.wait_ge(sem("e_gx"), 2 * (e + 1) + GATHER_AT.index(j) + 1)
                    turn(u)
                    if j == 1 and not (isinstance(u, int) and u == 1):
                        scatter(1 - q)

                def expert(e, q, rounds, last=False):
                    base = first_chunk - 1
                    ahead = None if last else e
                    if isinstance(e, int) and e == 0:
                        gate_up(q, Chunk(first_chunk), Chunk(first_chunk + 1))
                        turn(0)
                    else:
                        unit(e, q, 0, base, rounds, U_E * e)
                    unit(e, q, 1, base + 3, rounds, U_E * e + 1)
                    for lo_u, hi_u in ((2, 6), (6, 10), (10, U_E)):
                        if lo_u == 6:
                            for j in range(lo_u, hi_u):
                                unit(ahead, q, j, base + 3 * j, rounds, U_E * e + j)
                            continue
                        with pe.Fori(0, (hi_u - lo_u) // 2) as it:
                            for j in range(lo_u, lo_u + 2):
                                unit(None, q, j if j > 2 else -1, base + 3 * j, rounds + it, U_E * e + j + it * 2)

                for g in range(2):
                    gather(0, 0, g, g)
                pe.wait_ge(sem("rt_spread"), 4)
                for b in range(4, 8):
                    pe.matmul(ps[b][:, :], zeros[0:1, :], cst[0:1, 0:512], start=True, stop=False, skip_group_check=True)
                pe.wait_ge(sem("e_gx"), 2)
                expert(0, 0, 0)
                with pe.Fori(0, (NE - 2) // 2) as pair:
                    for s in range(2):
                        expert(pair * 2 + 1 + s, 1 - s, (pair * 2 + 1 + s) * ROUNDS_E)
                expert(NE - 1, 1, (NE - 1) * ROUNDS_E, last=True)
                down(Chunk(first_chunk + 3 * U_MOE - 1), U_MOE - 1, False, True)
                pe.wait_ge(sem("e_oa"), NE)
                pe.wait_ge(sem("e_od"), NE)
                scatter(1)

            def heads(stage, work, masked):
                soft = [kind != "ret" for kind, _ in work]

                def turn_qk(i):
                    kind, n = work[i]
                    if i >= 2:
                        pe.wait_ge(*at(stage, "qk", i - 1))
                    for s in range(2):
                        for t in range(T):
                            if kind == "mla":
                                src = (qc, kc)[s][:, t, n, :]
                            elif kind == "dil":
                                col = 1024 + 512 * s + HD * n
                                src = h[:, t, col:col + P]
                            else:
                                col = ((C_RQ, C_RK) if kind == "ret" else (C_MQ, C_MK))[s] + HD * n
                                src = h[:, t, col:col + P]
                            w = src.shape[-1]
                            m = pe.transpose(ps[i % 2][0:w, s * S + t * P:s * S + (t + 1) * P], src, ident)
                    m.then_inc(sem("tq"), 1)

                def scores(i):
                    kind, n = work[i]
                    d = QD if kind == "mla" else HD
                    q, k = qkt[0:d, i % 2, 0:S], qkt[0:d, i % 2, S:2 * S]
                    o = ps[2 + i % 2]
                    pe.wait_ge(*at(stage, "qk", i + 1))
                    if i >= 2 and soft[i - 2]:
                        pe.wait_ge(*at(stage, "sf", sum(soft[:i - 1])))
                    elif i >= 2:
                        pe.wait_ge(*at(stage, "pt", i - 1))
                    if kind == "ret":
                        pe.matmul(o[:, 0:S], k[:, 0:P], q, start=True, stop=True)
                        m = pe.matmul(o[:, S:S + P], k[:, P:S], q[:, P:S], start=True, stop=True)
                    else:
                        pe.matmul(o[:, 0:P], q[:, 0:P], k[:, 0:P], start=True, stop=True)
                        m = pe.matmul(o[:, P:P + S], q[:, P:S], k, start=True, stop=True)
                    m.then_inc(sem("s"), 1)

                def turn_p(i):
                    if not soft[i]:
                        return
                    pe.wait_ge(*at(stage, "p", sum(soft[:i + 1])))
                    for b in range(3):
                        m = pe.transpose(ps[4 + i % 2][:, b * P:(b + 1) * P], prob[:, i % 2, b * P:(b + 1) * P], ident)
                    m.then_inc(sem("tp"), 1)

                def outputs(i):
                    kind, n = work[i]
                    pt = probt[:, i % 2, :]
                    pe.wait_ge(*at(stage, "pt", i + 1))
                    if i >= 2:
                        pe.wait_ge(*at(stage, "o", i - 1))

                    def v(t):
                        if kind == "mla":
                            return vc[:, t, n, :]
                        col = {"ret": C_RV, "moba": C_MV, "dil": 2048}[kind] + HD * n
                        return h[:, t, col:col + HD]
                    o = ps[6 + i % 2]
                    pe.matmul(o[:, 0:HD], pt[:, 0:P], v(0), start=True, stop=True)
                    pe.matmul(o[:, HD:2 * HD], pt[:, P:2 * P], v(0), start=True, stop=False)
                    pe.matmul(o[:, HD:2 * HD], pt[:, 2 * P:3 * P], v(1), start=False, stop=True).then_inc(
                        sem("od"), 1)

                for i in range(len(work) + 3):
                    if i >= 3:
                        outputs(i - 3)
                    if 2 <= i < len(work) + 2:
                        turn_p(i - 2)
                    if 1 <= i < len(work) + 1:
                        scores(i - 1)
                    if i < len(work):
                        turn_qk(i)

            pe.wait_ge(sem("const_in"), 16)
            transpose_x("emb", x)
            xt_stage = "emb"
            for l in range(DEPTH):
                st = f"in{l}"

                def free_in(g, t):
                    if g >= 2:
                        pe.wait_ge(*at(st, f"ev{t}", g - 1))

                groups = [(512, 2)] * 5 + [(96, 1)]
                project(st, st, xth, xtl, groups, KD, lambda g, t: 2 * (g % 2) + t, (xt_stage, 4), free_in)
                transpose_x(f"lat{l}", h, kn=3, banks=(4, 5))
                for g, stage, ks in ((0, f"uq{l}", (0, 2)), (1, f"ukv{l}", (2, 3))):
                    width = 288 if g == 0 else 384
                    c = Chunk(AT[stage])
                    chunk(c)
                    pe.wait_ge(*at(f"lat{l}", "xt", 2))
                    if g == 0:
                        pe.wait_ge(*at(st, "ev0", 6))
                        pe.wait_ge(*at(st, "ev1", 6))
                    kn = ks[1] - ks[0]
                    wh = whi[:, c.split, 0:c.width].rearrange("p (k n) -> p k n", k=kn)
                    wl = wlo[:, c.split, 0:c.width].rearrange("p (k n) -> p k n", k=kn)
                    for t in range(T):
                        for half in range(2):
                            for k in range(kn):
                                m = mm3(ps[4 * g + 2 * t + half][:, 0:width], hth[:, ks[0] + k, t * P:(t + 1) * P],
                                        htl[:, ks[0] + k, t * P:(t + 1) * P], wh[:, k, half * width:(half + 1) * width],
                                        wl[:, k, half * width:(half + 1) * width], start=(k == 0), stop=(k == kn - 1))
                    m.then_inc(used, 1)
                pe.wait_ge(sem(f"rope{l}"), 1)
                heads(f"at{l}", heads_of_layer(), True)
                transpose_x(f"mix{l}", r)
                project(f"o{l}", f"o{l}", xth, xtl, [(512, 2)] * 2, KD, lambda g, t: 4 + 2 * t + g,
                        (f"mix{l}", KD), lambda g, t: None)
                transpose_x(f"ln1_{l}", x)
                pe.wait_ge(*at(f"ln1_{l}", "xt", 4))
                if l == 1:
                    c = Chunk(AT["router"])
                    chunk(c)
                    for t in range(T):
                        for k in range(KD):
                            m = mm3(ps[3][:, t * NE:(t + 1) * NE], xth[:, k, t * P:(t + 1) * P],
                                    xtl[:, k, t * P:(t + 1) * P], whi[:, c.split, k * NE:(k + 1) * NE],
                                    wlo[:, c.split, k * NE:(k + 1) * NE], start=(k == 0), stop=(k == KD - 1))
                    m.then_inc(used, 1)
                if l == 0:
                    ffn("f0", U_FF)
                    transpose_x("ln2_0", x)
                    xt_stage = "ln2_0"
                    continue
                pe.wait_ge(sem("rt_sel"), 1)
                pe.wait_ge(sem("route_in"), 16)
                sel = lg[:, 3]
                pe.matmul(ps[3][:, 32:40], earlier, sel[:, 0], start=True, stop=True)
                pe.matmul(ps[3][:, 40:48], earlier, sel[:, 1], start=True, stop=False)
                pe.matmul(ps[3][:, 40:48], ones, sel[:, 0], start=False, stop=True)
                pe.matmul(ps[3][:, 48:56], ones, sel[:, 0], start=True, stop=False)
                pe.matmul(ps[3][:, 48:56], ones, sel[:, 1], start=False, stop=True).then_inc(sem("rt_rank"), 1)
                pe.wait_ge(sem("rt_gated"), 1)
                for e in range(NE):
                    for t in range(T):
                        m = pe.transpose(ps[4 + e // 2][:, (e % 2) * S + t * P:(e % 2) * S + (t + 1) * P], gated[:, e, t], ident)
                    if e % 2:
                        m.then_inc(sem("rt_turned"), 1)
                pe.wait_ge(sem("rt_flag"), 1)
                overfull = pe.value_load(flag[0:1, 0:1], min_val=0, max_val=1)
                with pe.If(overfull == 0):
                    experts()
                with pe.Else():
                    pe.wait_ge(sem("rt_spread"), 4)
                    ffn("f1", U_MOE)

            transpose_x("n1", r)
            pe.wait_ge(*at("n1", "xt", KD))
            ffn("f2", U_FF)
            transpose_x("nmix", r)

            def free_in2(g, t):
                if g in (2, 3):
                    pe.wait_ge(*at("in2", "ev0", 2 * g - 3 + t))
                if g == 4:
                    pe.wait_ge(*at("in2", f"ev{t}", (5, 1)[t]))
            project("in2", "in2", xth, xtl, [(512, 2)] * 5, KD, lambda g, t: 2 * (g % 2) + t, ("nmix", KD), free_in2)
            pe.wait_ge(sem("ws_masked"), 1)
            for g in range(8):
                m = pe.transpose(ps[4 + g // 4][:, (g % 4) * P:(g % 4 + 1) * P], ws[:, g, :], ident)
            m.then_inc(sem("ws_tr"), 1)
            pe.wait_ge(sem("ws_t"), 2)
            pe.wait_ge(sem("v_norm"), 1)
            for g in range(8):
                m = pe.matmul(ps[6 + g // 4][:, (g % 4) * P:(g % 4 + 1) * P], wst[:, g, :],
                              h[:, :, 512 + HD * g:512 + HD * (g + 1)], start=True, stop=True)
            m.then_inc(sem("mixed"), 1)
            pe.wait_ge(sem("rot_done"), 1)
            pe.wait_ge(sem("ya"), 1)
            heads("dil", [("dil", n) for n in range(DIL_H)], True)
            transpose_x("mix2", r)
            project("out2", "out2", xth, xtl, [(512, 2)] * 2, KD, lambda g, t: 4 + 2 * t + g, ("mix2", KD),
                    lambda g, t: None)
            transpose_x("nmem", r)

            def free_k(b):
                if b == 4:
                    pe.wait_ge(*at("out2", "resid", 4))
            project_t("wk", "wk", ("nmem", KD), free_k)
            pe.wait_ge(*at("wk", "ev", KD))
            project("wv", "wv", xth, xtl, [(512, 2)] * 2, KD, lambda g, t: 2 * g + t, ("nmem", KD), lambda g, t: None)
            pe.wait_ge(*at("wv", "ev0", 2))
            pe.wait_ge(*at("wv", "ev1", 2))
            transpose_x("ncross", r)
            project_t("wq", "wq", ("ncross", KD), lambda b: None)
            pe.wait_ge(*at("wq", "ev", KD))
            for i in range(X_H + 2):
                if i >= 2:
                    n = i - 2
                    pe.wait_ge(sem("x_pt"), n + 1)
                    if n >= 2:
                        pe.wait_ge(sem("x_o"), n - 1)
                    for t in range(T):
                        for mt in range(T):
                            m = pe.matmul(ps[6 + n % 2][:, t * X_D:(t + 1) * X_D],
                                          probt[:, n % 2, (2 * t + mt) * P:(2 * t + mt + 1) * P],
                                          xv[:, mt, n * X_D:(n + 1) * X_D], start=(mt == 0), stop=(mt == 1))
                    m.then_inc(sem("x_od"), 1)
                if i < X_H:
                    if i >= 2:
                        pe.wait_ge(sem("x_p"), i - 1)
                    for t in range(T):
                        for k in range(2):
                            m = pe.matmul(ps[2 + i % 2][:, t * S:(t + 1) * S], qt[:, 2 * i + k, t * P:(t + 1) * P],
                                          kt[:, 2 * i + k, :], start=(k == 0), stop=(k == 1))
                    m.then_inc(sem("x_s"), 1)
                if 1 <= i < X_H + 1:
                    n = i - 1
                    pe.wait_ge(sem("x_p"), n + 1)
                    for b in range(4):
                        m = pe.transpose(ps[4 + n % 2][:, b * P:(b + 1) * P], prob[:, n % 2, b * P:(b + 1) * P], ident)
                    m.then_inc(sem("x_tp"), 1)
            transpose_x("xo", bc)
            project("xo", "xo", xth, xtl, [(512, 2)] * 2, KD, lambda g, t: 4 + 2 * t + g, ("xo", 4),
                    lambda g, t: None)
            transpose_x("n2", r)
            pe.wait_ge(*at("n2", "xt", KD))
            ffn("f3", U_FF)

        @block.scalar
        def _(act):
            cursor = [0]
            chained = [0]

            def link(ins):
                chained[0] += 1
                ins.then_inc(sem("act_chain"), 1)
                act.wait_ge(sem("act_chain"), chained[0])

            def hi(c):
                act.wait_ge(landed[c.raw], c.landed)
                if not (isinstance(c.n, int) and c.n < SPLIT):
                    act.wait_ge(used, c.n - SPLIT + 1)
                act.activation(whi[:, c.split, 0:c.width], raw[:, c.raw, 0:c.width], ACT.Copy).then_inc(hi_done, 1)

            def advance(upto):
                while cursor[0] <= min(upto, NCHUNK - 1):
                    hi(Chunk(cursor[0]))
                    cursor[0] += 1

            def split_x(stage, gain=None, kn=KD, dst=xth, banks=(0, 1, 2, 3)):
                for b in range((kn + 1) // 2):
                    act.wait_ge(*at(stage, "tr", b + 1))
                    ks = range(2 * b, min(2 * b + 2, kn))
                    if gain is None:
                        act.activation(dst[:, 2 * b:2 * b + 2, :], ps[banks[b]][:, :].rearrange("p (k s) -> p k s", k=2),
                                       ACT.Copy).then_inc(sem("xh"), 1)
                        continue
                    for k in ks:
                        act.activation(dst[:, k, :], ps[banks[b]][:, (k % 2) * S:(k % 2 + 1) * S], ACT.Copy,
                                       scale=cols[:, gain + k:gain + k + 1]).then_inc(sem("xh"), 1)

            def root(stage, src, n, scale, e):
                act.activation(sd[:, 0:n], src, ACT.Sqrt, bias=eps[:, e:e + 1], scale=scale).then_inc(sem("sd"), 1)

            def rms_stats(stage, parts):
                for n, (junk, src) in enumerate(parts):
                    link(act.activation(junk, src, ACT.Square, accum_out=ss[:, n:n + 1]))
                root(stage, ss[:, 0:len(parts)], len(parts), 1.0 / parts[0][1].shape[-1], 1)

            def evac(stage, g, t, dst, width, bank, func=ACT.Copy):
                act.wait_ge(*group_done(stage, g, t))
                act.activation(dst, ps[bank][:, 0:width], func).then_inc(sem("ev0"), 1)

            def ffn(name, units):
                first_chunk = AT[name]

                def unit(u, base, it, chunks):
                    n = base + LEAD
                    for j in range(chunks - 1):
                        if n + j < NCHUNK:
                            hi(Chunk(n + j, it))
                    act.wait_ge(used, base + LB * it + 2)
                    for t in range(T):
                        act.activation(sg[:, t, :], ps[t][:, 0:FU], ACT.Silu).then_inc(unit_sem(name, "sg"), 1)
                    if n + chunks - 1 < NCHUNK:
                        hi(Chunk(n + chunks - 1, it))
                    act.wait_ge(*at(name, "ut", u + 1))
                    act.activation(hth[:, 0:2, :], ps[2][:, :].rearrange("p (k s) -> p k s", k=2), ACT.Copy).then_inc(
                        unit_sem(name, "hh"), 1)

                advance(first_chunk + LEAD - 1)
                unit(0, first_chunk, 0, 2)
                unit(1, first_chunk + 2, 0, 3)
                loops = (units - 3) // UNROLL
                with act.Fori(0, loops) as it:
                    for j in range(UNROLL):
                        unit(it * UNROLL + 2 + j, first_chunk + 5 + 3 * j, it, 3)
                for u in range(2 + loops * UNROLL, units):
                    unit(u, first_chunk + 3 * u - 1, 0, 3)
                cursor[0] = first_chunk + 3 * units - 1 + LEAD

            def experts():
                first_chunk = AT["f1"]

                def gathered(q, g, n, bank):
                    act.wait_ge(sem("e_ga"), n)
                    act.activation(xth[:, 4 * g:4 * g + 4, q * P:(q + 1) * P], ps[bank][:, :].rearrange("p (k s) -> p k s", k=4),
                                   ACT.Copy).then_inc(sem("e_gh"), 1)

                def outputs(q, done):
                    act.wait_ge(*done)
                    act.activation(r[:, q, 0:512], ps[2][:, :], ACT.Copy).then_inc(sem("e_oa"), 1)

                def unit(e, q, j, base, rounds, u, chunks=3):
                    n = base + LEAD
                    for i in range(chunks - 1):
                        hi(Chunk(n + i, rounds))
                    act.wait_ge(used, base + LB * rounds + 2)
                    act.activation(sg[:, 0, :], ps[0][:, 0:FU], ACT.Silu).then_inc(sem("e_sg"), 1)
                    if j in GATHER_AT and e is not None:
                        g = GATHER_AT.index(j)
                        gathered(1 - q, g, 2 * (e + 1) + g + 1, 1)
                    hi(Chunk(n + chunks - 1, rounds))
                    act.wait_ge(sem("e_ut"), u + 1)
                    act.activation(hth[:, 0:2, 0:P], ps[1][:, 0:2 * P].rearrange("p (k s) -> p k s", k=2), ACT.Copy).then_inc(
                        sem("e_hh"), 1)
                    if j == 0 and chunks == 3:
                        outputs(1 - q, (used, base + LB * rounds + 3))

                def expert(e, q, rounds, last=False):
                    base = first_chunk - 1
                    ahead = None if last else e
                    if isinstance(e, int) and e == 0:
                        unit(e, q, 0, first_chunk, 0, 0, chunks=2)
                    else:
                        unit(e, q, 0, base, rounds, U_E * e)
                    unit(e, q, 1, base + 3, rounds, U_E * e + 1)
                    for lo_u, hi_u in ((2, 6), (6, 10), (10, U_E)):
                        if lo_u == 6:
                            for j in range(lo_u, hi_u):
                                unit(ahead, q, j, base + 3 * j, rounds, U_E * e + j)
                            continue
                        with act.Fori(0, (hi_u - lo_u) // 2) as it:
                            for j in range(lo_u, lo_u + 2):
                                unit(None, q, -1, base + 3 * j, rounds + it, U_E * e + j + it * 2)

                for g in range(2):
                    gathered(0, g, g + 1, g)
                advance(first_chunk + LEAD - 1)
                expert(0, 0, 0)
                with act.Fori(0, (NE - 2) // 2) as pair:
                    for s in range(2):
                        expert(pair * 2 + 1 + s, 1 - s, (pair * 2 + 1 + s) * ROUNDS_E)
                expert(NE - 1, 1, (NE - 1) * ROUNDS_E, last=True)
                outputs(1, (used, first_chunk + 3 * U_MOE))
                cursor[0] = first_chunk + 3 * U_MOE - 1 + LEAD

            def heads(stage, work, last):
                soft = [kind != "ret" for kind, _ in work]
                for i in range(len(work) + 1):
                    if i < len(work):
                        d = QD if work[i][0] == "mla" else HD
                        act.wait_ge(*at(stage, "tq", i + 1))
                        act.activation(qkt[0:d, i % 2, :], ps[i % 2][0:d, :], ACT.Copy).then_inc(sem("qk"), 1)
                    if i >= 1 and soft[i - 1]:
                        n = i - 1
                        act.wait_ge(*at(stage, "mx", sum(soft[:i])))
                        act.activation(prob[:, n % 2, 0:P], prob[:, n % 2, 0:P], ACT.Exp, bias=nmax[:, n, 0:1],
                                       accum_out=rsum[:, n, 0:1])
                        act.activation(prob[:, n % 2, P:3 * P], prob[:, n % 2, P:3 * P], ACT.Exp, bias=nmax[:, n, 1:2],
                                       accum_out=rsum[:, n, 1:2]).then_inc(sem("p"), 1)
                    if i == 1:
                        advance(last + LEAD)

            act.wait_ge(sem("eps_set"), 2)
            act.wait_ge(sem("cols_in"), 16)
            advance(LEAD - 1)
            act.wait_ge(*at("emb", "mv", T))
            root("emb", mv[:, :, 1], T, 1.0, 0)
            split_x("emb")
            for l in range(DEPTH):
                st = f"in{l}"
                for g in range(6):
                    last = AT[st] + 2 * g + (1 if g < 5 else 0)
                    advance(last + LEAD)
                    width = 512 if g < 5 else 96
                    evac(st, g, 0, h[:, 0, 512 * g:512 * g + width], width, 2 * (g % 2))
                    if g == 0:
                        act.wait_ge(*at(st, "ev1", 1))
                        act.wait_ge(*at(st, "ev0", 1))
                        for t in range(T):
                            link(act.activation(prob[:, t, 0:256], h[:, t, 0:256], ACT.Square, accum_out=ss[:, t:t + 1]))
                            link(act.activation(prob[:, t, 256:384], h[:, t, 256:384], ACT.Square,
                                                accum_out=ss[:, 2 + t:3 + t]))
                        link(act.activation(sd[:, 0:2], ss[:, 0:2], ACT.Sqrt, bias=eps[:, 1:2], scale=1.0 / 256))
                        act.activation(sd[:, 2:4], ss[:, 2:4], ACT.Sqrt, bias=eps[:, 1:2], scale=1.0 / 128).then_inc(
                            sem("sd"), 1)
                last = AT[f"ukv{l}"]
                act.wait_ge(*at(st, "ev0", 6))
                act.wait_ge(*at(st, "ev1", 6))
                act.activation(h[:, :, C_RG:C_RG + 320], h[:, :, C_RG:C_RG + 320], ACT.Silu).then_inc(sem(f"gate{l}"), 1)
                split_x(f"lat{l}", COLS[f"q{l}"], 3, hth, (4, 5))
                advance(last + LEAD)
                act.wait_ge(used, AT[f"uq{l}"] + 1)
                for t in range(T):
                    for half in range(2):
                        act.activation(qc[:, t, 3 * half:3 * half + 3, :],
                                       ps[2 * t + half][:, 0:288].rearrange("p (h d) -> p h d", h=3),
                                       ACT.Copy).then_inc(sem("ev"), 1)
                heads(f"at{l}", heads_of_layer(), last)
                act.wait_ge(*at(f"at{l}", "o", 16))
                for t in range(T):
                    link(act.activation(prob[:, t, 0:384], r[:, t, 0:384], ACT.Square, accum_out=ss[:, t:t + 1]))
                    link(act.activation(prob[:, t, 0:320], r[:, t, O_MOBA:D], ACT.Square, accum_out=ss[:, 2 + t:3 + t]))
                link(act.activation(sd[:, 0:2], ss[:, 0:2], ACT.Sqrt, bias=eps[:, 1:2], scale=1.0 / 384))
                act.activation(sd[:, 2:4], ss[:, 2:4], ACT.Sqrt, bias=eps[:, 1:2], scale=1.0 / 320).then_inc(
                    sem("sd"), 1)
                act.wait_ge(sem(f"ret{l}_var"), 1)
                act.activation(gs[:, 2, 0:10], gs[:, 1, 0:10], ACT.Sqrt, bias=eps[:, 1:2], scale=1.0 / HD).then_inc(
                    sem("sd"), 1)
                split_x(f"mix{l}", COLS[f"mix{l}"])
                advance(AT[f"o{l}"] + 3 + LEAD)
                act.wait_ge(*at(f"ln1_{l}", "mv", T))
                root(f"ln1_{l}", mv[:, :, 1], T, 1.0, 0)
                split_x(f"ln1_{l}")
                if l == 1:
                    advance(AT["router"] + LEAD)
                    act.wait_ge(sem("rt_max"), 1)
                    for t in range(T):
                        act.activation(lg[:, 1, t, :], lg[:, 0, t, :], ACT.Exp, bias=small[:, 0, t:t + 1]).then_inc(
                            sem("rt_exp"), 1)
                if l == 0:
                    ffn("f0", U_FF)
                else:
                    for b in range(4):
                        act.wait_ge(sem("rt_turned"), b + 1)
                        act.activation(spread[:, 2 * b:2 * b + 2, :], ps[4 + b][:, :].rearrange("p (e s) -> p e s", e=2),
                                       ACT.Copy).then_inc(sem("rt_spread"), 1)
                    act.wait_ge(sem("rt_flag"), 1)
                    overfull = act.value_load(flag[0:1, 0:1], min_val=0, max_val=1)
                    n = cursor[0]
                    with act.If(overfull == 0):
                        experts()
                    with act.Else():
                        cursor[0] = n
                        ffn("f1", U_MOE)
                act.wait_ge(*at(f"ln2_{l}", "mv", T))
                root(f"ln2_{l}", mv[:, :, 1], T, 1.0, 0)
                if l == 0:
                    split_x(f"ln2_{l}")

            def rms_of_x(stage):
                rms_stats(stage, [(r[:, t, :], x[:, t, :]) for t in range(T)])

            act.wait_ge(*at("ln2_1", "x", T))
            rms_of_x("n1")
            split_x("n1", COLS["ffn1"])
            ffn("f2", U_FF)
            act.wait_ge(sem("angle"), 1)
            act.activation(rot[:, 4], rot[:, 2], ACT.Sin).then_inc(sem("sines"), 1)
            act.activation(rot[:, 5], rot[:, 2], ACT.Sin, scale=0.5).then_inc(sem("sines"), 1)
            act.wait_ge(*at("f2", "resid", 4))
            rms_of_x("nmix")
            split_x("nmix", COLS["in2"])
            for g in range(5):
                advance(AT["in2"] + 2 * g + 1 + LEAD)
                evac("in2", g, 0, h[:, 0, 512 * g:512 * g + 512], 512, 2 * (g % 2), ACT.Gelu if g < 2 else ACT.Copy)
                if g < 2:
                    evac("in2", g, 1, h[:, 1, 512 * g:512 * g + 512], 512, 2 * (g % 2) + 1, ACT.Gelu)
            last = AT["in2"] + 9
            act.wait_ge(sem("sgu_var"), 1)
            act.activation(gs[:, 2, :], gs[:, 1, :], ACT.Sqrt, bias=eps[:, 0:1], scale=1.0 / HD).then_inc(sem("sd"), 1)
            act.wait_ge(sem("ws_tr"), 1)
            for b in range(2):
                act.activation(wst[:, 4 * b:4 * b + 4, :], ps[4 + b][:, :].rearrange("p (g j) -> p g j", g=4),
                               ACT.Copy).then_inc(sem("ws_t"), 1)
            heads("dil", [("dil", n) for n in range(DIL_H)], last)
            act.wait_ge(*at("dil", "o", DIL_H))
            rms_stats("mix2", [(prob[:, t, :], r[:, t, 512 * a:512 * a + 512]) for a in range(2) for t in range(T)])
            split_x("mix2", COLS["out2"])
            advance(AT["out2"] + 3 + LEAD)
            act.wait_ge(sem("mem_in"), 16)
            for t in range(T):
                link(act.activation(bc[:, 1, :], r[:, t, :], ACT.Square, accum_out=ss[:, t:t + 1]))
            root("nmem", ss[:, 0:T], T, 1.0 / D, 1)
            split_x("nmem", COLS["mem"])
            for j in range(KD):
                advance(AT["wk"] + 2 * (j // 4) + 1 + LEAD)
                act.wait_ge(*tile_done("wk", j))
                act.activation(kt[:, j, :], ps[j][:, 0:S], ACT.Copy).then_inc(sem("ev"), 1)
            for g in range(2):
                advance(AT["wv"] + 2 * g + 1 + LEAD)
                evac("wv", g, 0, xv[:, 0, 512 * g:512 * g + 512], 512, 2 * g)
            act.wait_ge(*at("nmem", "tr", 4))
            rms_of_x("ncross")
            split_x("ncross", COLS["cross"])
            for j in range(KD):
                advance(AT["wq"] + 2 * (j // 4) + 1 + LEAD)
                act.wait_ge(*tile_done("wq", j))
                act.activation(qt[:, j, :], ps[j][:, 0:S], ACT.Copy).then_inc(sem("ev"), 1)
            last = AT["wq"] + 3
            for i in range(X_H):
                act.wait_ge(sem("x_mx"), i + 1)
                if i >= 2:
                    act.wait_ge(sem("x_tp"), i - 1)
                for t in range(T):
                    m = act.activation(prob[:, i % 2, t * S:(t + 1) * S], ps[2 + i % 2][:, t * S:(t + 1) * S], ACT.Exp,
                                       bias=nmax[:, i, t:t + 1], scale=X_D ** -0.5, accum_out=rsum[:, i, t:t + 1])
                m.then_inc(sem("x_p"), 1)
                advance(last + 1 + i if i < SPLIT else 0)
            split_x("xo")
            advance(AT["xo"] + 3 + LEAD)
            act.wait_ge(*at("xo", "resid", 4))
            rms_of_x("n2")
            split_x("n2", COLS["ffn2"])
            ffn("f3", U_FF)
            act.wait_ge(*at("f3", "resid", 4))
            rms_of_x("fin")

        @block.vector
        def _(dve):
            cursor = [0]
            chained = [0]

            def link(ins):
                chained[0] += 1
                ins.then_inc(sem("dve_chain"), 1)
                dve.wait_ge(sem("dve_chain"), chained[0])

            def lo(c):
                dve.wait_ge(hi_done, c.n + 1)
                dve.tensor_tensor(wlo[:, c.split, 0:c.width], raw[:, c.raw, 0:c.width], f32(whi[:, c.split, 0:c.width]),
                                  ALU.subtract).then_inc(lo_done, 1)

            def advance(upto):
                while cursor[0] <= min(upto, NCHUNK - 1):
                    lo(Chunk(cursor[0]))
                    cursor[0] += 1

            def split_x(stage, gain=None, kn=KD, dsth=xth, dstl=xtl, banks=(0, 1, 2, 3)):
                for b in range((kn + 1) // 2):
                    if gain is None:
                        dve.wait_ge(*at(stage, "xh", b + 1))
                        dve.tensor_tensor(dstl[:, 2 * b:2 * b + 2, :], ps[banks[b]][:, :].rearrange("p (k s) -> p k s", k=2),
                                          f32(dsth[:, 2 * b:2 * b + 2, :]), ALU.subtract).then_inc(sem("xt"), 1)
                        continue
                    n = min(2 * b + 2, kn)
                    dve.wait_ge(*at(stage, "xh", n))
                    for k in range(2 * b, n):
                        m = dve.scalar_tensor_tensor(out=dstl[:, k, :], in0=ps[banks[b]][:, (k % 2) * S:(k % 2 + 1) * S],
                                                     scalar=cols[:, gain + k:gain + k + 1], in1=f32(dsth[:, k, :]),
                                                     op0=ALU.mult, op1=ALU.subtract)
                        if kn == KD or k % 2 == 1 or k == kn - 1:
                            m.then_inc(sem("xt"), 1)

            def layer_norm(stage, row):
                for t in range(T):
                    for a in range(2):
                        m = dve.bn_stats(bn[:, t, a, :], r[:, t, 512 * a:512 * a + 512])
                    link(m)
                    dve.bn_aggr(mv[:, t, :], bn[:, t, :, :].rearrange("p a s -> p (a s)")).then_inc(sem("mv"), 1)
                dve.wait_ge(*at(stage, "mv", T))
                dve.wait_ge(sem(f"rows{row}"), 16)
                for t in range(T):
                    link(dve.scalar_tensor_tensor(out=r[:, t, :], in0=r[:, t, :], scalar=mv[:, t, 0:1], in1=bc[:, 0, :],
                                                  op0=ALU.subtract, op1=ALU.mult))
                dve.wait_ge(*at(stage, "sd", 1))
                link(dve.reciprocal(rstd[:, 0:T], sd[:, 0:T]))
                for t in range(T):
                    dve.scalar_tensor_tensor(out=x[:, t, :], in0=r[:, t, :], scalar=rstd[:, t:t + 1], in1=bc[:, 1, :],
                                             op0=ALU.mult, op1=ALU.add).then_inc(sem("x"), 1)

            def residual(stage, done, dst, a, b):
                dve.wait_ge(*done)
                for t in range(T):
                    for n in range(2):
                        cut = slice(512 * n, 512 * n + 512)
                        p = ps[4 + 2 * t + n][:, :]
                        if b == 1.0:
                            m = dve.scalar_tensor_tensor(out=dst[:, t, cut], in0=x[:, t, cut], scalar=float(a), in1=p,
                                                         op0=ALU.mult, op1=ALU.add)
                        else:
                            m = dve.scalar_tensor_tensor(out=dst[:, t, cut], in0=p, scalar=float(b), in1=x[:, t, cut],
                                                         op0=ALU.mult, op1=ALU.add)
                        m.then_inc(sem("resid"), 1)
                dve.wait_ge(*at(stage, "resid", 4))

            def rms_scale(stage, src, dst=None):
                dst = r if dst is None else dst
                dve.wait_ge(*at(stage, "sd", 1))
                link(dve.reciprocal(rstd[:, 0:T], sd[:, 0:T]))
                for t in range(T):
                    dve.tensor_scalar(dst[:, t, :], src[:, t, :], rstd[:, t:t + 1], None, ALU.mult).then_inc(
                        sem("x"), 1)

            def evac(stage, g, t, dst, width, bank):
                dve.wait_ge(*group_done(stage, g, t))
                dve.tensor_copy(dst, ps[bank][:, 0:width]).then_inc(sem("ev1"), 1)

            def ffn(name, units, gated=False):
                first_chunk = AT[name]

                def unit(u, base, it, chunks, pair):
                    n = base + LEAD
                    for j in range(chunks - 1):
                        if n + j < NCHUNK:
                            lo(Chunk(n + j, it))
                    for t in range(T):
                        dve.wait_ge(*at(name, "sg", 2 * u + t + 1))
                        if gated:
                            m = dve.scalar_tensor_tensor(out=hs[:, t, :], in0=sg[:, t, :], scalar=gexp[:, pair, t:t + 1],
                                                         in1=ps[t][:, FU:2 * FU], op0=ALU.mult, op1=ALU.mult)
                        else:
                            m = dve.tensor_tensor(hs[:, t, :], sg[:, t, :], ps[t][:, FU:2 * FU], ALU.mult)
                        m.then_inc(unit_sem(name, "hu"), 1)
                    if n + chunks - 1 < NCHUNK:
                        lo(Chunk(n + chunks - 1, it))
                    dve.wait_ge(*at(name, "hh", u + 1))
                    dve.tensor_tensor(htl[:, 0:2, :], ps[2][:, :].rearrange("p (k s) -> p k s", k=2),
                                      f32(hth[:, 0:2, :]), ALU.subtract).then_inc(unit_sem(name, "ht"), 1)

                advance(first_chunk + LEAD - 1)
                unit(0, first_chunk, 0, 2, 0)
                unit(1, first_chunk + 2, 0, 3, 0)
                loops = (units - 3) // UNROLL
                with dve.Fori(0, loops) as it:
                    for j in range(UNROLL):
                        unit(it * UNROLL + 2 + j, first_chunk + 5 + 3 * j, it, 3, it * (UNROLL // 2) + 1 + j // 2)
                for u in range(2 + loops * UNROLL, units):
                    unit(u, first_chunk + 3 * u - 1, 0, 3, u // 2)
                cursor[0] = first_chunk + 3 * units - 1 + LEAD

            def experts():
                first_chunk = AT["f1"]

                def gathered(q, g, n, bank):
                    dve.wait_ge(sem("e_gh"), n)
                    cut = slice(q * P, (q + 1) * P)
                    dve.tensor_tensor(xtl[:, 4 * g:4 * g + 4, cut], ps[bank][:, :].rearrange("p (k s) -> p k s", k=4),
                                      f32(xth[:, 4 * g:4 * g + 4, cut]), ALU.subtract).then_inc(sem("e_gx"), 1)

                def outputs(e, q, done):
                    if not (isinstance(e, int) and e == 0):
                        dve.wait_ge(sem("e_sc"), e)
                    dve.tensor_copy(spread_now, spread[:, e, :])
                    dve.wait_ge(*done)
                    dve.tensor_copy(r[:, q, 512:D], ps[3][:, :]).then_inc(sem("e_od"), 1)

                def unit(e, q, j, base, rounds, u, chunks=3):
                    n = base + LEAD
                    for i in range(chunks - 1):
                        lo(Chunk(n + i, rounds))
                    dve.wait_ge(sem("e_sg"), u + 1)
                    dve.tensor_tensor(hs[:, 0, :], sg[:, 0, :], ps[0][:, FU:2 * FU], ALU.mult).then_inc(sem("e_h"), 1)
                    if j in GATHER_AT and e is not None:
                        g = GATHER_AT.index(j)
                        gathered(1 - q, g, 2 * (e + 1) + g + 1, 1)
                    lo(Chunk(n + chunks - 1, rounds))
                    dve.wait_ge(sem("e_hh"), u + 1)
                    dve.tensor_tensor(htl[:, 0:2, 0:P], ps[1][:, 0:2 * P].rearrange("p (k s) -> p k s", k=2),
                                      f32(hth[:, 0:2, 0:P]), ALU.subtract).then_inc(sem("e_ht"), 1)
                    if j == 0 and chunks == 3:
                        outputs(e - 1, 1 - q, (used, base + LB * rounds + 3))

                def expert(e, q, rounds, last=False):
                    base = first_chunk - 1
                    ahead = None if last else e
                    if isinstance(e, int) and e == 0:
                        unit(e, q, 0, first_chunk, 0, 0, chunks=2)
                    else:
                        unit(e, q, 0, base, rounds, U_E * e)
                    unit(e, q, 1, base + 3, rounds, U_E * e + 1)
                    for lo_u, hi_u in ((2, 6), (6, 10), (10, U_E)):
                        if lo_u == 6:
                            for j in range(lo_u, hi_u):
                                unit(ahead, q, j, base + 3 * j, rounds, U_E * e + j)
                            continue
                        with dve.Fori(0, (hi_u - lo_u) // 2) as it:
                            for j in range(lo_u, lo_u + 2):
                                unit(None, q, -1, base + 3 * j, rounds + it, U_E * e + j + it * 2)

                for g in range(2):
                    gathered(0, g, g + 1, g)
                advance(first_chunk + LEAD - 1)
                expert(0, 0, 0)
                with dve.Fori(0, (NE - 2) // 2) as pair:
                    for s in range(2):
                        expert(pair * 2 + 1 + s, 1 - s, (pair * 2 + 1 + s) * ROUNDS_E)
                expert(NE - 1, 1, (NE - 1) * ROUNDS_E, last=True)
                outputs(NE - 1, 1, (used, first_chunk + 3 * U_MOE))
                cursor[0] = first_chunk + 3 * U_MOE - 1 + LEAD

            def rotate(x1, x2, cos, sin, tmp):
                dve.tensor_tensor(tmp[0], x1, cos, ALU.mult)
                dve.tensor_tensor(tmp[1], x2, sin, ALU.mult)
                dve.tensor_tensor(tmp[2], x1, sin, ALU.mult)
                link(dve.tensor_tensor(tmp[3], x2, cos, ALU.mult))
                dve.tensor_tensor(x1, tmp[0], tmp[1], ALU.subtract)
                m = dve.tensor_tensor(x2, tmp[2], tmp[3], ALU.add)
                link(m)

            def heads(stage, work, last):
                soft = [kind != "ret" for kind, _ in work]
                for i in range(1, len(work) + 3 + 1):
                    if i - 1 < len(work):
                        n = i - 1
                        kind, hn = work[n]
                        dve.wait_ge(*at(stage, "s", n + 1))
                        if kind == "ret":
                            dve.tensor_tensor(probt[:, n % 2, 0:S], ps[2 + n % 2][:, 0:S], c_ret[:, hn, :], ALU.mult)
                            dve.tensor_tensor(probt[:, n % 2, S:S + P], ps[2 + n % 2][:, S:S + P], c_ret[:, hn, 0:P],
                                              ALU.mult).then_inc(sem("pt"), 1)
                        else:
                            mask = c_moba[:, hn, :] if kind == "moba" else const(kind)
                            scale = QD ** -0.5 if kind == "mla" else HD ** -0.5
                            dve.scalar_tensor_tensor(out=prob[:, n % 2, 0:3 * P], in0=ps[2 + n % 2][:, 0:3 * P], scalar=scale,
                                                     in1=mask, op0=ALU.mult, op1=ALU.add).then_inc(sem("sf"), 1)
                            dve.wait_ge(*at(stage, "sf", sum(soft[:n + 1])))
                            dve.tensor_reduce(nmax[:, n, 0:1], prob[:, n % 2, 0:P], AX, ALU.max, negate=True)
                            dve.tensor_reduce(nmax[:, n, 1:2], prob[:, n % 2, P:3 * P], AX, ALU.max, negate=True).then_inc(
                                sem("mx"), 1)
                    if 0 <= i - 2 < len(work) and soft[i - 2]:
                        n = i - 2
                        dve.wait_ge(*at(stage, "tp", sum(soft[:n + 1])))
                        dve.tensor_copy(probt[:, n % 2, 0:3 * P], ps[4 + n % 2][:, 0:3 * P]).then_inc(sem("pt"), 1)
                    if 0 <= i - 3 < len(work):
                        n = i - 3
                        kind, hn = work[n]
                        col = {"ret": O_RET, "moba": O_MOBA, "mla": 0, "dil": 512}[kind] + HD * hn
                        dve.wait_ge(*at(stage, "od", n + 1))
                        if kind == "ret":
                            dve.tensor_copy(r[:, :, col:col + HD], ps[6 + n % 2][:, 0:2 * HD].rearrange(
                                "p (t d) -> p t d", t=T)).then_inc(sem("o"), 1)
                        else:
                            link(dve.reciprocal(rinv[:, n, :], rsum[:, n, :]))
                            for t in range(T):
                                m = dve.tensor_scalar(r[:, t, col:col + HD], ps[6 + n % 2][:, t * HD:(t + 1) * HD],
                                                      rinv[:, n, t:t + 1], None, ALU.mult)
                            m.then_inc(sem("o"), 1)
                    if i == 2:
                        advance(last + LEAD)

            def group_var(stage, v, groups, scratch):
                link(dve.tensor_reduce(gs[:, 0, 0:groups], v, AX, ALU.add))
                link(dve.tensor_scalar(gs[:, 0, 0:groups], gs[:, 0, 0:groups], 1.0 / HD, None, ALU.mult))
                return None

            dve.wait_ge(sem("x_in"), 16)
            dve.wait_ge(sem("const_in"), 16)
            dve.wait_ge(sem("cols_in"), 16)
            advance(LEAD - 1)
            layer_norm("emb", 0)
            split_x("emb")
            for l in range(DEPTH):
                st = f"in{l}"
                for g in range(6):
                    last = AT[st] + 2 * g + (1 if g < 5 else 0)
                    advance(last + LEAD)
                    width = 512 if g < 5 else 96
                    evac(st, g, 1, h[:, 1, 512 * g:512 * g + width], width, 2 * (g % 2) + 1)
                    if g == 1:
                        dve.wait_ge(*at(f"lat{l}", "sd", 1))
                        link(dve.reciprocal(rstd[:, :], sd[:, :]))
                        for t in range(T):
                            dve.tensor_scalar(h[:, t, 0:256], h[:, t, 0:256], rstd[:, t:t + 1], None, ALU.mult)
                            dve.tensor_scalar(h[:, t, 256:384], h[:, t, 256:384], rstd[:, 2 + t:3 + t], None,
                                              ALU.mult).then_inc(sem("x"), 1)
                    if g == 3:
                        dve.wait_ge(*at(st, "ev0", 3))
                        dve.wait_ge(*at(st, "ev1", 3))
                        for t in range(T):
                            v = h[:, t, C_RQ:C_RV].rearrange("p (h d) -> p h d", d=HD)
                            tmp = [r[:, a // 2, 320 * (a % 2):320 * (a % 2) + 320].rearrange("p (h d) -> p h d", d=32)
                                   for a in range(4)]
                            cos, sin = (const(c)[:, 32 * t:32 * t + 32].unsqueeze(1).to_broadcast([P, 10, 32])
                                        for c in ("cos_b", "sin_b"))
                            rotate(v[:, :, 0:32], v[:, :, 32:64], cos, sin, tmp)
                        v = h[:, :, C_ROPE:C_RQ]
                        tmp = [small[:, 2 * a:2 * a + 2, :] for a in range(4)]
                        cos, sin = (const(c).rearrange("p (t d) -> p t d", t=T) for c in ("cos_a", "sin_a"))
                        rotate(v[:, :, 0:16], v[:, :, 16:32], cos, sin, tmp)
                last = AT[f"ukv{l}"]
                split_x(f"lat{l}", COLS[f"q{l}"], 3, hth, htl, (4, 5))
                advance(last + LEAD)
                dve.wait_ge(used, AT[f"ukv{l}"] + 1)
                for t in range(T):
                    for half in range(2):
                        kv = ps[4 + 2 * t + half][:, 0:384].rearrange("p (h d) -> p h d", h=3)
                        dve.tensor_copy(kc[:, t, 3 * half:3 * half + 3, 0:NOPE], kv[:, :, 0:NOPE])
                        dve.tensor_copy(vc[:, t, 3 * half:3 * half + 3, :], kv[:, :, NOPE:])
                    link(dve.tensor_copy(kc[:, t, :, NOPE:QD],
                                         h[:, t, C_ROPE:C_RQ].unsqueeze(1).to_broadcast([P, MLA_H, ROPE])))
                dve.wait_ge(*at(f"uq{l}", "ev", 4))
                for t in range(T):
                    tmp = [r[:, a // 2, 320 * (a % 2):320 * (a % 2) + 96].rearrange("p (h d) -> p h d", d=16)
                           for a in range(4)]
                    cos, sin = (const(c)[:, 16 * t:16 * t + 16].unsqueeze(1).to_broadcast([P, MLA_H, 16])
                                for c in ("cos_a", "sin_a"))
                    rotate(qc[:, t, :, NOPE:NOPE + 16], qc[:, t, :, NOPE + 16:QD], cos, sin, tmp)
                dve.wait_ge(*at(st, "ev0", 6))
                dve.wait_ge(sem(f"gate{l}"), 1)
                dve.sem_inc(sem(f"rope{l}"), 1)
                heads(f"at{l}", heads_of_layer(), last)
                ov = r[:, :, O_RET:O_MOBA].rearrange("p t (h d) -> p t h d", d=HD)
                gv = gs[:, :, 0:10].rearrange("p s (t h) -> p s t h", t=T)
                gg = h[:, :, C_RG:C_RG + 320].rearrange("p t (h d) -> p t h d", d=HD)
                dve.wait_ge(*at(f"at{l}", "o", 16))
                link(dve.tensor_reduce(gv[:, 0], ov, AX, ALU.add))
                link(dve.tensor_scalar(gs[:, 0, 0:10], gs[:, 0, 0:10], 1.0 / HD, None, ALU.mult))
                sq = h[:, :, C_RQ:C_RK].rearrange("p t (h d) -> p t h d", d=HD)
                for t in range(T):
                    link(dve.tensor_tensor(ov[:, t], ov[:, t], gv[:, 0, t].unsqueeze(2).to_broadcast([P, RET_H, HD]),
                                           ALU.subtract))
                link(dve.tensor_tensor(sq, ov, ov, ALU.mult))
                dve.tensor_reduce(gv[:, 1], sq, AX, ALU.add).then_inc(sem(f"ret{l}_var"), 1)
                dve.wait_ge(*at(f"ret{l}", "sd", 1))
                link(dve.reciprocal(gs[:, 3, 0:10], gs[:, 2, 0:10]))
                for t in range(T):
                    link(dve.tensor_tensor(ov[:, t], ov[:, t], gv[:, 3, t].unsqueeze(2).to_broadcast([P, RET_H, HD]), ALU.mult))
                link(dve.tensor_tensor(ov, ov, gg, ALU.mult))
                dve.wait_ge(*at(f"mix{l}", "sd", 1))
                link(dve.reciprocal(rstd[:, :], sd[:, :]))
                for t in range(T):
                    dve.tensor_scalar(r[:, t, 0:384], r[:, t, 0:384], rstd[:, t:t + 1], None, ALU.mult)
                    dve.tensor_scalar(r[:, t, O_MOBA:D], r[:, t, O_MOBA:D], rstd[:, 2 + t:3 + t], None, ALU.mult).then_inc(
                        sem("x"), 1)
                split_x(f"mix{l}", COLS[f"mix{l}"])
                advance(AT[f"o{l}"] + 3 + LEAD)
                residual(f"o{l}", (used, AT[f"o{l}"] + 4), r, ALPHA, 1.0)
                layer_norm(f"ln1_{l}", 2 + 4 * l)
                split_x(f"ln1_{l}")
                if l == 1:
                    advance(AT["router"] + LEAD)
                    dve.wait_ge(used, AT["router"] + 1)
                    link(dve.tensor_copy(lg[:, 0], ps[3][:, 0:T * NE].rearrange("p (t e) -> p t e", t=T)))
                    dve.tensor_reduce(small[:, 0, 0:T], lg[:, 0], AX, ALU.max, negate=True).then_inc(sem("rt_max"), 1)
                    tri8 = const("tri8").rearrange("p (e f) -> p e f", e=NE)
                    for t in range(T):
                        mine = lg[:, 0, t].unsqueeze(2).to_broadcast([P, NE, NE])
                        other = lg[:, 0, t].unsqueeze(1).to_broadcast([P, NE, NE])
                        dve.tensor_tensor(lg3[:, 0, t], other, mine, ALU.is_gt)
                        link(dve.tensor_tensor(lg3[:, 1, t], other, mine, ALU.is_equal))
                        link(dve.tensor_tensor(lg3[:, 1, t], lg3[:, 1, t], tri8, ALU.mult))
                        link(dve.tensor_tensor(lg3[:, 0, t], lg3[:, 0, t], lg3[:, 1, t], ALU.add))
                        link(dve.tensor_reduce(lg[:, 2, t], lg3[:, 0, t], AX, ALU.add))
                    dve.tensor_scalar(lg[:, 3], lg[:, 2], 2.0, None, ALU.is_lt).then_inc(sem("rt_sel"), 1)
                    dve.wait_ge(sem("rt_sel"), 1)
                    dve.wait_ge(sem("rt_exp"), T)
                    link(dve.tensor_tensor(lg[:, 4], lg[:, 1], lg[:, 3], ALU.mult))
                    link(dve.tensor_reduce(small[:, 1, 0:T], lg[:, 4], AX, ALU.add))
                    link(dve.reciprocal(small[:, 2, 0:T], small[:, 1, 0:T]))
                    for t in range(T):
                        link(dve.tensor_scalar(lg[:, 5, t], lg[:, 4, t], small[:, 2, t:t + 1], None, ALU.mult))
                        link(dve.tensor_copy(gexp[:, :, t].rearrange("p (e n) -> p e n", e=NE),
                                             lg[:, 5, t].unsqueeze(2).to_broadcast([P, NE, U_MOE // 2 // NE])))
                    dve.wait_ge(sem("rt_rank"), 1)
                    link(dve.scalar_tensor_tensor(out=lg[:, 6], in0=ps[3][:, 32:48].rearrange("p (t e) -> p t e", t=T), scalar=1.0,
                                                  in1=lg[:, 3], op0=ALU.add, op1=ALU.mult))
                    link(dve.tensor_scalar(lg[:, 6], lg[:, 6], -1.0, None, ALU.add))
                    link(dve.tensor_reduce(small[:, 4, 0:1], ps[3][:, 48:56], AX, ALU.max))
                    link(dve.tensor_scalar(flag[:, :], small[:, 4, 0:1], float(P), None, ALU.is_gt))
                    for e in range(NE):
                        for t in range(T):
                            dve.tensor_scalar(onehot[:, e, t], slots, lg[:, 6, t, e:e + 1], None, ALU.is_equal)
                    for e in range(NE):
                        for t in range(T):
                            m = dve.tensor_scalar(gated[:, e, t], slots, lg[:, 6, t, e:e + 1], lg[:, 5, t, e:e + 1],
                                                  ALU.is_equal, ALU.mult)
                    m.then_inc(sem("rt_gated"), 1)
                    dve.wait_ge(sem("rt_gated"), 1)
                    dve.sem_inc(sem("rt_flag"), 1)
                    overfull = dve.value_load(flag[0:1, 0:1], min_val=0, max_val=1)
                    n = cursor[0]
                    with dve.If(overfull == 0):
                        experts()
                        residual("f1", (sem("e_sc"), NE), r, ALPHA, 1.0)
                    with dve.Else():
                        cursor[0] = n
                        ffn("f1", U_MOE, gated=True)
                        residual("f1", (used, AT["f1"] + 3 * U_MOE), r, ALPHA, 1.0)
                else:
                    ffn("f0", U_FF)
                    residual("f0", (used, AT["f0"] + 3 * U_FF), r, ALPHA, 1.0)
                layer_norm(f"ln2_{l}", 4 + 4 * l)
                if l == 0:
                    split_x(f"ln2_{l}")

            rms_scale("n1", x)
            split_x("n1", COLS["ffn1"])
            ffn("f2", U_FF)
            ang, turns, red = rot[:, 0], rot[:, 1], rot[:, 2]
            dve.wait_ge(sem("pos_in"), 16)
            link(dve.tensor_copy(small[:, 3, 0:T], posi[:, :]))
            for t in range(T):
                link(dve.tensor_scalar(ang[:, t], const("inv_freq"), small[:, 3, t:t + 1], None, ALU.mult))
            magic = 1.5 * 2.0 ** 23
            link(dve.tensor_scalar(turns, ang, float(1 / (2 * np.pi)), magic, ALU.mult, ALU.add))
            link(dve.tensor_scalar(turns, turns, magic, None, ALU.subtract))
            two_pi = 2 * np.pi
            p1 = 6.28125
            p2 = float(np.floor((two_pi - p1) * 2 ** 21) / 2 ** 21)
            p3 = float(np.float32(two_pi - p1 - p2))
            link(dve.scalar_tensor_tensor(out=red, in0=turns, scalar=-p1, in1=ang, op0=ALU.mult, op1=ALU.add))
            link(dve.scalar_tensor_tensor(out=red, in0=turns, scalar=-p2, in1=red, op0=ALU.mult, op1=ALU.add))
            link(dve.scalar_tensor_tensor(out=red, in0=turns, scalar=-p3, in1=red, op0=ALU.mult, op1=ALU.add))
            lim = 3.1415925
            dve.tensor_scalar(red, red, lim, -lim, ALU.min, ALU.max).then_inc(sem("angle"), 1)
            residual("f2", (used, AT["f2"] + 3 * U_FF), x, 1.0, 0.5)
            dve.wait_ge(sem("sines"), 2)
            cosr, sinr = rot[:, 3], rot[:, 4]
            link(dve.tensor_tensor(rot[:, 5], rot[:, 5], rot[:, 5], ALU.mult))
            link(dve.tensor_scalar(cosr, rot[:, 5], -2.0, 1.0, ALU.mult, ALU.add))
            rms_scale("nmix", x)
            split_x("nmix", COLS["in2"])
            for g in range(5):
                advance(AT["in2"] + 2 * g + 1 + LEAD)
                if g >= 2:
                    evac("in2", g, 1, h[:, 1, 512 * g:512 * g + 512], 512, 2 * (g % 2) + 1)
                if g == 0:
                    dve.wait_ge(sem("ws_in"), 16)
                    dve.tensor_tensor(ws, ws, const("tril").unsqueeze(1).to_broadcast([P, 8, P]), ALU.mult).then_inc(
                        sem("ws_masked"), 1)
                if g == 2:
                    dve.wait_ge(*at("in2", "ev0", 4))
                    dve.wait_ge(sem("rows10"), 16)
                    gv = gs[:, :, :].rearrange("p s (t h) -> p s t h", t=T)
                    for t in range(T):
                        v = h[:, t, 512:1024].rearrange("p (h d) -> p h d", d=HD)
                        sq = r[:, t, 0:512].rearrange("p (h d) -> p h d", d=HD)
                        link(dve.tensor_reduce(gv[:, 0, t], v, AX, ALU.add))
                        link(dve.tensor_scalar(gv[:, 0, t], gv[:, 0, t], 1.0 / HD, None, ALU.mult))
                        link(dve.tensor_tensor(v, v, gv[:, 0, t].unsqueeze(2).to_broadcast([P, 8, HD]), ALU.subtract))
                        link(dve.tensor_tensor(sq, v, v, ALU.mult))
                        m = dve.tensor_reduce(gv[:, 1, t], sq, AX, ALU.add)
                        if t == 0:
                            link(m)
                    m.then_inc(sem("sgu_var"), 1)
            last = AT["in2"] + 9
            dve.wait_ge(*at("sgu", "sd", 1))
            link(dve.reciprocal(gs[:, 3, :], gs[:, 2, :]))
            for t in range(T):
                v = h[:, t, 512:1024].rearrange("p (h d) -> p h d", d=HD)
                link(dve.tensor_tensor(v, v, gv[:, 3, t].unsqueeze(2).to_broadcast([P, 8, HD]), ALU.mult))
                link(dve.tensor_tensor(h[:, t, 512:1024], h[:, t, 512:1024], bc[:, 0, 0:512], ALU.mult))
                m = dve.tensor_tensor(h[:, t, 512:1024], h[:, t, 512:1024], bc[:, 0, 512:1024], ALU.add)
                if t == 0:
                    link(m)
            m.then_inc(sem("v_norm"), 1)
            dve.wait_ge(*at("in2", "ev0", 7))
            dve.wait_ge(*at("in2", "ev1", 3))
            for t in range(T):
                v = h[:, t, 1024:2048].rearrange("p (h d) -> p h d", d=HD)
                tmp = [r[:, 0, 512 + P * a:512 + P * (a + 1)].rearrange("p (h d) -> p h d", d=8) for a in range(4)]
                cos, sin = (c[:, t].unsqueeze(1).to_broadcast([P, 16, 8]) for c in (cosr, sinr))
                rotate(v[:, :, 0:8], v[:, :, 8:16], cos, sin, tmp)
            dve.sem_inc(sem("rot_done"), 1)
            dve.wait_ge(sem("mixed"), 1)
            for g in range(8):
                m = dve.scalar_tensor_tensor(
                    out=r[:, :, HD * g:HD * (g + 1)],
                    in0=ps[6 + g // 4][:, (g % 4) * P:(g % 4 + 1) * P].rearrange("p (t d) -> p t d", t=T),
                    scalar=cols[:, COLS["b_s"] + g:COLS["b_s"] + g + 1], in1=h[:, :, HD * g:HD * (g + 1)],
                    op0=ALU.add, op1=ALU.mult)
            m.then_inc(sem("ya"), 1)
            heads("dil", [("dil", n) for n in range(DIL_H)], last)
            dve.wait_ge(*at("mix2", "sd", 1))
            link(dve.reciprocal(rstd[:, :], sd[:, :]))
            for t in range(T):
                dve.tensor_scalar(r[:, t, 0:512], r[:, t, 0:512], rstd[:, t:t + 1], None, ALU.mult)
                dve.tensor_scalar(r[:, t, 512:D], r[:, t, 512:D], rstd[:, 2 + t:3 + t], None, ALU.mult).then_inc(
                    sem("x"), 1)
            split_x("mix2", COLS["out2"])
            advance(AT["out2"] + 3 + LEAD)
            residual("out2", (used, AT["out2"] + 4), x, 1.0, 1.0)
            rms_scale("nmem", r)
            split_x("nmem", COLS["mem"])
            advance(AT["wk"] + 3 + LEAD)
            for g in range(2):
                advance(AT["wv"] + 2 * g + 1 + LEAD)
                evac("wv", g, 1, xv[:, 1, 512 * g:512 * g + 512], 512, 2 * g + 1)
            rms_scale("ncross", x)
            split_x("ncross", COLS["cross"])
            last = AT["wq"] + 3
            advance(last + LEAD)
            for i in range(X_H + 2):
                if i < X_H:
                    dve.wait_ge(sem("x_s"), i + 1)
                    link(dve.tensor_reduce(nmax[:, i, :], ps[2 + i % 2][:, :].rearrange("p (t m) -> p t m", t=T), AX, ALU.max,
                                           negate=True))
                    dve.tensor_scalar(nmax[:, i, :], nmax[:, i, :], X_D ** -0.5, None, ALU.mult).then_inc(sem("x_mx"), 1)
                if 1 <= i < X_H + 1:
                    n = i - 1
                    dve.wait_ge(sem("x_tp"), n + 1)
                    if n >= 2:
                        dve.wait_ge(sem("x_od"), n - 1)
                    dve.tensor_copy(probt[:, n % 2, :], ps[4 + n % 2][:, :]).then_inc(sem("x_pt"), 1)
                if i >= 2:
                    n = i - 2
                    dve.wait_ge(sem("x_od"), n + 1)
                    link(dve.reciprocal(rinv[:, n, :], rsum[:, n, :]))
                    for t in range(T):
                        m = dve.tensor_scalar(bc[:, t, n * X_D:(n + 1) * X_D], ps[6 + n % 2][:, t * X_D:(t + 1) * X_D],
                                              rinv[:, n, t:t + 1], None, ALU.mult)
                        if n < X_H - 1 and t == T - 1:
                            m.then_inc(sem("x_o"), 1)
                        if n == X_H - 1:
                            m.then_inc(sem("x"), 1)
                advance(last + 1 + i if i < SPLIT else 0)
            split_x("xo")
            advance(AT["xo"] + 3 + LEAD)
            residual("xo", (used, AT["xo"] + 4), x, 1.0, 1.0)
            rms_scale("n2", x)
            split_x("n2", COLS["ffn2"])
            ffn("f3", U_FF)
            residual("f3", (used, AT["f3"] + 3 * U_FF), x, 1.0, 0.5)
            dve.wait_ge(*at("fin", "sd", 1))
            dve.wait_ge(sem("rows11"), 16)
            link(dve.reciprocal(rstd[:, 0:T], sd[:, 0:T]))
            for t in range(T):
                dve.scalar_tensor_tensor(out=r[:, t, :], in0=x[:, t, :], scalar=rstd[:, t:t + 1], in1=bc[:, 0, :],
                                         op0=ALU.mult, op1=ALU.mult).then_inc(sem("final"), 1)


def shape_constants():
    f = np.float32
    i = np.arange(S)[:, None]
    j = np.arange(S)[None, :]
    parts = {}
    log_gamma = np.log(f(1.0) - f(2.0) ** (-f(5.0) - np.arange(RET_H, dtype=f)))
    dist = np.maximum(i.T - np.arange(P)[:, None], 0).astype(f)
    decay = np.exp(log_gamma[:, None, None] * dist) * (i.T >= np.arange(P)[:, None]) * f(HD ** -0.5)
    parts["ret"] = decay.transpose(1, 0, 2)

    def tiles(m):
        return np.concatenate([m[0:P, 0:P], m[P:S, :]], axis=1)

    causal = np.where(j <= i, 0.0, NEG)
    parts["mla"] = tiles(causal)
    slopes = f(2.0) ** (f(-8.0) * (np.arange(MOBA_H, dtype=f) + 1) / f(MOBA_H))
    parts["moba"] = np.stack([tiles(np.where(j <= i, -s * (i - j).astype(f), NEG)) for s in slopes], axis=1)
    count = sum(((j <= i) & ((i - j) % d == 0) & (i - j <= w)).astype(f) for w, d in ((128, 1), (512, 4), (2048, 16)))
    parts["dil"] = tiles(np.where(count > 0, np.log(np.maximum(count, 1)), NEG))
    for name, dim in (("a", 32), ("b", 64)):
        inv = f(10000.0) ** (-np.arange(0, dim, 2, dtype=f) / f(dim))
        ang = np.arange(S, dtype=f)[:, None] * inv[None, :]
        for fn, g in (("cos", np.cos), ("sin", np.sin)):
            parts[f"{fn}_{name}"] = g(ang).reshape(T, P, dim // 2).transpose(1, 0, 2)
    inv = f(500000.0) ** (f(-2.0) * np.arange(8, dtype=f) / f(16))
    parts["inv_freq"] = np.broadcast_to(inv, (P, 8))
    parts["ident"] = np.eye(P)
    parts["tril"] = np.tril(np.ones((P, P)))
    parts["tri8"] = np.broadcast_to(np.tril(np.ones((NE, NE)), -1).reshape(1, 64), (P, 64))
    return np.concatenate([np.asarray(parts[n], f).reshape(P, -1) for n, _ in CONST_PARTS], axis=1)


def route_constants():
    n = np.arange(P)
    parts = [n[:, None] < n[None, :], np.ones((P, P)), np.broadcast_to(n, (P, P)), np.zeros((P, P))]
    return np.concatenate([q.astype(np.float32) for q in parts], axis=1)


def lay_out_stream(a):
    big = np.zeros((NCHUNK, P, CW), np.float32)

    def project(name, w):
        n = AT[name]
        for c in range(0, w.shape[1], 512):
            part = w[:, c:c + 512]
            wide = part.shape[1]
            v = part.reshape(KD, P, wide).transpose(1, 0, 2)
            if wide == 512:
                big[n] = v[:, 0:4].reshape(P, CW)
                big[n + 1] = v[:, 4:8].reshape(P, CW)
                n += 2
            else:
                big[n, :, 0:KD * wide] = v.reshape(P, KD * wide)
                n += 1

    def ffn(name, gate, up, down):
        units = gate.shape[0] * gate.shape[2] // FU
        per = units // gate.shape[0]
        first_chunk = AT[name]
        for u in range(units):
            e, c = u // per, (u % per) * FU
            gu = np.concatenate([gate[e, :, c:c + FU].reshape(KD, P, FU), up[e, :, c:c + FU].reshape(KD, P, FU)], axis=2)
            v = gu.transpose(1, 0, 2)
            first = first_chunk + max(3 * u - 1, 0)
            big[first] = v[:, 0:4].reshape(P, CW)
            big[first + 1] = v[:, 4:8].reshape(P, CW)
            last = first_chunk + (3 * u + 4 if u < units - 1 else 3 * u + 2)
            big[last] = down[e, c:c + FU].reshape(2, P, D).transpose(1, 0, 2).reshape(P, CW)

    for l in range(DEPTH):
        project(f"in{l}", a["w_in"][l])
        big[AT[f"uq{l}"], :, 0:1152] = a["w_uq"][l].reshape(2, P, 576).transpose(1, 0, 2).reshape(P, 1152)
        big[AT[f"ukv{l}"], :, 0:768] = a["w_ukv"][l]
        project(f"o{l}", a["w_o"][l])
    ffn("f0", a["ffn_w_gate"], a["ffn_w_up"], a["ffn_w_down"])
    big[AT["router"], :, 0:KD * NE] = a["router"][0].reshape(KD, P, NE).transpose(1, 0, 2).reshape(P, KD * NE)
    ffn("f1", a["exp_w_gate"][0], a["exp_w_up"][0], a["exp_w_down"][0])
    ffn("f2", a["ffn1_w_gate_2"], a["ffn1_w_up_2"], a["ffn1_w_down_2"])
    project("in2", a["w_in_2"][0])
    project("out2", a["w_out_2"][0])
    project("wk", a["cross_wk_2"][0])
    project("wv", a["cross_wv_2"][0])
    project("wq", a["cross_wq_2"][0])
    project("xo", a["cross_wo_2"][0])
    ffn("f3", a["ffn2_w_gate_2"], a["ffn2_w_up_2"], a["ffn2_w_down_2"])
    return big


def kernel(**inputs):
    import concourse.bacc as bacc
    from concourse.bass_utils import run_bass_kernel_spmd

    a = {k: np.asarray(v) for k, v in inputs.items()}
    one = np.ones(O_MOBA - O_RET, np.float32)
    gains = []
    for l in range(DEPTH):
        gains += [a["q_norm_g"][l], a["kv_norm_g"][l], a["beta_mla"][l], one, a["beta_moba"][l]]
    gains += [a["ffn1_norm_2"][0], a["mix_norm_2"][0], a["out_norm_a_2"][0], a["out_norm_b_2"][0], a["cross_norm_2"][0],
              a["mem_norm_2"][0], a["ffn2_norm_2"][0], a["sgu_b_s_2"][0].reshape(-1)]
    rows = [a["ln_emb_g"], a["ln_emb_b"]]
    for l in range(DEPTH):
        rows += [a["ln1_g"][l], a["ln1_b"][l], a["ln2_g"][l], a["ln2_b"][l]]
    rows += [np.concatenate([a["sgu_ln_g_2"][0], a["sgu_ln_b_2"][0]]), a["final_norm_2"]]
    arrays = {
        "stream": lay_out_stream(a),
        "x": a["x"][0],
        "mem": a["mem_2"][0],
        "positions": np.ascontiguousarray(a["positions_2"][0].reshape(T, P).T),
        "consts": shape_constants(),
        "route": route_constants(),
        "cols": np.ascontiguousarray(np.concatenate(gains).reshape(NCOL, P).T),
        "rows": np.stack(rows),
        "spatial": a["sgu_w_s_2"][0],
    }
    nc = bacc.Bacc("TRN2", target_bir_lowering=False, num_devices=1)
    args = [nc.dram_tensor(f"in_{n}", v.shape, mybir.dt.from_np(v.dtype), kind="ExternalInput").ap() for n, v in arrays.items()]
    out = nc.dram_tensor("out", (S, D), F32, kind="ExternalOutput").ap()
    program(nc, *args, out)
    result = run_bass_kernel_spmd(nc, [{f"in_{n}": v for n, v in arrays.items()}], core_ids=[0])
    return result.results[0]["out"].reshape(1, S, D)
```

```python
from contextlib import ExitStack
from math import lcm

import numpy as np

import concourse.bass as bass
from concourse import mybir

ALU = mybir.AluOpType
ACT = mybir.ActivationFunctionType
F32 = mybir.dt.float32
F32R = mybir.dt.float32r
I32 = mybir.dt.int32
AX = mybir.AxisListType.X

P = 128
T = 2
S = T * P
D = 1024
KD = D // P
CW = 2048
RAW = 6
SPLIT = 3
LEAD = SPLIT - 1
LATENTS_AT = 4
RET_SUMS_AT = 10
ROOTS_AT, SCALE_AT = 14, 17
GATING_ROOTS_AT, GATING_SCALE_AT = 3, 5
QUERIES_AT = 4
FU = 256
UNROLL = lcm(RAW, SPLIT, 3) // 3
LB = 3 * UNROLL

DEPTH = 2
ALPHA = (2 * DEPTH) ** 0.25
LN_EPS = 1e-5
RMS_EPS = 1e-6
MLA_H, NOPE, ROPE = 6, 64, 32
QD = NOPE + ROPE
RET_H = MOBA_H = 5
HD = 64
DIL_H = 8
X_H, X_D = 4, 256
D_IN = 2656
D_IN2 = 2560
C_ROPE, C_RQ, C_RK, C_RV, C_RG, C_MQ, C_MK, C_MV = 384, 416, 736, 1056, 1376, 1696, 2016, 2336
O_RET, O_MOBA = 384, 704
D_FF, D_FFE, NE = 2816, 3584, 8
U_FF = D_FF // FU
U_E = D_FFE // FU
U_MOE = NE * U_E
ROUNDS_E = 3 * U_E // RAW
GATHER_AT = (6, 9)
NEG = -1e30

CONST_PARTS = [("ret", RET_H * S), ("moba", MOBA_H * 384), ("mla", 384), ("dil", 384), ("cos_a", T * 16),
               ("sin_a", T * 16), ("cos_b", T * 32), ("sin_b", T * 32), ("inv_freq", 8),
               ("tril", P), ("tri8", 64), ("ident", P)]
CONST_AT, CONST_W = {}, 0
for _name, _w in CONST_PARTS:
    CONST_AT[_name] = (CONST_W, CONST_W + _w)
    CONST_W += _w

COLS = {}
_n = 0
for _name, _w in [("q0", 2), ("kv0", 1), ("mix0", 8), ("q1", 2), ("kv1", 1), ("mix1", 8), ("ffn1", 8),
                  ("in2", 8), ("out2", 8), ("cross", 8), ("mem", 8), ("ffn2", 8), ("b_s", 8)]:
    COLS[_name] = _n
    _n += _w
NCOL = _n

PROJ = [CW] * 2


def ffn_widths(units):
    return [CW] * (3 * units)


STREAM = []
for _l in range(DEPTH):
    STREAM += [(f"in{_l}", PROJ * 5 + [KD * 96]), (f"ukv{_l}", [768]), (f"uq{_l}", [2 * 576]), (f"o{_l}", PROJ * 2)]
    STREAM += [("f0", ffn_widths(U_FF))] if _l == 0 else [("router", [KD * NE]), ("f1", ffn_widths(U_MOE))]
STREAM += [("f2", ffn_widths(U_FF)), ("in2", PROJ * 5), ("out2", PROJ * 2), ("wk", PROJ * 2), ("wv", PROJ * 2),
           ("wq", PROJ * 2), ("xo", PROJ * 2), ("f3", ffn_widths(U_FF))]
AT, WIDTH = {}, []
for _name, _ws in STREAM:
    AT[_name] = len(WIDTH)
    WIDTH += _ws
NCHUNK = len(WIDTH)
STREAM_LENGTH = [(_name, len(_ws)) for _name, _ws in STREAM]


LAYERS = range(DEPTH)
N_HEADS = RET_H + MOBA_H + MLA_H
N_SOFT = MOBA_H + MLA_H


def _by_layer(*parts, skip=()):
    return [(f"{n}{l}", c) for l in LAYERS for n, c in parts if f"{n}{l}" not in skip]


_ffns = [("f0", U_FF), ("f2", U_FF), ("f3", U_FF)]
RAISED = {
    "tr": [("emb", 4)] + _by_layer(("lat", 2), ("mix", 4), ("ln1_", 4), ("ln2_", 4), skip=("ln2_1",))
    + [(n, 4) for n in ("n1", "nmix", "mix2", "nmem", "ncross", "xo", "n2")],
    "xh": [("emb", 4)] + _by_layer(("lat", 3), ("mix", KD), ("ln1_", 4), ("ln2_", 4), skip=("ln2_1",))
    + [(n, 4 if n == "xo" else KD) for n in ("n1", "nmix", "mix2", "nmem", "ncross", "xo", "n2")],
    "xt": [("emb", 4)] + _by_layer(("lat", 2), ("mix", KD), ("ln1_", 4), ("ln2_", 4), skip=("ln2_1",))
    + [(n, 4 if n == "xo" else KD) for n in ("n1", "nmix", "mix2", "nmem", "ncross", "xo", "n2")],
    "sd": [("emb", T)] + _by_layer(("lat", 1), ("early", 2), ("mix", 1), ("ln1_", T), ("ln2_", T))
    + [(n, 1 if n in ("sgu", "mixa", "mix2") else T) for n in ("n1", "nmix", "sgu", "mixa", "mix2", "nmem", "ncross", "n2", "fin")],
    "x": [("emb", T)] + _by_layer(("lat", T), ("mix", T), ("ln1_", T), ("ln2_", T))
    + [(n, T) for n in ("n1", "nmix", "mix2", "nmem", "ncross", "xo", "n2")],
    "mv": [("emb", 1)] + _by_layer(("ln1_", 1), ("ln2_", 1)),
    "pj": _by_layer(("in", 6), ("o", 2)) + [("in2", 5), ("out2", 2), ("wk", 6), ("wv", 2), ("wq", 6), ("xo", 2)],
    "ev0": _by_layer(("in", 6)) + [("in2", 7), ("wv", 2)],
    "ev1": _by_layer(("in", 6)) + [("in2", 3), ("wv", 2)],
    "ev": _by_layer(("uq", 4)) + [("wk", KD), ("wq", KD)],
    "resid": [(n, 4) for n in ("o0", "f0", "o1", "f1", "f2", "out2", "xo", "f3")],
}
for _k in ("tq", "qk", "s", "pt", "od", "o"):
    RAISED[_k] = [("at0", N_HEADS), ("at1", N_HEADS), ("dil", DIL_H)]
for _k in ("sf", "mx", "p", "tp", "ri"):
    RAISED[_k] = [("at0", N_SOFT), ("at1", N_SOFT), ("dil", DIL_H)]
UNIT_KINDS = ("sg", "hu", "ut", "hh", "ht")
for _k, _c in (("sg", T), ("hu", T), ("ut", 1), ("hh", 1), ("ht", 1)):
    RAISED[_k] = [(n, _c * u) for n, u in _ffns]


def before(stage, kind):
    total = 0
    for name, count in RAISED[kind]:
        if name == stage:
            return total
        total += count
    raise KeyError((stage, kind))


class Chunk:

    def __init__(self, base, it=0):
        self.raw = base % RAW
        self.split = base % SPLIT
        self.width = WIDTH[base]
        self.base = base
        self.n = base + LB * it
        self.landed = 16 * (base // RAW + 1) + (16 * (LB // RAW)) * it


def heads_of_layer():
    return ([("ret", n) for n in range(RET_H)] + [("moba", n) for n in range(MOBA_H)]
            + [("mla", n) for n in range(MLA_H)])


def program(nc, stream, x_in, mem_in, pos_in, consts, route_in, cols_in, rows_in, ws_in, out):
    with ExitStack() as ctx:
        def sb(name, shape, dt=F32):
            return ctx.enter_context(nc.sbuf_tensor(name, shape, dt))

        sems = {}

        def sem(name):
            if name not in sems:
                sems[name] = ctx.enter_context(nc.semaphore(name))
            return sems[name]

        def at(stage, kind, count):
            if stage == "f1" and kind in UNIT_KINDS:
                return sem(f"f1_{kind}"), count
            return sem(kind), count + before(stage, kind)

        def unit_sem(stage, kind):
            return sem(f"f1_{kind}" if stage == "f1" else kind)

        def group_done(name, g, t):
            if t < T - 1:
                return at(name, "pj", g + 1)
            return used, AT[name] + min(2 * g + 2, dict(STREAM_LENGTH)[name])

        def tile_done(name, j):
            if j % 4 < 3:
                return at(name, "pj", 3 * (j // 4) + j % 4 + 1)
            return used, AT[name] + 2 * (j // 4) + 2

        raw = sb("raw", [P, RAW, CW])
        whi = sb("whi", [P, SPLIT, CW], F32R)
        wlo = sb("wlo", [P, SPLIT, CW], F32R)
        x = sb("resid", [P, T, D])
        r = sb("r", [P, T, D])
        xth = sb("xth", [P, KD, S], F32R)
        xtl = sb("xtl", [P, KD, S], F32R)
        h = sb("h", [P, T, D_IN])
        qc = sb("qc", [P, T, MLA_H, QD])
        kc = sb("kc", [P, T, MLA_H, QD])
        vc = sb("vc", [P, T, MLA_H, NOPE])
        qkt = sb("qkt", [P, 2, 512])
        prob = sb("prob", [P, 2, 512])
        probt = sb("probt", [P, 2, 512])
        hth = sb("hth", [P, 3, S], F32R)
        htl = sb("htl", [P, 3, S], F32R)
        bc = sb("bc", [P, 2, D])
        cst = sb("cst", [P, CONST_W])
        cols = sb("cols", [P, NCOL])
        bn = sb("bn", [P, 2, 6])
        mv = sb("mv", [P, T, 2])
        nmax = sb("nmax", [P, 16, T])
        rsum = sb("rsum", [P, 16, T])
        rinv = sb("rinv", [P, 16, T])
        ss = sb("ss", [P, 4])
        sd = sb("sd", [P, 4])
        rstd = sb("rstd", [P, 4])
        gs = sb("gs", [P, 4, 16])
        eps = sb("eps", [P, 2])
        flag = sb("flag", [P, 1], I32)
        small = sb("small", [P, 8, 16])
        lg = sb("lg", [P, 8, T, NE])
        posi = sb("posi", [P, T], I32)
        rot = sb("rot", [P, 6, T, 8])
        ps = [ctx.enter_context(nc.psum_tensor(f"ps{b}", [P, 512], F32)) for b in range(8)]

        def const(name):
            a, b = CONST_AT[name]
            return cst[:, a:b]

        ident = const("ident")
        c_ret = const("ret").rearrange("p (h i) -> p h i", h=RET_H)
        c_moba = const("moba").rearrange("p (h i) -> p h i", h=MOBA_H)
        sg = prob[:, :, 0:FU]
        hs = probt[:, :, 0:FU]
        hflat = h[:, :, :].rearrange("p t n -> p (t n)")
        onehot = hflat[:, 0:NE * S].rearrange("p (e t s) -> p e t s", e=NE, t=T)
        spread = hflat[:, NE * S:2 * NE * S].rearrange("p (e s) -> p e s", e=NE)
        spread_now = hflat[:, 2 * NE * S:2 * NE * S + S]
        route = hflat[:, 2 * NE * S + S:2 * NE * S + S + 4 * P].rearrange("p (n s) -> p n s", n=4)
        earlier, ones, slots, zeros = (route[:, n, :] for n in range(4))
        gated = r[:, :, :].rearrange("p t n -> p (t n)").rearrange("p (e t s) -> p e t s", e=NE, t=T)
        gexp = qkt[:, 0, 0:U_MOE].rearrange("p (n t) -> p n t", t=T)
        lg3 = qkt[:, 1, 0:4 * NE * NE].rearrange("p (a t e f) -> p a t e f", a=2, t=T, e=NE)
        kt = hflat[:, 0:KD * S].rearrange("p (k s) -> p k s", k=KD)
        xv = hflat[:, KD * S:2 * KD * S].rearrange("p (t n) -> p t n", t=T)
        qt = r[:, :, :].rearrange("p t n -> p (t n)").rearrange("p (k s) -> p k s", k=KD)
        ws = kc[:, :, :, :].rearrange("p t h d -> p (t h d)")[:, 0:8 * P].rearrange("p (g j) -> p g j", g=8)
        wst = qc[:, :, :, :].rearrange("p t h d -> p (t h d)")[:, 0:8 * P].rearrange("p (g j) -> p g j", g=8)

        landed = [sem(f"landed{n}") for n in range(RAW)]
        hi_done = sem("hi_done")
        lo_done = sem("lo_done")
        used = sem("used")

        def f32(ap):
            return ap.bitcast(F32)

        block = ctx.enter_context(nc.Block())

        @block.sync
        def _(sp):
            def load(c):
                if not (isinstance(c.n, int) and c.n < RAW):
                    sp.wait_ge(lo_done, c.n - RAW + 1)
                sp.dma_start(raw[:, c.raw, 0:c.width], stream[c.n, :, 0:c.width]).then_inc(landed[c.raw], 16)

            for t in range(T):
                sp.wait_ge(sem(f"x_in{t}"), 16)
            n = 0
            while n < NCHUNK:
                if any(n == AT[f] for f in ("f0", "f1", "f2", "f3")):
                    name = next(f for f in ("f0", "f1", "f2", "f3") if n == AT[f])
                    loops = 3 * (U_MOE if name == "f1" else U_FF) // LB
                    with sp.Fori(0, loops) as it:
                        for j in range(LB):
                            load(Chunk(n + j, it))
                    n += loops * LB
                else:
                    load(Chunk(n))
                    n += 1

        @block.gpsimd
        def _(pool):
            pool.memset(eps[:, 0:1], LN_EPS).then_inc(sem("eps_set"), 1)
            pool.memset(eps[:, 1:2], RMS_EPS).then_inc(sem("eps_set"), 1)
            for t in range(T):
                pool.dma_start(r[:, t, :], x_in[t * P:(t + 1) * P, :]).then_inc(sem(f"x_in{t}"), 16)

            def rows(n, count, free, value):
                if free:
                    pool.wait_ge(*at(free[0], free[1], value))
                pool.dma_start(bc[:, 0:count, :], rows_in[n:n + count, :].partition_broadcast(P)).then_inc(
                    sem(f"rows{n}"), 16)

            rows(0, 2, None, 0)
            pool.dma_start(ident, consts[:, CONST_AT["ident"][0]:CONST_AT["ident"][1]]).then_inc(sem("ident_in"), 16)
            pool.dma_start(cols[:, :], cols_in).then_inc(sem("cols_in"), 16)
            pool.wait_ge(*at("emb", "x", 1))
            pool.dma_start(cst[:, 0:CONST_AT["ident"][0]], consts[:, 0:CONST_AT["ident"][0]]).then_inc(sem("const_in"), 16)
            pool.dma_start(posi[:, :], pos_in).then_inc(sem("pos_in"), 16)
            for l in range(DEPTH):
                rows(2 + 4 * l, 2, ("emb" if l == 0 else "ln2_0", "x"), T)
                rows(4 + 4 * l, 2, (f"ln1_{l}", "x"), T)
                if l == 1:
                    pool.wait_ge(*at("mix1", "x", T))
                    pool.dma_start(route, route_in.rearrange("p (n s) -> p n s", n=4)).then_inc(sem("route_in"), 16)
            rows(10, 1, ("ln2_1", "x"), T)
            pool.wait_ge(*at("ln2_1", "x", T))
            pool.dma_start(ws, ws_in.rearrange("g i j -> i g j")).then_inc(sem("ws_in"), 16)
            pool.wait_ge(sem("v_norm"), 1)
            pool.dma_start(bc[:, :, :], mem_in.rearrange("(t p) d -> p t d", p=P)).then_inc(sem("mem_in"), 16)
            rows(11, 1, ("xo", "tr"), 4)
            for t in range(T):
                pool.wait_ge(sem("final"), t + 1)
                pool.dma_start(out[t * P:(t + 1) * P, :], r[:, t, :]).then_inc(sem("stored"), 16)
            pool.wait_ge(sem("stored"), 16 * T)

        @block.tensor
        def _(pe):
            def mm3(o, ah, al, bh, bl, start, stop):
                pe.matmul(o, ah, bh, start=start, stop=False, skip_group_check=True)
                pe.matmul(o, ah, bl, start=False, stop=False, skip_group_check=True)
                return pe.matmul(o, al, bh, start=False, stop=stop, skip_group_check=True)

            def chunk(c):
                pe.wait_ge(lo_done, c.n + 1)

            def split_done(stage, k):
                pe.wait_ge(*at(stage, "xt", (k // 2 + 1) * dict(RAISED["xt"])[stage] // (KD // 2)))

            def transpose_x(stage, src, kn=KD, banks=(0, 1, 2, 3)):
                for t in range(T):
                    pe.wait_ge(*at(stage, "x", t + 1))
                    for k in range(kn):
                        m = pe.transpose(ps[banks[k // 2]][:, (k % 2) * S + t * P:(k % 2) * S + (t + 1) * P],
                                         src[:, t, k * P:(k + 1) * P], ident)
                        if t == T - 1 and (k % 2 == 1 or k == kn - 1):
                            m.then_inc(sem("tr"), 1)

            def project(name, stage, ah, al, groups, kn, bank, ready, free, turned_in_course=None):
                n = AT[name]
                for g, (width, chunks) in enumerate(groups):
                    if g == 1 and turned_in_course:
                        transpose_x(*turned_in_course)
                    if g == LATENTS_AT and name.startswith("in") and name != "in2":
                        transpose_x(f"lat{name[2:]}", h, kn=3, banks=(4, 5))
                    per = kn // chunks
                    for j in range(chunks):
                        c = Chunk(n)
                        n += 1
                        chunk(c)
                        wh = whi[:, c.split, 0:per * width].rearrange("p (k n) -> p k n", k=per)
                        wl = wlo[:, c.split, 0:per * width].rearrange("p (k n) -> p k n", k=per)
                        for t in range(T):
                            if j == 0:
                                free(g, t)
                            for k in range(per):
                                kk = j * per + k
                                if ready and g == 0 and t == 0:
                                    split_done(ready, kk)
                                m = mm3(ps[bank(g, t)][:, 0:width], ah[:, kk, t * P:(t + 1) * P],
                                        al[:, kk, t * P:(t + 1) * P], wh[:, k, :], wl[:, k, :],
                                        start=(kk == 0), stop=(kk == kn - 1))
                            if j == chunks - 1 and t < T - 1:
                                m.then_inc(sem("pj"), 1)
                        m.then_inc(used, 1)

            def project_t(name, stage, ready, free):
                for g in range(2):
                    for j in range(2):
                        c = Chunk(AT[name] + 2 * g + j)
                        chunk(c)
                        wh = whi[:, c.split, :].rearrange("p (k n) -> p k n", k=4)
                        wl = wlo[:, c.split, :].rearrange("p (k n) -> p k n", k=4)
                        for q in range(4):
                            if j == 0:
                                free(4 * g + q)
                                if g == 0:
                                    split_done(ready, 2 * q)
                            for k in range(4):
                                kk = 4 * j + k
                                if g == 0 and q == 0:
                                    split_done(ready, kk)
                                m = mm3(ps[4 * g + q][:, 0:S], wh[:, k, q * P:(q + 1) * P], wl[:, k, q * P:(q + 1) * P],
                                        xth[:, kk, :], xtl[:, kk, :], start=(kk == 0), stop=(kk == 7))
                            if j == 1 and q < 3:
                                m.then_inc(sem("pj"), 1)
                        m.then_inc(used, 1)

            def ffn(name, units, ready=None):
                first_chunk = AT[name]

                def gate_up(a, b, ready=None):
                    for j, c in enumerate((a, b)):
                        chunk(c)
                        wh = whi[:, c.split, :].rearrange("p (k n) -> p k n", k=4)
                        wl = wlo[:, c.split, :].rearrange("p (k n) -> p k n", k=4)
                        for t in range(T):
                            for k in range(4):
                                kk = 4 * j + k
                                if ready and t == 0:
                                    split_done(ready, kk)
                                m = mm3(ps[t][:, :], xth[:, kk, t * P:(t + 1) * P], xtl[:, kk, t * P:(t + 1) * P],
                                        wh[:, k, :], wl[:, k, :], start=(kk == 0), stop=(kk == 7))
                        m.then_inc(used, 1)

                def down(c, u, first, last):
                    chunk(c)
                    pe.wait_ge(*at(name, "ht", u + 1))
                    wh = whi[:, c.split, :].rearrange("p (k n) -> p k n", k=2)
                    wl = wlo[:, c.split, :].rearrange("p (k n) -> p k n", k=2)
                    for t in range(T):
                        for n in range(2):
                            for k in range(2):
                                m = mm3(ps[4 + 2 * t + n][:, :], hth[:, k, t * P:(t + 1) * P], htl[:, k, t * P:(t + 1) * P],
                                        wh[:, k, n * 512:(n + 1) * 512], wl[:, k, n * 512:(n + 1) * 512],
                                        start=first and k == 0, stop=last and k == 1)
                    m.then_inc(used, 1)

                def turn(u):
                    pe.wait_ge(*at(name, "hu", 2 * u + 2))
                    for t in range(T):
                        for k in range(2):
                            m = pe.transpose(ps[2][:, k * S + t * P:k * S + (t + 1) * P], hs[:, t, k * P:(k + 1) * P], ident)
                    m.then_inc(unit_sem(name, "ut"), 1)

                def unit(u, base, it, first):
                    gate_up(Chunk(base, it), Chunk(base + 1, it))
                    down(Chunk(base + 2, it), u - 1, first, False)
                    turn(u)

                gate_up(Chunk(first_chunk), Chunk(first_chunk + 1), ready)
                turn(0)
                unit(1, first_chunk + 2, 0, True)
                loops = (units - 3) // UNROLL
                with pe.Fori(0, loops) as it:
                    for j in range(UNROLL):
                        unit(it * UNROLL + 2 + j, first_chunk + 5 + 3 * j, it, False)
                for u in range(2 + loops * UNROLL, units):
                    unit(u, first_chunk + 3 * u - 1, 0, False)
                down(Chunk(first_chunk + 3 * units - 1), units - 1, False, True)

            def experts():
                first_chunk = AT["f1"]

                def gather(e, q, g, bank):
                    for k in range(4):
                        for t in range(T):
                            m = pe.matmul(ps[bank][:, k * P:(k + 1) * P], x[:, t, (4 * g + k) * P:(4 * g + k + 1) * P],
                                          onehot[:, e, t, :], start=(t == 0), stop=(t == T - 1))
                    m.then_inc(sem("e_ga"), 1)

                def gate_up(q, a, b):
                    for j, c in enumerate((a, b)):
                        chunk(c)
                        wh = whi[:, c.split, :].rearrange("p (k n) -> p k n", k=4)
                        wl = wlo[:, c.split, :].rearrange("p (k n) -> p k n", k=4)
                        for k in range(4):
                            kk = 4 * j + k
                            m = mm3(ps[0][:, :], xth[:, kk, q * P:(q + 1) * P], xtl[:, kk, q * P:(q + 1) * P],
                                    wh[:, k, :], wl[:, k, :], start=(kk == 0), stop=(kk == 7))
                        m.then_inc(used, 1)

                def down(c, u, first, last):
                    chunk(c)
                    pe.wait_ge(sem("e_ht"), u + 1)
                    wh = whi[:, c.split, :].rearrange("p (k n) -> p k n", k=2)
                    wl = wlo[:, c.split, :].rearrange("p (k n) -> p k n", k=2)
                    for n in range(2):
                        for k in range(2):
                            m = mm3(ps[2 + n][:, :], hth[:, k, 0:P], htl[:, k, 0:P], wh[:, k, n * 512:(n + 1) * 512],
                                    wl[:, k, n * 512:(n + 1) * 512], start=first and k == 0, stop=last and k == 1)
                    m.then_inc(used, 1)

                def turn(u):
                    pe.wait_ge(sem("e_h"), u + 1)
                    for k in range(2):
                        m = pe.transpose(ps[1][:, k * P:(k + 1) * P], hs[:, 0, k * P:(k + 1) * P], ident)
                    m.then_inc(sem("e_ut"), 1)

                def turn_gates():
                    pe.wait_ge(sem("rt_gated"), 1)
                    for e in range(NE):
                        for t in range(T):
                            m = pe.transpose(ps[4 + e // 2][:, (e % 2) * S + t * P:(e % 2) * S + (t + 1) * P], gated[:, e, t],
                                             ident)
                        if e % 2:
                            m.then_inc(sem("rt_turned"), 1)

                def clear_sums():
                    pe.wait_ge(sem("rt_spread"), 4)
                    for b in range(4, 8):
                        pe.matmul(ps[b][:, :], zeros[0:1, :], cst[0:1, 0:512], start=True, stop=False,
                                  skip_group_check=True)

                def scatter(q):
                    for t in range(T):
                        for n in range(2):
                            m = pe.matmul(ps[4 + 2 * t + n][:, :], spread_now[:, t * P:(t + 1) * P], r[:, q, n * 512:(n + 1) * 512],
                                          start=False, stop=False, skip_group_check=True)
                    m.then_inc(sem("e_sc"), 1)

                def unit(e, q, j, base, rounds, u):
                    gate_up(q, Chunk(base, rounds), Chunk(base + 1, rounds))
                    gathering = j in GATHER_AT and e is not None
                    if gathering:
                        pe.wait_ge(sem("e_ht"), u)
                        gather(e + 1, 1 - q, GATHER_AT.index(j), 1)
                    if j == 1 and not (isinstance(u, int) and u == 1):
                        pe.wait_ge(sem("e_oa"), e)
                        pe.wait_ge(sem("e_od"), e)
                    if not (isinstance(u, int) and u == 0):
                        down(Chunk(base + 2, rounds), u - 1, j == 1, j == 0)
                    if gathering:
                        pe.wait_ge(sem("e_gx"), 2 * (e + 1) + GATHER_AT.index(j) + 1)
                    turn(u)
                    if j == 1 and not (isinstance(u, int) and u == 1):
                        scatter(1 - q)

                def expert(e, q, rounds, last=False):
                    base = first_chunk - 1
                    ahead = None if last else e
                    if isinstance(e, int) and e == 0:
                        gate_up(q, Chunk(first_chunk), Chunk(first_chunk + 1))
                        turn(0)
                        turn_gates()
                    else:
                        unit(e, q, 0, base, rounds, U_E * e)
                    unit(e, q, 1, base + 3, rounds, U_E * e + 1)
                    if isinstance(e, int) and e == 0:
                        clear_sums()
                    for lo_u, hi_u in ((2, 6), (6, 10), (10, U_E)):
                        if lo_u == 6:
                            for j in range(lo_u, hi_u):
                                unit(ahead, q, j, base + 3 * j, rounds, U_E * e + j)
                            continue
                        with pe.Fori(0, (hi_u - lo_u) // 2) as it:
                            for j in range(lo_u, lo_u + 2):
                                unit(None, q, j if j > 2 else -1, base + 3 * j, rounds + it, U_E * e + j + it * 2)

                pe.wait_ge(sem("rt_one"), 1)
                for g in range(2):
                    gather(0, 0, g, g)
                pe.wait_ge(sem("e_gx"), 2)
                expert(0, 0, 0)
                with pe.Fori(0, (NE - 2) // 2) as pair:
                    for s in range(2):
                        expert(pair * 2 + 1 + s, 1 - s, (pair * 2 + 1 + s) * ROUNDS_E)
                expert(NE - 1, 1, (NE - 1) * ROUNDS_E, last=True)
                down(Chunk(first_chunk + 3 * U_MOE - 1), U_MOE - 1, False, True)
                pe.wait_ge(sem("e_oa"), NE)
                pe.wait_ge(sem("e_od"), NE)
                scatter(1)

            def heads(stage, work, masked):
                soft = [kind != "ret" for kind, _ in work]

                def turn_qk(i):
                    kind, n = work[i]
                    if i >= 2:
                        pe.wait_ge(*at(stage, "qk", i - 1))
                    if (kind, n) == ("mla", 0):
                        pe.wait_ge(sem(f"rope{stage[2:]}"), 1)
                    for s in range(2):
                        for t in range(T):
                            if kind == "mla":
                                src = (qc, kc)[s][:, t, n, :]
                            elif kind == "dil":
                                col = 1024 + 512 * s + HD * n
                                src = h[:, t, col:col + P]
                            else:
                                col = ((C_RQ, C_RK) if kind == "ret" else (C_MQ, C_MK))[s] + HD * n
                                src = h[:, t, col:col + P]
                            w = src.shape[-1]
                            m = pe.transpose(ps[i % 2][0:w, s * S + t * P:s * S + (t + 1) * P], src, ident)
                    m.then_inc(sem("tq"), 1)

                def scores(i):
                    kind, n = work[i]
                    d = QD if kind == "mla" else HD
                    q, k = qkt[0:d, i % 2, 0:S], qkt[0:d, i % 2, S:2 * S]
                    o = ps[2 + i % 2]
                    pe.wait_ge(*at(stage, "qk", i + 1))
                    if i >= 2 and soft[i - 2]:
                        pe.wait_ge(*at(stage, "sf", sum(soft[:i - 1])))
                    elif i >= 2:
                        pe.wait_ge(*at(stage, "pt", i - 1))
                    if kind == "ret":
                        pe.matmul(o[:, 0:S], k[:, 0:P], q, start=True, stop=True)
                        m = pe.matmul(o[:, S:S + P], k[:, P:S], q[:, P:S], start=True, stop=True)
                    else:
                        pe.matmul(o[:, 0:P], q[:, 0:P], k[:, 0:P], start=True, stop=True)
                        m = pe.matmul(o[:, P:P + S], q[:, P:S], k, start=True, stop=True)
                    m.then_inc(sem("s"), 1)

                def turn_p(i):
                    if not soft[i]:
                        return
                    pe.wait_ge(*at(stage, "p", sum(soft[:i + 1])))
                    for b in range(3):
                        m = pe.transpose(ps[4 + i % 2][:, b * P:(b + 1) * P], prob[:, i % 2, b * P:(b + 1) * P], ident)
                    m.then_inc(sem("tp"), 1)

                def outputs(i):
                    kind, n = work[i]
                    pt = probt[:, i % 2, :]
                    pe.wait_ge(*at(stage, "pt", i + 1))
                    if i >= 2:
                        pe.wait_ge(*at(stage, "o", i - 1))
                    elif stage != "dil":
                        pe.wait_ge(sem(f"kv{stage[2:]}"), 1)

                    def v(t):
                        if kind == "mla":
                            return vc[:, t, n, :]
                        col = {"ret": C_RV, "moba": C_MV, "dil": 2048}[kind] + HD * n
                        return h[:, t, col:col + HD]
                    o = ps[6 + i % 2]
                    pe.matmul(o[:, 0:HD], pt[:, 0:P], v(0), start=True, stop=True)
                    pe.matmul(o[:, HD:2 * HD], pt[:, P:2 * P], v(0), start=True, stop=False)
                    pe.matmul(o[:, HD:2 * HD], pt[:, 2 * P:3 * P], v(1), start=False, stop=True).then_inc(
                        sem("od"), 1)

                for i in range(len(work) + 4):
                    if i < len(work):
                        turn_qk(i)
                    if 0 <= i - 3 < len(work) and not soft[i - 3]:
                        outputs(i - 3)
                    if i >= 4 and soft[i - 4]:
                        outputs(i - 4)
                    if 3 <= i < len(work) + 3:
                        turn_p(i - 3)
                    if 1 <= i < len(work) + 1:
                        scores(i - 1)

            pe.wait_ge(sem("ident_in"), 16)
            transpose_x("emb", x)
            xt_stage = "emb"
            for l in range(DEPTH):
                st = f"in{l}"

                def free_in(g, t):
                    if g >= 2:
                        pe.wait_ge(*at(st, f"ev{t}", g - 1))

                groups = [(512, 2)] * 5 + [(96, 1)]
                project(st, st, xth, xtl, groups, KD, lambda g, t: 2 * (g % 2) + t, xt_stage, free_in)
                for g, stage, ks in ((1, f"ukv{l}", (2, 3)), (0, f"uq{l}", (0, 2))):
                    width = 288 if g == 0 else 384
                    c = Chunk(AT[stage])
                    chunk(c)
                    pe.wait_ge(*at(f"lat{l}", "xt", 2))
                    if g == 0:
                        pe.wait_ge(*at(st, "ev0", 6))
                        pe.wait_ge(*at(st, "ev1", 6))
                    kn = ks[1] - ks[0]
                    wh = whi[:, c.split, 0:c.width].rearrange("p (k n) -> p k n", k=kn)
                    wl = wlo[:, c.split, 0:c.width].rearrange("p (k n) -> p k n", k=kn)
                    for t in range(T):
                        for half in range(2):
                            for k in range(kn):
                                m = mm3(ps[4 * g + 2 * t + half][:, 0:width], hth[:, ks[0] + k, t * P:(t + 1) * P],
                                        htl[:, ks[0] + k, t * P:(t + 1) * P], wh[:, k, half * width:(half + 1) * width],
                                        wl[:, k, half * width:(half + 1) * width], start=(k == 0), stop=(k == kn - 1))
                    m.then_inc(used, 1)
                pe.wait_ge(sem(f"ret{l}_qk"), 1)
                pe.wait_ge(*at(f"uq{l}", "ev", 4))
                heads(f"at{l}", heads_of_layer(), True)
                transpose_x(f"mix{l}", r)
                project(f"o{l}", f"o{l}", xth, xtl, [(512, 2)] * 2, KD, lambda g, t: 4 + 2 * t + g,
                        f"mix{l}", lambda g, t: None)
                transpose_x(f"ln1_{l}", x)
                if l == 1:
                    c = Chunk(AT["router"])
                    chunk(c)
                    split_done("ln1_1", KD - 1)
                    for t in range(T):
                        for k in range(KD):
                            m = mm3(ps[3][:, t * NE:(t + 1) * NE], xth[:, k, t * P:(t + 1) * P],
                                    xtl[:, k, t * P:(t + 1) * P], whi[:, c.split, k * NE:(k + 1) * NE],
                                    wlo[:, c.split, k * NE:(k + 1) * NE], start=(k == 0), stop=(k == KD - 1))
                    m.then_inc(used, 1)
                if l == 0:
                    ffn("f0", U_FF, "ln1_0")
                    transpose_x("ln2_0", x)
                    xt_stage = "ln2_0"
                    continue
                pe.wait_ge(sem("rt_sel"), 1)
                pe.wait_ge(sem("route_in"), 16)
                sel = lg[:, 3]
                pe.matmul(ps[3][:, 32:40], earlier, sel[:, 0], start=True, stop=True)
                pe.matmul(ps[3][:, 40:48], earlier, sel[:, 1], start=True, stop=False)
                pe.matmul(ps[3][:, 40:48], ones, sel[:, 0], start=False, stop=True)
                pe.matmul(ps[3][:, 48:56], ones, sel[:, 0], start=True, stop=False)
                pe.matmul(ps[3][:, 48:56], ones, sel[:, 1], start=False, stop=True).then_inc(sem("rt_rank"), 1)
                pe.wait_ge(sem("rt_flag"), 1)
                overfull = pe.value_load(flag[0:1, 0:1], min_val=0, max_val=1)
                with pe.If(overfull == 0):
                    experts()
                with pe.Else():
                    ffn("f1", U_MOE)

            transpose_x("n1", r)
            ffn("f2", U_FF, "n1")
            transpose_x("nmix", r)

            def free_in2(g, t):
                if g in (2, 3):
                    pe.wait_ge(*at("in2", "ev0", 2 * g - 3 + t))
                if g == 4:
                    pe.wait_ge(*at("in2", f"ev{t}", (5, 1)[t]))
            project("in2", "in2", xth, xtl, [(512, 2)] * 5, KD, lambda g, t: 2 * (g % 2) + t, "nmix", free_in2)
            pe.wait_ge(sem("ws_masked"), 1)
            for g in range(8):
                m = pe.transpose(ps[4 + g // 4][:, (g % 4) * P:(g % 4 + 1) * P], ws[:, g, :], ident)
            m.then_inc(sem("ws_tr"), 1)
            pe.wait_ge(sem("ws_t"), 2)
            pe.wait_ge(sem("v_norm"), 1)
            for g in range(8):
                m = pe.matmul(ps[6 + g // 4][:, (g % 4) * P:(g % 4 + 1) * P], wst[:, g, :],
                              h[:, :, 512 + HD * g:512 + HD * (g + 1)], start=True, stop=True)
            m.then_inc(sem("mixed"), 1)
            pe.wait_ge(sem("rot_done"), 1)
            pe.wait_ge(sem("ya"), 1)
            heads("dil", [("dil", n) for n in range(DIL_H)], True)
            transpose_x("mix2", r)
            project("out2", "out2", xth, xtl, [(512, 2)] * 2, KD, lambda g, t: 4 + 2 * t + g, "mix2",
                    lambda g, t: None, ("nmem", bc))

            def free_k(b):
                if b == 4:
                    pe.wait_ge(*at("out2", "resid", 4))
            project_t("wk", "wk", "nmem", free_k)
            pe.wait_ge(*at("wk", "ev", KD))
            project("wv", "wv", xth, xtl, [(512, 2)] * 2, KD, lambda g, t: 2 * g + t, None, lambda g, t: None,
                    ("ncross", r, KD, (4, 5, 6, 7)))

            def free_q(b):
                if b < 4:
                    pe.wait_ge(*at("wv", f"ev{b % 2}", b // 2 + 1))
            project_t("wq", "wq", "ncross", free_q)
            pe.wait_ge(*at("wq", "ev", KD))
            for i in range(X_H + 2):
                if i >= 2:
                    n = i - 2
                    pe.wait_ge(sem("x_pt"), n + 1)
                    if n >= 2:
                        pe.wait_ge(sem("x_o"), n - 1)
                    for t in range(T):
                        for mt in range(T):
                            m = pe.matmul(ps[6 + n % 2][:, t * X_D:(t + 1) * X_D],
                                          probt[:, n % 2, (2 * t + mt) * P:(2 * t + mt + 1) * P],
                                          xv[:, mt, n * X_D:(n + 1) * X_D], start=(mt == 0), stop=(mt == 1))
                    m.then_inc(sem("x_od"), 1)
                if i < X_H:
                    if i >= 2:
                        pe.wait_ge(sem("x_p"), i - 1)
                    for t in range(T):
                        for k in range(2):
                            m = pe.matmul(ps[2 + i % 2][:, t * S:(t + 1) * S], qt[:, 2 * i + k, t * P:(t + 1) * P],
                                          kt[:, 2 * i + k, :], start=(k == 0), stop=(k == 1))
                    m.then_inc(sem("x_s"), 1)
                if 1 <= i < X_H + 1:
                    n = i - 1
                    pe.wait_ge(sem("x_p"), n + 1)
                    for b in range(4):
                        m = pe.transpose(ps[4 + n % 2][:, b * P:(b + 1) * P], prob[:, n % 2, b * P:(b + 1) * P], ident)
                    m.then_inc(sem("x_tp"), 1)
            transpose_x("xo", bc)
            project("xo", "xo", xth, xtl, [(512, 2)] * 2, KD, lambda g, t: 4 + 2 * t + g, "xo",
                    lambda g, t: None)
            transpose_x("n2", r)
            ffn("f3", U_FF, "n2")

        @block.scalar
        def _(act):
            cursor = [0]
            chained = [0]

            def link(ins):
                chained[0] += 1
                ins.then_inc(sem("act_chain"), 1)
                act.wait_ge(sem("act_chain"), chained[0])

            def hi(c):
                act.wait_ge(landed[c.raw], c.landed)
                if not (isinstance(c.n, int) and c.n < SPLIT):
                    act.wait_ge(used, c.n - SPLIT + 1)
                act.activation(whi[:, c.split, 0:c.width], raw[:, c.raw, 0:c.width], ACT.Copy).then_inc(hi_done, 1)

            def advance(upto):
                while cursor[0] <= min(upto, NCHUNK - 1):
                    hi(Chunk(cursor[0]))
                    cursor[0] += 1

            def split_x(stage, gain=None, kn=KD, dst=xth, banks=(0, 1, 2, 3)):
                for b in range((kn + 1) // 2):
                    act.wait_ge(*at(stage, "tr", b + 1))
                    ks = range(2 * b, min(2 * b + 2, kn))
                    if gain is None:
                        act.activation(dst[:, 2 * b:2 * b + 2, :], ps[banks[b]][:, :].rearrange("p (k s) -> p k s", k=2),
                                       ACT.Copy).then_inc(sem("xh"), 1)
                        continue
                    for k in ks:
                        act.activation(dst[:, k, :], ps[banks[b]][:, (k % 2) * S:(k % 2 + 1) * S], ACT.Copy,
                                       scale=cols[:, gain + k:gain + k + 1]).then_inc(sem("xh"), 1)

            def ln_roots(stage, ready):
                act.wait_ge(*ready)
                link(act.activation(x[:, 1, :], r[:, 1, :], ACT.Copy, accum_out=ss[:, 0:1]))
                link(act.activation(ss[:, 1:2], ss[:, 0:1], ACT.Copy, scale=-1.0 / D))
                act.wait_ge(*at(stage, "mv", 1))
                act.activation(sd[:, 0:1], mv[:, 0, 1:2], ACT.Sqrt, bias=eps[:, 0:1]).then_inc(sem("sd"), 1)
                link(act.activation(x[:, 1, :], r[:, 1, :], ACT.Square, bias=ss[:, 1:2], accum_out=ss[:, 2:3]))
                act.activation(sd[:, 1:2], ss[:, 2:3], ACT.Sqrt, bias=eps[:, 0:1], scale=1.0 / D).then_inc(sem("sd"), 1)

            def rms_roots(stage, tile_ready, junk, src):
                for t in range(T):
                    if tile_ready:
                        act.wait_ge(*tile_ready(t))
                    link(act.activation(junk[:, t, :], src[:, t, :], ACT.Square, accum_out=ss[:, t:t + 1]))
                    act.activation(sd[:, t:t + 1], ss[:, t:t + 1], ACT.Sqrt, bias=eps[:, 1:2], scale=1.0 / D).then_inc(
                        sem("sd"), 1)

            def evac(stage, g, t, dst, width, bank, func=ACT.Copy):
                act.wait_ge(*group_done(stage, g, t))
                act.activation(dst, ps[bank][:, 0:width], func).then_inc(sem("ev0"), 1)

            def ffn(name, units):
                first_chunk = AT[name]

                def unit(u, base, it, chunks):
                    n = base + LEAD
                    for j in range(chunks - 1):
                        if n + j < NCHUNK:
                            hi(Chunk(n + j, it))
                    act.wait_ge(used, base + LB * it + 2)
                    for t in range(T):
                        act.activation(sg[:, t, :], ps[t][:, 0:FU], ACT.Silu).then_inc(unit_sem(name, "sg"), 1)
                    if n + chunks - 1 < NCHUNK:
                        hi(Chunk(n + chunks - 1, it))
                    act.wait_ge(*at(name, "ut", u + 1))
                    act.activation(hth[:, 0:2, :], ps[2][:, :].rearrange("p (k s) -> p k s", k=2), ACT.Copy).then_inc(
                        unit_sem(name, "hh"), 1)

                advance(first_chunk + LEAD - 1)
                unit(0, first_chunk, 0, 2)
                unit(1, first_chunk + 2, 0, 3)
                loops = (units - 3) // UNROLL
                with act.Fori(0, loops) as it:
                    for j in range(UNROLL):
                        unit(it * UNROLL + 2 + j, first_chunk + 5 + 3 * j, it, 3)
                for u in range(2 + loops * UNROLL, units):
                    unit(u, first_chunk + 3 * u - 1, 0, 3)
                cursor[0] = first_chunk + 3 * units - 1 + LEAD

            def experts():
                first_chunk = AT["f1"]

                def gathered(q, g, n, bank):
                    act.wait_ge(sem("e_ga"), n)
                    act.activation(xth[:, 4 * g:4 * g + 4, q * P:(q + 1) * P], ps[bank][:, :].rearrange("p (k s) -> p k s", k=4),
                                   ACT.Copy).then_inc(sem("e_gh"), 1)

                def outputs(q, done):
                    act.wait_ge(*done)
                    act.activation(r[:, q, 0:512], ps[2][:, :], ACT.Copy).then_inc(sem("e_oa"), 1)

                def unit(e, q, j, base, rounds, u, chunks=3):
                    n = base + LEAD
                    for i in range(chunks - 1):
                        hi(Chunk(n + i, rounds))
                    act.wait_ge(used, base + LB * rounds + 2)
                    act.activation(sg[:, 0, :], ps[0][:, 0:FU], ACT.Silu).then_inc(sem("e_sg"), 1)
                    if j in GATHER_AT and e is not None:
                        g = GATHER_AT.index(j)
                        gathered(1 - q, g, 2 * (e + 1) + g + 1, 1)
                    hi(Chunk(n + chunks - 1, rounds))
                    act.wait_ge(sem("e_ut"), u + 1)
                    act.activation(hth[:, 0:2, 0:P], ps[1][:, 0:2 * P].rearrange("p (k s) -> p k s", k=2), ACT.Copy).then_inc(
                        sem("e_hh"), 1)
                    if j == 0 and chunks == 3:
                        outputs(1 - q, (used, base + LB * rounds + 3))

                def expert(e, q, rounds, last=False):
                    base = first_chunk - 1
                    ahead = None if last else e
                    if isinstance(e, int) and e == 0:
                        unit(e, q, 0, first_chunk, 0, 0, chunks=2)
                        for b in range(4):
                            act.wait_ge(sem("rt_turned"), b + 1)
                            act.activation(spread[:, 2 * b:2 * b + 2, :], ps[4 + b][:, :].rearrange("p (e s) -> p e s", e=2),
                                           ACT.Copy).then_inc(sem("rt_spread"), 1)
                    else:
                        unit(e, q, 0, base, rounds, U_E * e)
                    unit(e, q, 1, base + 3, rounds, U_E * e + 1)
                    for lo_u, hi_u in ((2, 6), (6, 10), (10, U_E)):
                        if lo_u == 6:
                            for j in range(lo_u, hi_u):
                                unit(ahead, q, j, base + 3 * j, rounds, U_E * e + j)
                            continue
                        with act.Fori(0, (hi_u - lo_u) // 2) as it:
                            for j in range(lo_u, lo_u + 2):
                                unit(None, q, -1, base + 3 * j, rounds + it, U_E * e + j + it * 2)

                for g in range(2):
                    gathered(0, g, g + 1, g)
                advance(first_chunk + LEAD - 1)
                expert(0, 0, 0)
                with act.Fori(0, (NE - 2) // 2) as pair:
                    for s in range(2):
                        expert(pair * 2 + 1 + s, 1 - s, (pair * 2 + 1 + s) * ROUNDS_E)
                expert(NE - 1, 1, (NE - 1) * ROUNDS_E, last=True)
                outputs(1, (used, first_chunk + 3 * U_MOE))
                cursor[0] = first_chunk + 3 * U_MOE - 1 + LEAD

            def heads(stage, work, last):
                soft = [kind != "ret" for kind, _ in work]
                for i in range(len(work) + 1):
                    if i < len(work):
                        d = QD if work[i][0] == "mla" else HD
                        act.wait_ge(*at(stage, "tq", i + 1))
                        act.activation(qkt[0:d, i % 2, :], ps[i % 2][0:d, :], ACT.Copy).then_inc(sem("qk"), 1)
                    if i >= 1 and soft[i - 1]:
                        n = i - 1
                        act.wait_ge(*at(stage, "mx", sum(soft[:i])))
                        act.activation(prob[:, n % 2, 0:P], prob[:, n % 2, 0:P], ACT.Exp, bias=nmax[:, n, 0:1],
                                       accum_out=rsum[:, n, 0:1])
                        act.activation(prob[:, n % 2, P:3 * P], prob[:, n % 2, P:3 * P], ACT.Exp, bias=nmax[:, n, 1:2],
                                       accum_out=rsum[:, n, 1:2]).then_inc(sem("p"), 1)
                    if i == 1:
                        advance(last + LEAD)
                    if stage != "dil" and i == ROOTS_AT:
                        act.wait_ge(sem(f"ret{stage[2:]}_var"), 1)
                        act.activation(gs[:, 2, 0:10], gs[:, 1, 0:10], ACT.Sqrt, bias=eps[:, 1:2], scale=1.0 / HD).then_inc(
                            sem("sd"), 1)
                        act.wait_ge(*at(stage, "o", RET_H + MOBA_H))
                        for t in range(T):
                            m = act.activation(h[:, t, C_RK:C_RK + 320], r[:, t, O_MOBA:D], ACT.Square,
                                               accum_out=ss[:, 2 + t:3 + t])
                        link(m)
                        act.activation(sd[:, 2:4], ss[:, 2:4], ACT.Sqrt, bias=eps[:, 1:2], scale=1.0 / 320).then_inc(
                            sem("sd"), 1)
                    if stage == "dil" and i == GATING_ROOTS_AT:
                        act.wait_ge(sem("ya"), 1)
                        for t in range(T):
                            m = act.activation(h[:, t, 0:512], r[:, t, 0:512], ACT.Square, accum_out=ss[:, t:t + 1])
                        link(m)
                        act.activation(sd[:, 0:2], ss[:, 0:2], ACT.Sqrt, bias=eps[:, 1:2], scale=1.0 / 512).then_inc(
                            sem("sd"), 1)

            act.wait_ge(sem("eps_set"), 2)
            ln_roots("emb", (sem("x_in1"), 16))
            advance(LEAD - 1)
            split_x("emb")
            act.wait_ge(sem("cols_in"), 16)
            for l in range(DEPTH):
                st = f"in{l}"
                for g in range(6):
                    last = AT[st] + 2 * g + (1 if g < 5 else 0)
                    advance(last + LEAD)
                    width = 512 if g < 5 else 96
                    evac(st, g, 0, h[:, 0, 512 * g:512 * g + width], width, 2 * (g % 2))
                    if g == 0:
                        act.wait_ge(*at(st, "ev1", 1))
                        act.wait_ge(*at(st, "ev0", 1))
                        for t in range(T):
                            link(act.activation(prob[:, t, 0:256], h[:, t, 0:256], ACT.Square, accum_out=ss[:, t:t + 1]))
                            link(act.activation(prob[:, t, 256:384], h[:, t, 256:384], ACT.Square,
                                                accum_out=ss[:, 2 + t:3 + t]))
                        link(act.activation(sd[:, 0:2], ss[:, 0:2], ACT.Sqrt, bias=eps[:, 1:2], scale=1.0 / 256))
                        act.activation(sd[:, 2:4], ss[:, 2:4], ACT.Sqrt, bias=eps[:, 1:2], scale=1.0 / 128).then_inc(
                            sem("sd"), 1)
                    if g == LATENTS_AT - 1:
                        split_x(f"lat{l}", COLS[f"q{l}"], 3, hth, (4, 5))
                last = AT[f"uq{l}"]
                act.wait_ge(*at(st, "ev0", 6))
                act.wait_ge(*at(st, "ev1", 6))
                advance(last + LEAD)
                act.activation(h[:, :, C_RG:C_RG + 320], h[:, :, C_RG:C_RG + 320], ACT.Silu).then_inc(sem(f"gate{l}"), 1)
                act.wait_ge(used, AT[f"uq{l}"] + 1)
                for t in range(T):
                    for half in range(2):
                        act.activation(qc[:, t, 3 * half:3 * half + 3, :],
                                       ps[2 * t + half][:, 0:288].rearrange("p (h d) -> p h d", h=3),
                                       ACT.Copy).then_inc(sem("ev"), 1)
                heads(f"at{l}", heads_of_layer(), last)
                act.wait_ge(*at(f"at{l}", "o", 16))
                for t in range(T):
                    m = act.activation(prob[:, t, 0:384], r[:, t, 0:384], ACT.Square, accum_out=ss[:, t:t + 1])
                link(m)
                act.activation(sd[:, 0:2], ss[:, 0:2], ACT.Sqrt, bias=eps[:, 1:2], scale=1.0 / 384).then_inc(sem("sd"), 1)
                split_x(f"mix{l}", COLS[f"mix{l}"])
                advance(AT[f"o{l}"] + 3 + LEAD)
                ln_roots(f"ln1_{l}", at(f"o{l}", "resid", 4))
                split_x(f"ln1_{l}")
                if l == 1:
                    advance(AT["router"] + LEAD)
                    act.wait_ge(sem("rt_max"), 1)
                    for t in range(T):
                        act.activation(lg[:, 1, t, :], lg[:, 0, t, :], ACT.Exp, bias=small[:, 0, t:t + 1]).then_inc(
                            sem("rt_exp"), 1)
                if l == 0:
                    ffn("f0", U_FF)
                else:
                    act.wait_ge(sem("rt_flag"), 1)
                    overfull = act.value_load(flag[0:1, 0:1], min_val=0, max_val=1)
                    n = cursor[0]
                    with act.If(overfull == 0):
                        experts()
                    with act.Else():
                        cursor[0] = n
                        ffn("f1", U_MOE)
                ln_roots(f"ln2_{l}", at(f"f{l}", "resid", 4))
                if l == 0:
                    split_x(f"ln2_{l}")

            def rms_of_x(stage, before):
                rms_roots(stage, lambda t: at(before, "resid", 2 * t + 2), r, x)

            rms_roots("n1", lambda t: at("ln2_1", "x", t + 1), r, x)
            split_x("n1", COLS["ffn1"])
            ffn("f2", U_FF)
            act.wait_ge(sem("angle"), 1)
            act.activation(rot[:, 4], rot[:, 2], ACT.Sin).then_inc(sem("sines"), 1)
            act.activation(rot[:, 5], rot[:, 2], ACT.Sin, scale=0.5).then_inc(sem("sines"), 1)
            rms_of_x("nmix", "f2")
            split_x("nmix", COLS["in2"])
            for g in range(5):
                advance(AT["in2"] + 2 * g + 1 + LEAD)
                evac("in2", g, 0, h[:, 0, 512 * g:512 * g + 512], 512, 2 * (g % 2), ACT.Gelu if g < 2 else ACT.Copy)
                if g < 2:
                    evac("in2", g, 1, h[:, 1, 512 * g:512 * g + 512], 512, 2 * (g % 2) + 1, ACT.Gelu)
            last = AT["in2"] + 9
            act.wait_ge(sem("sgu_var"), 1)
            act.activation(gs[:, 2, :], gs[:, 1, :], ACT.Sqrt, bias=eps[:, 0:1], scale=1.0 / HD).then_inc(sem("sd"), 1)
            act.wait_ge(sem("ws_tr"), 1)
            for b in range(2):
                act.activation(wst[:, 4 * b:4 * b + 4, :], ps[4 + b][:, :].rearrange("p (g j) -> p g j", g=4),
                               ACT.Copy).then_inc(sem("ws_t"), 1)
            heads("dil", [("dil", n) for n in range(DIL_H)], last)
            act.wait_ge(*at("dil", "o", DIL_H))
            for t in range(T):
                m = act.activation(prob[:, t, :], r[:, t, 512:D], ACT.Square, accum_out=ss[:, 2 + t:3 + t])
            link(m)
            act.activation(sd[:, 2:4], ss[:, 2:4], ACT.Sqrt, bias=eps[:, 1:2], scale=1.0 / 512).then_inc(sem("sd"), 1)
            split_x("mix2", COLS["out2"])
            act.wait_ge(sem("mem_in"), 16)
            rms_roots("nmem", None, r, bc)
            advance(AT["out2"] + 3 + LEAD)
            act.wait_ge(used, AT["out2"] + 4)
            split_x("nmem", COLS["mem"])
            rms_of_x("ncross", "out2")
            for j in range(KD):
                advance(AT["wk"] + 2 * (j // 4) + 1 + LEAD)
                act.wait_ge(*tile_done("wk", j))
                act.activation(kt[:, j, :], ps[j][:, 0:S], ACT.Copy).then_inc(sem("ev"), 1)
            for g in range(2):
                advance(AT["wv"] + 2 * g + 1 + LEAD)
                if g == 1:
                    act.wait_ge(used, AT["wv"] + 4)
                    split_x("ncross", COLS["cross"], banks=(4, 5, 6, 7))
                evac("wv", g, 0, xv[:, 0, 512 * g:512 * g + 512], 512, 2 * g)
            for j in range(KD):
                advance(AT["wq"] + 2 * (j // 4) + 1 + LEAD)
                act.wait_ge(*tile_done("wq", j))
                act.activation(qt[:, j, :], ps[j][:, 0:S], ACT.Copy).then_inc(sem("ev"), 1)
            last = AT["wq"] + 3
            for i in range(X_H):
                act.wait_ge(sem("x_mx"), i + 1)
                if i >= 2:
                    act.wait_ge(sem("x_tp"), i - 1)
                for t in range(T):
                    m = act.activation(prob[:, i % 2, t * S:(t + 1) * S], ps[2 + i % 2][:, t * S:(t + 1) * S], ACT.Exp,
                                       bias=nmax[:, i, t:t + 1], scale=X_D ** -0.5, accum_out=rsum[:, i, t:t + 1])
                m.then_inc(sem("x_p"), 1)
                advance(last + 1 + i if i < SPLIT else 0)
            split_x("xo")
            advance(AT["xo"] + 3 + LEAD)
            rms_of_x("n2", "xo")
            split_x("n2", COLS["ffn2"])
            ffn("f3", U_FF)
            rms_of_x("fin", "f3")

        @block.vector
        def _(dve):
            cursor = [0]
            chained = [0]

            def link(ins):
                chained[0] += 1
                ins.then_inc(sem("dve_chain"), 1)
                dve.wait_ge(sem("dve_chain"), chained[0])

            def lo(c):
                dve.wait_ge(hi_done, c.n + 1)
                dve.tensor_tensor(wlo[:, c.split, 0:c.width], raw[:, c.raw, 0:c.width], f32(whi[:, c.split, 0:c.width]),
                                  ALU.subtract).then_inc(lo_done, 1)

            def advance(upto):
                while cursor[0] <= min(upto, NCHUNK - 1):
                    lo(Chunk(cursor[0]))
                    cursor[0] += 1

            def split_x(stage, gain=None, kn=KD, dsth=xth, dstl=xtl, banks=(0, 1, 2, 3)):
                for b in range((kn + 1) // 2):
                    if gain is None:
                        dve.wait_ge(*at(stage, "xh", b + 1))
                        dve.tensor_tensor(dstl[:, 2 * b:2 * b + 2, :], ps[banks[b]][:, :].rearrange("p (k s) -> p k s", k=2),
                                          f32(dsth[:, 2 * b:2 * b + 2, :]), ALU.subtract).then_inc(sem("xt"), 1)
                        continue
                    n = min(2 * b + 2, kn)
                    dve.wait_ge(*at(stage, "xh", n))
                    for k in range(2 * b, n):
                        m = dve.scalar_tensor_tensor(out=dstl[:, k, :], in0=ps[banks[b]][:, (k % 2) * S:(k % 2 + 1) * S],
                                                     scalar=cols[:, gain + k:gain + k + 1], in1=f32(dsth[:, k, :]),
                                                     op0=ALU.mult, op1=ALU.subtract)
                        if kn == KD or k % 2 == 1 or k == kn - 1:
                            m.then_inc(sem("xt"), 1)

            def layer_norm(stage, row, tile):
                for t in range(T):
                    tile(t)
                for a in range(2):
                    m = dve.bn_stats(bn[:, a, :], r[:, 0, 512 * a:512 * a + 512])
                link(m)
                dve.bn_aggr(mv[:, 0, :], bn[:, :, :].rearrange("p a s -> p (a s)")).then_inc(sem("mv"), 1)
                dve.wait_ge(*at(stage, "mv", 1))
                dve.wait_ge(sem(f"rows{row}"), 16)
                for t in range(T):
                    if t == 0:
                        mean, sign = mv[:, 0, 0:1], ALU.subtract
                    else:
                        mean, sign = ss[:, 1:2], ALU.add
                        dve.wait_ge(*at(stage, "sd", T))
                    link(dve.scalar_tensor_tensor(out=r[:, t, :], in0=r[:, t, :], scalar=mean, in1=bc[:, 0, :],
                                                  op0=sign, op1=ALU.mult))
                    dve.wait_ge(*at(stage, "sd", t + 1))
                    link(dve.reciprocal(rstd[:, t:t + 1], sd[:, t:t + 1]))
                    dve.scalar_tensor_tensor(out=x[:, t, :], in0=r[:, t, :], scalar=rstd[:, t:t + 1], in1=bc[:, 1, :],
                                             op0=ALU.mult, op1=ALU.add).then_inc(sem("x"), 1)

            def sums(stage, dst, a, b, t):
                for n in range(2):
                    cut = slice(512 * n, 512 * n + 512)
                    p = ps[4 + 2 * t + n][:, :]
                    if b == 1.0:
                        m = dve.scalar_tensor_tensor(out=dst[:, t, cut], in0=x[:, t, cut], scalar=float(a), in1=p,
                                                     op0=ALU.mult, op1=ALU.add)
                    else:
                        m = dve.scalar_tensor_tensor(out=dst[:, t, cut], in0=p, scalar=float(b), in1=x[:, t, cut],
                                                     op0=ALU.mult, op1=ALU.add)
                    m.then_inc(sem("resid"), 1)
                dve.wait_ge(*at(stage, "resid", 2 * t + 2))

            def residual(stage, done, b):
                dve.wait_ge(*done)
                for t in range(T):
                    sums(stage, x, 1.0, b, t)

            def rms_scale(stage, src, dst=None):
                dst = r if dst is None else dst
                for t in range(T):
                    dve.wait_ge(*at(stage, "sd", t + 1))
                    link(dve.reciprocal(rstd[:, t:t + 1], sd[:, t:t + 1]))
                    dve.tensor_scalar(dst[:, t, :], src[:, t, :], rstd[:, t:t + 1], None, ALU.mult).then_inc(
                        sem("x"), 1)

            def evac(stage, g, t, dst, width, bank):
                dve.wait_ge(*group_done(stage, g, t))
                dve.tensor_copy(dst, ps[bank][:, 0:width]).then_inc(sem("ev1"), 1)

            def ffn(name, units, gated=False):
                first_chunk = AT[name]

                def unit(u, base, it, chunks, pair):
                    n = base + LEAD
                    for j in range(chunks - 1):
                        if n + j < NCHUNK:
                            lo(Chunk(n + j, it))
                    for t in range(T):
                        dve.wait_ge(*at(name, "sg", 2 * u + t + 1))
                        if gated:
                            m = dve.scalar_tensor_tensor(out=hs[:, t, :], in0=sg[:, t, :], scalar=gexp[:, pair, t:t + 1],
                                                         in1=ps[t][:, FU:2 * FU], op0=ALU.mult, op1=ALU.mult)
                        else:
                            m = dve.tensor_tensor(hs[:, t, :], sg[:, t, :], ps[t][:, FU:2 * FU], ALU.mult)
                        m.then_inc(unit_sem(name, "hu"), 1)
                    if n + chunks - 1 < NCHUNK:
                        lo(Chunk(n + chunks - 1, it))
                    dve.wait_ge(*at(name, "hh", u + 1))
                    dve.tensor_tensor(htl[:, 0:2, :], ps[2][:, :].rearrange("p (k s) -> p k s", k=2),
                                      f32(hth[:, 0:2, :]), ALU.subtract).then_inc(unit_sem(name, "ht"), 1)

                advance(first_chunk + LEAD - 1)
                unit(0, first_chunk, 0, 2, 0)
                unit(1, first_chunk + 2, 0, 3, 0)
                loops = (units - 3) // UNROLL
                with dve.Fori(0, loops) as it:
                    for j in range(UNROLL):
                        unit(it * UNROLL + 2 + j, first_chunk + 5 + 3 * j, it, 3, it * (UNROLL // 2) + 1 + j // 2)
                for u in range(2 + loops * UNROLL, units):
                    unit(u, first_chunk + 3 * u - 1, 0, 3, u // 2)
                cursor[0] = first_chunk + 3 * units - 1 + LEAD

            def experts():
                first_chunk = AT["f1"]

                def gathered(q, g, n, bank):
                    dve.wait_ge(sem("e_gh"), n)
                    cut = slice(q * P, (q + 1) * P)
                    dve.tensor_tensor(xtl[:, 4 * g:4 * g + 4, cut], ps[bank][:, :].rearrange("p (k s) -> p k s", k=4),
                                      f32(xth[:, 4 * g:4 * g + 4, cut]), ALU.subtract).then_inc(sem("e_gx"), 1)

                def outputs(e, q, done):
                    if not (isinstance(e, int) and e == 0):
                        dve.wait_ge(sem("e_sc"), e)
                    dve.tensor_copy(spread_now, spread[:, e, :])
                    dve.wait_ge(*done)
                    dve.tensor_copy(r[:, q, 512:D], ps[3][:, :]).then_inc(sem("e_od"), 1)

                def unit(e, q, j, base, rounds, u, chunks=3):
                    n = base + LEAD
                    for i in range(chunks - 1):
                        lo(Chunk(n + i, rounds))
                    dve.wait_ge(sem("e_sg"), u + 1)
                    dve.tensor_tensor(hs[:, 0, :], sg[:, 0, :], ps[0][:, FU:2 * FU], ALU.mult).then_inc(sem("e_h"), 1)
                    if j in GATHER_AT and e is not None:
                        g = GATHER_AT.index(j)
                        gathered(1 - q, g, 2 * (e + 1) + g + 1, 1)
                    lo(Chunk(n + chunks - 1, rounds))
                    dve.wait_ge(sem("e_hh"), u + 1)
                    dve.tensor_tensor(htl[:, 0:2, 0:P], ps[1][:, 0:2 * P].rearrange("p (k s) -> p k s", k=2),
                                      f32(hth[:, 0:2, 0:P]), ALU.subtract).then_inc(sem("e_ht"), 1)
                    if j == 0 and chunks == 3:
                        outputs(e - 1, 1 - q, (used, base + LB * rounds + 3))

                def expert(e, q, rounds, last=False):
                    base = first_chunk - 1
                    ahead = None if last else e
                    if isinstance(e, int) and e == 0:
                        unit(e, q, 0, first_chunk, 0, 0, chunks=2)
                    else:
                        unit(e, q, 0, base, rounds, U_E * e)
                    unit(e, q, 1, base + 3, rounds, U_E * e + 1)
                    for lo_u, hi_u in ((2, 6), (6, 10), (10, U_E)):
                        if lo_u == 6:
                            for j in range(lo_u, hi_u):
                                unit(ahead, q, j, base + 3 * j, rounds, U_E * e + j)
                            continue
                        with dve.Fori(0, (hi_u - lo_u) // 2) as it:
                            for j in range(lo_u, lo_u + 2):
                                unit(None, q, -1, base + 3 * j, rounds + it, U_E * e + j + it * 2)

                def slots_of(e):
                    for t in range(T):
                        m = dve.tensor_scalar(onehot[:, e, t], slots, lg[:, 6, t, e:e + 1], None, ALU.is_equal)
                    return m

                slots_of(0).then_inc(sem("rt_one"), 1)
                advance(first_chunk + LEAD - 1)
                for g in range(2):
                    gathered(0, g, g + 1, g)
                for e in range(NE):
                    if e > 0:
                        slots_of(e)
                    for t in range(T):
                        m = dve.tensor_scalar(gated[:, e, t], slots, lg[:, 6, t, e:e + 1], lg[:, 5, t, e:e + 1],
                                              ALU.is_equal, ALU.mult)
                m.then_inc(sem("rt_gated"), 1)
                expert(0, 0, 0)
                with dve.Fori(0, (NE - 2) // 2) as pair:
                    for s in range(2):
                        expert(pair * 2 + 1 + s, 1 - s, (pair * 2 + 1 + s) * ROUNDS_E)
                expert(NE - 1, 1, (NE - 1) * ROUNDS_E, last=True)
                outputs(NE - 1, 1, (used, first_chunk + 3 * U_MOE))
                cursor[0] = first_chunk + 3 * U_MOE - 1 + LEAD

            def rotate(x1, x2, cos, sin, tmp):
                dve.tensor_tensor(tmp[0], x1, cos, ALU.mult)
                dve.tensor_tensor(tmp[1], x2, sin, ALU.mult)
                dve.tensor_tensor(tmp[2], x1, sin, ALU.mult)
                link(dve.tensor_tensor(tmp[3], x2, cos, ALU.mult))
                dve.tensor_tensor(x1, tmp[0], tmp[1], ALU.subtract)
                m = dve.tensor_tensor(x2, tmp[2], tmp[3], ALU.add)
                link(m)

            ov = r[:, :, O_RET:O_MOBA].rearrange("p t (h d) -> p t h d", d=HD)
            ret_gs = gs[:, :, 0:10].rearrange("p s (t h) -> p s t h", t=T)

            def rotate_queries(l):
                dve.wait_ge(*at(f"uq{l}", "ev", 4))
                for t in range(T):
                    tmp = [r[:, a // 2, 96 * (a % 2):96 * (a % 2) + 96].rearrange("p (h d) -> p h d", d=16)
                           for a in range(4)]
                    cos, sin = (const(c)[:, 16 * t:16 * t + 16].unsqueeze(1).to_broadcast([P, MLA_H, 16])
                                for c in ("cos_a", "sin_a"))
                    rotate(qc[:, t, :, NOPE:NOPE + 16], qc[:, t, :, NOPE + 16:QD], cos, sin, tmp)
                dve.sem_inc(sem(f"rope{l}"), 1)

            def retention_sums(l):
                dve.wait_ge(*at(f"at{l}", "o", RET_H))
                link(dve.tensor_reduce(ret_gs[:, 0], ov, AX, ALU.add))
                link(dve.tensor_scalar(gs[:, 0, 0:10], gs[:, 0, 0:10], 1.0 / HD, None, ALU.mult))
                sq = h[:, :, C_RQ:C_RK].rearrange("p t (h d) -> p t h d", d=HD)
                for t in range(T):
                    m = dve.tensor_tensor(ov[:, t], ov[:, t], ret_gs[:, 0, t].unsqueeze(2).to_broadcast([P, RET_H, HD]),
                                          ALU.subtract)
                link(m)
                link(dve.tensor_tensor(sq, ov, ov, ALU.mult))
                dve.tensor_reduce(ret_gs[:, 1], sq, AX, ALU.add).then_inc(sem(f"ret{l}_var"), 1)

            def retention_norm(l):
                gg = h[:, :, C_RG:C_RG + 320].rearrange("p t (h d) -> p t h d", d=HD)
                dve.wait_ge(*at(f"early{l}", "sd", 1))
                link(dve.reciprocal(gs[:, 3, 0:10], gs[:, 2, 0:10]))
                for t in range(T):
                    m = dve.tensor_tensor(ov[:, t], ov[:, t], ret_gs[:, 3, t].unsqueeze(2).to_broadcast([P, RET_H, HD]),
                                          ALU.mult)
                link(m)
                dve.wait_ge(sem(f"gate{l}"), 1)
                dve.tensor_tensor(ov, ov, gg, ALU.mult)

            def scale_part(n, a, b):
                link(dve.reciprocal(rstd[:, n:n + T], sd[:, n:n + T]))
                for t in range(T):
                    m = dve.tensor_scalar(r[:, t, a:b], r[:, t, a:b], rstd[:, n + t:n + t + 1], None, ALU.mult)
                return m

            def heads(stage, work, last):
                soft = [kind != "ret" for kind, _ in work]
                for i in range(1, len(work) + 4):
                    if i - 1 < len(work):
                        n = i - 1
                        kind, hn = work[n]
                        dve.wait_ge(*at(stage, "s", n + 1))
                        if kind == "ret":
                            dve.tensor_tensor(probt[:, n % 2, 0:S], ps[2 + n % 2][:, 0:S], c_ret[:, hn, :], ALU.mult)
                            dve.tensor_tensor(probt[:, n % 2, S:S + P], ps[2 + n % 2][:, S:S + P], c_ret[:, hn, 0:P],
                                              ALU.mult).then_inc(sem("pt"), 1)
                        else:
                            mask = c_moba[:, hn, :] if kind == "moba" else const(kind)
                            scale = QD ** -0.5 if kind == "mla" else HD ** -0.5
                            dve.scalar_tensor_tensor(out=prob[:, n % 2, 0:3 * P], in0=ps[2 + n % 2][:, 0:3 * P], scalar=scale,
                                                     in1=mask, op0=ALU.mult, op1=ALU.add).then_inc(sem("sf"), 1)
                    done = i - 4 if i >= 4 and soft[i - 4] else i - 3
                    if i >= 4 and soft[i - 4]:
                        dve.reciprocal(rinv[:, done, :], rsum[:, done, :]).then_inc(sem("ri"), 1)
                    if 0 <= i - 3 < len(work) and soft[i - 3]:
                        n = i - 3
                        dve.wait_ge(*at(stage, "tp", sum(soft[:n + 1])))
                        dve.tensor_copy(probt[:, n % 2, 0:3 * P], ps[4 + n % 2][:, 0:3 * P]).then_inc(sem("pt"), 1)
                    if i - 1 < len(work) and soft[i - 1]:
                        n = i - 1
                        dve.wait_ge(*at(stage, "sf", sum(soft[:n + 1])))
                        dve.tensor_reduce(nmax[:, n, 0:1], prob[:, n % 2, 0:P], AX, ALU.max, negate=True)
                        dve.tensor_reduce(nmax[:, n, 1:2], prob[:, n % 2, P:3 * P], AX, ALU.max, negate=True).then_inc(
                            sem("mx"), 1)
                    if i >= 4 and soft[i - 4] or 0 <= i - 3 < len(work) and not soft[i - 3]:
                        n = done
                        kind, hn = work[n]
                        col = {"ret": O_RET, "moba": O_MOBA, "mla": 0, "dil": 512}[kind] + HD * hn
                        dve.wait_ge(*at(stage, "od", n + 1))
                        if kind == "ret":
                            dve.tensor_copy(r[:, :, col:col + HD], ps[6 + n % 2][:, 0:2 * HD].rearrange(
                                "p (t d) -> p t d", t=T)).then_inc(sem("o"), 1)
                        else:
                            dve.wait_ge(*at(stage, "ri", sum(soft[:n + 1])))
                            for t in range(T):
                                m = dve.tensor_scalar(r[:, t, col:col + HD], ps[6 + n % 2][:, t * HD:(t + 1) * HD],
                                                      rinv[:, n, t:t + 1], None, ALU.mult)
                            m.then_inc(sem("o"), 1)
                    if i == 2:
                        advance(last + LEAD)
                    if stage != "dil":
                        if i == QUERIES_AT:
                            rotate_queries(int(stage[2:]))
                        if i == RET_SUMS_AT:
                            retention_sums(int(stage[2:]))
                        if i == SCALE_AT:
                            retention_norm(int(stage[2:]))
                            dve.wait_ge(*at(f"early{stage[2:]}", "sd", 2))
                            scale_part(2, O_MOBA, D)
                    elif i == GATING_SCALE_AT:
                        dve.wait_ge(*at("mixa", "sd", 1))
                        scale_part(0, 0, 512)

            layer_norm("emb", 0, lambda t: dve.wait_ge(sem(f"x_in{t}"), 16))
            split_x("emb")
            advance(LEAD - 1)
            dve.wait_ge(sem("cols_in"), 16)
            dve.wait_ge(sem("const_in"), 16)
            for l in range(DEPTH):
                st = f"in{l}"
                for g in range(6):
                    last = AT[st] + 2 * g + (1 if g < 5 else 0)
                    advance(last + LEAD)
                    width = 512 if g < 5 else 96
                    evac(st, g, 1, h[:, 1, 512 * g:512 * g + width], width, 2 * (g % 2) + 1)
                    if g == 1:
                        dve.wait_ge(*at(f"lat{l}", "sd", 1))
                        link(dve.reciprocal(rstd[:, :], sd[:, :]))
                        for t in range(T):
                            dve.tensor_scalar(h[:, t, 0:256], h[:, t, 0:256], rstd[:, t:t + 1], None, ALU.mult)
                            dve.tensor_scalar(h[:, t, 256:384], h[:, t, 256:384], rstd[:, 2 + t:3 + t], None,
                                              ALU.mult).then_inc(sem("x"), 1)
                    if g == 3:
                        dve.wait_ge(*at(st, "ev0", 3))
                        dve.wait_ge(*at(st, "ev1", 3))
                        for t in range(T):
                            v = h[:, t, C_RQ:C_RV].rearrange("p (h d) -> p h d", d=HD)
                            tmp = [r[:, a // 2, 320 * (a % 2):320 * (a % 2) + 320].rearrange("p (h d) -> p h d", d=32)
                                   for a in range(4)]
                            cos, sin = (const(c)[:, 32 * t:32 * t + 32].unsqueeze(1).to_broadcast([P, 10, 32])
                                        for c in ("cos_b", "sin_b"))
                            rotate(v[:, :, 0:32], v[:, :, 32:64], cos, sin, tmp)
                        v = h[:, :, C_ROPE:C_RQ]
                        tmp = [small[:, 2 * a:2 * a + 2, :] for a in range(4)]
                        cos, sin = (const(c).rearrange("p (t d) -> p t d", t=T) for c in ("cos_a", "sin_a"))
                        rotate(v[:, :, 0:16], v[:, :, 16:32], cos, sin, tmp)
                        dve.sem_inc(sem(f"ret{l}_qk"), 1)
                    if g == LATENTS_AT - 1:
                        split_x(f"lat{l}", COLS[f"q{l}"], 3, hth, htl, (4, 5))
                last = AT[f"uq{l}"]
                advance(last + LEAD)
                dve.wait_ge(used, AT[f"ukv{l}"] + 1)
                for t in range(T):
                    for half in range(2):
                        kv = ps[4 + 2 * t + half][:, 0:384].rearrange("p (h d) -> p h d", h=3)
                        dve.tensor_copy(kc[:, t, 3 * half:3 * half + 3, 0:NOPE], kv[:, :, 0:NOPE])
                        dve.tensor_copy(vc[:, t, 3 * half:3 * half + 3, :], kv[:, :, NOPE:])
                    link(dve.tensor_copy(kc[:, t, :, NOPE:QD],
                                         h[:, t, C_ROPE:C_RQ].unsqueeze(1).to_broadcast([P, MLA_H, ROPE])))
                dve.sem_inc(sem(f"kv{l}"), 1)
                heads(f"at{l}", heads_of_layer(), last)
                dve.wait_ge(*at(f"mix{l}", "sd", 1))
                link(dve.reciprocal(rstd[:, 0:T], sd[:, 0:T]))
                for t in range(T):
                    dve.tensor_scalar(r[:, t, 0:384], r[:, t, 0:384], rstd[:, t:t + 1], None, ALU.mult).then_inc(sem("x"), 1)
                split_x(f"mix{l}", COLS[f"mix{l}"])
                advance(AT[f"o{l}"] + 3 + LEAD)
                dve.wait_ge(used, AT[f"o{l}"] + 4)
                layer_norm(f"ln1_{l}", 2 + 4 * l, lambda t: sums(f"o{l}", r, ALPHA, 1.0, t))
                split_x(f"ln1_{l}")
                if l == 1:
                    advance(AT["router"] + LEAD)
                    dve.wait_ge(used, AT["router"] + 1)
                    link(dve.tensor_copy(lg[:, 0], ps[3][:, 0:T * NE].rearrange("p (t e) -> p t e", t=T)))
                    dve.tensor_reduce(small[:, 0, 0:T], lg[:, 0], AX, ALU.max, negate=True).then_inc(sem("rt_max"), 1)
                    tri8 = const("tri8").rearrange("p (e f) -> p e f", e=NE)
                    for t in range(T):
                        mine = lg[:, 0, t].unsqueeze(2).to_broadcast([P, NE, NE])
                        other = lg[:, 0, t].unsqueeze(1).to_broadcast([P, NE, NE])
                        dve.tensor_tensor(lg3[:, 0, t], other, mine, ALU.is_gt)
                        m = dve.tensor_tensor(lg3[:, 1, t], other, mine, ALU.is_equal)
                    link(m)
                    for t in range(T):
                        m = dve.tensor_tensor(lg3[:, 1, t], lg3[:, 1, t], tri8, ALU.mult)
                    link(m)
                    link(dve.tensor_tensor(lg3[:, 0], lg3[:, 0], lg3[:, 1], ALU.add))
                    link(dve.tensor_reduce(lg[:, 2], lg3[:, 0], AX, ALU.add))
                    dve.tensor_scalar(lg[:, 3], lg[:, 2], 2.0, None, ALU.is_lt).then_inc(sem("rt_sel"), 1)
                    dve.wait_ge(sem("rt_sel"), 1)
                    dve.wait_ge(sem("rt_exp"), T)
                    link(dve.tensor_tensor(lg[:, 4], lg[:, 1], lg[:, 3], ALU.mult))
                    link(dve.tensor_reduce(small[:, 1, 0:T], lg[:, 4], AX, ALU.add))
                    link(dve.reciprocal(small[:, 2, 0:T], small[:, 1, 0:T]))
                    for t in range(T):
                        link(dve.tensor_scalar(lg[:, 5, t], lg[:, 4, t], small[:, 2, t:t + 1], None, ALU.mult))
                        link(dve.tensor_copy(gexp[:, :, t].rearrange("p (e n) -> p e n", e=NE),
                                             lg[:, 5, t].unsqueeze(2).to_broadcast([P, NE, U_MOE // 2 // NE])))
                    dve.wait_ge(sem("rt_rank"), 1)
                    link(dve.scalar_tensor_tensor(out=lg[:, 6], in0=ps[3][:, 32:48].rearrange("p (t e) -> p t e", t=T), scalar=1.0,
                                                  in1=lg[:, 3], op0=ALU.add, op1=ALU.mult))
                    link(dve.tensor_scalar(lg[:, 6], lg[:, 6], -1.0, None, ALU.add))
                    link(dve.tensor_reduce(small[:, 4, 0:1], ps[3][:, 48:56], AX, ALU.max))
                    link(dve.tensor_scalar(flag[:, :], small[:, 4, 0:1], float(P), None, ALU.is_gt))
                    dve.sem_inc(sem("rt_flag"), 1)
                    overfull = dve.value_load(flag[0:1, 0:1], min_val=0, max_val=1)
                    n = cursor[0]
                    with dve.If(overfull == 0):
                        experts()
                        dve.wait_ge(sem("e_sc"), NE)
                    with dve.Else():
                        cursor[0] = n
                        ffn("f1", U_MOE, gated=True)
                        dve.wait_ge(used, AT["f1"] + 3 * U_MOE)
                else:
                    ffn("f0", U_FF)
                    dve.wait_ge(used, AT["f0"] + 3 * U_FF)
                layer_norm(f"ln2_{l}", 4 + 4 * l, lambda t: sums(f"f{l}", r, ALPHA, 1.0, t))
                if l == 0:
                    split_x(f"ln2_{l}")

            rms_scale("n1", x)
            split_x("n1", COLS["ffn1"])
            ffn("f2", U_FF)
            ang, turns, red = rot[:, 0], rot[:, 1], rot[:, 2]
            dve.wait_ge(sem("pos_in"), 16)
            link(dve.tensor_copy(small[:, 3, 0:T], posi[:, :]))
            for t in range(T):
                link(dve.tensor_scalar(ang[:, t], const("inv_freq"), small[:, 3, t:t + 1], None, ALU.mult))
            magic = 1.5 * 2.0 ** 23
            link(dve.tensor_scalar(turns, ang, float(1 / (2 * np.pi)), magic, ALU.mult, ALU.add))
            link(dve.tensor_scalar(turns, turns, magic, None, ALU.subtract))
            two_pi = 2 * np.pi
            p1 = 6.28125
            p2 = float(np.floor((two_pi - p1) * 2 ** 21) / 2 ** 21)
            p3 = float(np.float32(two_pi - p1 - p2))
            link(dve.scalar_tensor_tensor(out=red, in0=turns, scalar=-p1, in1=ang, op0=ALU.mult, op1=ALU.add))
            link(dve.scalar_tensor_tensor(out=red, in0=turns, scalar=-p2, in1=red, op0=ALU.mult, op1=ALU.add))
            link(dve.scalar_tensor_tensor(out=red, in0=turns, scalar=-p3, in1=red, op0=ALU.mult, op1=ALU.add))
            lim = 3.1415925
            dve.tensor_scalar(red, red, lim, -lim, ALU.min, ALU.max).then_inc(sem("angle"), 1)
            residual("f2", (used, AT["f2"] + 3 * U_FF), 0.5)
            dve.wait_ge(sem("sines"), 2)
            cosr, sinr = rot[:, 3], rot[:, 4]
            link(dve.tensor_tensor(rot[:, 5], rot[:, 5], rot[:, 5], ALU.mult))
            link(dve.tensor_scalar(cosr, rot[:, 5], -2.0, 1.0, ALU.mult, ALU.add))
            rms_scale("nmix", x)
            split_x("nmix", COLS["in2"])
            for g in range(5):
                advance(AT["in2"] + 2 * g + 1 + LEAD)
                if g >= 2:
                    evac("in2", g, 1, h[:, 1, 512 * g:512 * g + 512], 512, 2 * (g % 2) + 1)
                if g == 0:
                    dve.wait_ge(sem("ws_in"), 16)
                    dve.tensor_tensor(ws, ws, const("tril").unsqueeze(1).to_broadcast([P, 8, P]), ALU.mult).then_inc(
                        sem("ws_masked"), 1)
                if g == 2:
                    dve.wait_ge(*at("in2", "ev0", 4))
                    dve.wait_ge(sem("rows10"), 16)
                    gv = gs[:, :, :].rearrange("p s (t h) -> p s t h", t=T)
                    for t in range(T):
                        v = h[:, t, 512:1024].rearrange("p (h d) -> p h d", d=HD)
                        sq = r[:, t, 0:512].rearrange("p (h d) -> p h d", d=HD)
                        link(dve.tensor_reduce(gv[:, 0, t], v, AX, ALU.add))
                        link(dve.tensor_scalar(gv[:, 0, t], gv[:, 0, t], 1.0 / HD, None, ALU.mult))
                        link(dve.tensor_tensor(v, v, gv[:, 0, t].unsqueeze(2).to_broadcast([P, 8, HD]), ALU.subtract))
                        link(dve.tensor_tensor(sq, v, v, ALU.mult))
                        m = dve.tensor_reduce(gv[:, 1, t], sq, AX, ALU.add)
                        if t == 0:
                            link(m)
                    m.then_inc(sem("sgu_var"), 1)
            last = AT["in2"] + 9
            dve.wait_ge(*at("sgu", "sd", 1))
            link(dve.reciprocal(gs[:, 3, :], gs[:, 2, :]))
            for t in range(T):
                v = h[:, t, 512:1024].rearrange("p (h d) -> p h d", d=HD)
                link(dve.tensor_tensor(v, v, gv[:, 3, t].unsqueeze(2).to_broadcast([P, 8, HD]), ALU.mult))
                link(dve.tensor_tensor(h[:, t, 512:1024], h[:, t, 512:1024], bc[:, 0, 0:512], ALU.mult))
                m = dve.tensor_tensor(h[:, t, 512:1024], h[:, t, 512:1024], bc[:, 0, 512:1024], ALU.add)
                if t == 0:
                    link(m)
            m.then_inc(sem("v_norm"), 1)
            dve.wait_ge(*at("in2", "ev0", 7))
            dve.wait_ge(*at("in2", "ev1", 3))
            for t in range(T):
                v = h[:, t, 1024:2048].rearrange("p (h d) -> p h d", d=HD)
                tmp = [r[:, 0, 512 + P * a:512 + P * (a + 1)].rearrange("p (h d) -> p h d", d=8) for a in range(4)]
                cos, sin = (c[:, t].unsqueeze(1).to_broadcast([P, 16, 8]) for c in (cosr, sinr))
                rotate(v[:, :, 0:8], v[:, :, 8:16], cos, sin, tmp)
            dve.sem_inc(sem("rot_done"), 1)
            dve.wait_ge(sem("mixed"), 1)
            for g in range(8):
                m = dve.scalar_tensor_tensor(
                    out=r[:, :, HD * g:HD * (g + 1)],
                    in0=ps[6 + g // 4][:, (g % 4) * P:(g % 4 + 1) * P].rearrange("p (t d) -> p t d", t=T),
                    scalar=cols[:, COLS["b_s"] + g:COLS["b_s"] + g + 1], in1=h[:, :, HD * g:HD * (g + 1)],
                    op0=ALU.add, op1=ALU.mult)
            m.then_inc(sem("ya"), 1)
            heads("dil", [("dil", n) for n in range(DIL_H)], last)
            dve.wait_ge(*at("mix2", "sd", 1))
            link(dve.reciprocal(rstd[:, 2:4], sd[:, 2:4]))
            for t in range(T):
                dve.tensor_scalar(r[:, t, 512:D], r[:, t, 512:D], rstd[:, 2 + t:3 + t], None, ALU.mult).then_inc(
                    sem("x"), 1)
            split_x("mix2", COLS["out2"])
            rms_scale("nmem", bc, bc)
            advance(AT["out2"] + 3 + LEAD)
            split_x("nmem", COLS["mem"])
            residual("out2", (used, AT["out2"] + 4), 1.0)
            rms_scale("ncross", x)
            advance(AT["wk"] + 3 + LEAD)
            for g in range(2):
                advance(AT["wv"] + 2 * g + 1 + LEAD)
                if g == 1:
                    split_x("ncross", COLS["cross"], banks=(4, 5, 6, 7))
                evac("wv", g, 1, xv[:, 1, 512 * g:512 * g + 512], 512, 2 * g + 1)
            last = AT["wq"] + 3
            advance(last + LEAD)
            for i in range(X_H + 2):
                if i < X_H:
                    dve.wait_ge(sem("x_s"), i + 1)
                    link(dve.tensor_reduce(nmax[:, i, :], ps[2 + i % 2][:, :].rearrange("p (t m) -> p t m", t=T), AX, ALU.max,
                                           negate=True))
                    dve.tensor_scalar(nmax[:, i, :], nmax[:, i, :], X_D ** -0.5, None, ALU.mult).then_inc(sem("x_mx"), 1)
                if 1 <= i < X_H + 1:
                    n = i - 1
                    dve.wait_ge(sem("x_tp"), n + 1)
                    if n >= 2:
                        dve.wait_ge(sem("x_od"), n - 1)
                    dve.tensor_copy(probt[:, n % 2, :], ps[4 + n % 2][:, :]).then_inc(sem("x_pt"), 1)
                if i >= 2:
                    n = i - 2
                    dve.wait_ge(sem("x_od"), n + 1)
                    link(dve.reciprocal(rinv[:, n, :], rsum[:, n, :]))
                    for t in range(T):
                        m = dve.tensor_scalar(bc[:, t, n * X_D:(n + 1) * X_D], ps[6 + n % 2][:, t * X_D:(t + 1) * X_D],
                                              rinv[:, n, t:t + 1], None, ALU.mult)
                        if n < X_H - 1 and t == T - 1:
                            m.then_inc(sem("x_o"), 1)
                        if n == X_H - 1:
                            m.then_inc(sem("x"), 1)
                advance(last + 1 + i if i < SPLIT else 0)
            split_x("xo")
            advance(AT["xo"] + 3 + LEAD)
            residual("xo", (used, AT["xo"] + 4), 1.0)
            rms_scale("n2", x)
            split_x("n2", COLS["ffn2"])
            ffn("f3", U_FF)
            residual("f3", (used, AT["f3"] + 3 * U_FF), 0.5)
            dve.wait_ge(sem("rows11"), 16)
            for t in range(T):
                dve.wait_ge(*at("fin", "sd", t + 1))
                link(dve.reciprocal(rstd[:, t:t + 1], sd[:, t:t + 1]))
                dve.scalar_tensor_tensor(out=r[:, t, :], in0=x[:, t, :], scalar=rstd[:, t:t + 1], in1=bc[:, 0, :],
                                         op0=ALU.mult, op1=ALU.mult).then_inc(sem("final"), 1)


def shape_constants():
    f = np.float32
    i = np.arange(S)[:, None]
    j = np.arange(S)[None, :]
    parts = {}
    log_gamma = np.log(f(1.0) - f(2.0) ** (-f(5.0) - np.arange(RET_H, dtype=f)))
    dist = np.maximum(i.T - np.arange(P)[:, None], 0).astype(f)
    decay = np.exp(log_gamma[:, None, None] * dist) * (i.T >= np.arange(P)[:, None]) * f(HD ** -0.5)
    parts["ret"] = decay.transpose(1, 0, 2)

    def tiles(m):
        return np.concatenate([m[0:P, 0:P], m[P:S, :]], axis=1)

    causal = np.where(j <= i, 0.0, NEG)
    parts["mla"] = tiles(causal)
    slopes = f(2.0) ** (f(-8.0) * (np.arange(MOBA_H, dtype=f) + 1) / f(MOBA_H))
    parts["moba"] = np.stack([tiles(np.where(j <= i, -s * (i - j).astype(f), NEG)) for s in slopes], axis=1)
    count = sum(((j <= i) & ((i - j) % d == 0) & (i - j <= w)).astype(f) for w, d in ((128, 1), (512, 4), (2048, 16)))
    parts["dil"] = tiles(np.where(count > 0, np.log(np.maximum(count, 1)), NEG))
    for name, dim in (("a", 32), ("b", 64)):
        inv = f(10000.0) ** (-np.arange(0, dim, 2, dtype=f) / f(dim))
        ang = np.arange(S, dtype=f)[:, None] * inv[None, :]
        for fn, g in (("cos", np.cos), ("sin", np.sin)):
            parts[f"{fn}_{name}"] = g(ang).reshape(T, P, dim // 2).transpose(1, 0, 2)
    inv = f(500000.0) ** (f(-2.0) * np.arange(8, dtype=f) / f(16))
    parts["inv_freq"] = np.broadcast_to(inv, (P, 8))
    parts["ident"] = np.eye(P)
    parts["tril"] = np.tril(np.ones((P, P)))
    parts["tri8"] = np.broadcast_to(np.tril(np.ones((NE, NE)), -1).reshape(1, 64), (P, 64))
    return np.concatenate([np.asarray(parts[n], f).reshape(P, -1) for n, _ in CONST_PARTS], axis=1)


def route_constants():
    n = np.arange(P)
    parts = [n[:, None] < n[None, :], np.ones((P, P)), np.broadcast_to(n, (P, P)), np.zeros((P, P))]
    return np.concatenate([q.astype(np.float32) for q in parts], axis=1)


def lay_out_stream(a):
    big = np.zeros((NCHUNK, P, CW), np.float32)

    def project(name, w):
        n = AT[name]
        for c in range(0, w.shape[1], 512):
            part = w[:, c:c + 512]
            wide = part.shape[1]
            v = part.reshape(KD, P, wide).transpose(1, 0, 2)
            if wide == 512:
                big[n] = v[:, 0:4].reshape(P, CW)
                big[n + 1] = v[:, 4:8].reshape(P, CW)
                n += 2
            else:
                big[n, :, 0:KD * wide] = v.reshape(P, KD * wide)
                n += 1

    def ffn(name, gate, up, down):
        units = gate.shape[0] * gate.shape[2] // FU
        per = units // gate.shape[0]
        first_chunk = AT[name]
        for u in range(units):
            e, c = u // per, (u % per) * FU
            gu = np.concatenate([gate[e, :, c:c + FU].reshape(KD, P, FU), up[e, :, c:c + FU].reshape(KD, P, FU)], axis=2)
            v = gu.transpose(1, 0, 2)
            first = first_chunk + max(3 * u - 1, 0)
            big[first] = v[:, 0:4].reshape(P, CW)
            big[first + 1] = v[:, 4:8].reshape(P, CW)
            last = first_chunk + (3 * u + 4 if u < units - 1 else 3 * u + 2)
            big[last] = down[e, c:c + FU].reshape(2, P, D).transpose(1, 0, 2).reshape(P, CW)

    for l in range(DEPTH):
        project(f"in{l}", a["w_in"][l])
        big[AT[f"uq{l}"], :, 0:1152] = a["w_uq"][l].reshape(2, P, 576).transpose(1, 0, 2).reshape(P, 1152)
        big[AT[f"ukv{l}"], :, 0:768] = a["w_ukv"][l]
        project(f"o{l}", a["w_o"][l])
    ffn("f0", a["ffn_w_gate"], a["ffn_w_up"], a["ffn_w_down"])
    big[AT["router"], :, 0:KD * NE] = a["router"][0].reshape(KD, P, NE).transpose(1, 0, 2).reshape(P, KD * NE)
    ffn("f1", a["exp_w_gate"][0], a["exp_w_up"][0], a["exp_w_down"][0])
    ffn("f2", a["ffn1_w_gate_2"], a["ffn1_w_up_2"], a["ffn1_w_down_2"])
    project("in2", a["w_in_2"][0])
    project("out2", a["w_out_2"][0])
    project("wk", a["cross_wk_2"][0])
    project("wv", a["cross_wv_2"][0])
    project("wq", a["cross_wq_2"][0])
    project("xo", a["cross_wo_2"][0])
    ffn("f3", a["ffn2_w_gate_2"], a["ffn2_w_up_2"], a["ffn2_w_down_2"])
    return big


def kernel(**inputs):
    import concourse.bacc as bacc
    from concourse.bass_utils import run_bass_kernel_spmd

    a = {k: np.asarray(v) for k, v in inputs.items()}
    one = np.ones(O_MOBA - O_RET, np.float32)
    gains = []
    for l in range(DEPTH):
        gains += [a["q_norm_g"][l], a["kv_norm_g"][l], a["beta_mla"][l], one, a["beta_moba"][l]]
    gains += [a["ffn1_norm_2"][0], a["mix_norm_2"][0], a["out_norm_a_2"][0], a["out_norm_b_2"][0], a["cross_norm_2"][0],
              a["mem_norm_2"][0], a["ffn2_norm_2"][0], a["sgu_b_s_2"][0].reshape(-1)]
    rows = [a["ln_emb_g"], a["ln_emb_b"]]
    for l in range(DEPTH):
        rows += [a["ln1_g"][l], a["ln1_b"][l], a["ln2_g"][l], a["ln2_b"][l]]
    rows += [np.concatenate([a["sgu_ln_g_2"][0], a["sgu_ln_b_2"][0]]), a["final_norm_2"]]
    arrays = {
        "stream": lay_out_stream(a),
        "x": a["x"][0],
        "mem": a["mem_2"][0],
        "positions": np.ascontiguousarray(a["positions_2"][0].reshape(T, P).T),
        "consts": shape_constants(),
        "route": route_constants(),
        "cols": np.ascontiguousarray(np.concatenate(gains).reshape(NCOL, P).T),
        "rows": np.stack(rows),
        "spatial": a["sgu_w_s_2"][0],
    }
    nc = bacc.Bacc("TRN2", target_bir_lowering=False, num_devices=1)
    args = [nc.dram_tensor(f"in_{n}", v.shape, mybir.dt.from_np(v.dtype), kind="ExternalInput").ap() for n, v in arrays.items()]
    out = nc.dram_tensor("out", (S, D), F32, kind="ExternalOutput").ap()
    program(nc, *args, out)
    result = run_bass_kernel_spmd(nc, [{f"in_{n}": v for n, v in arrays.items()}], core_ids=[0])
    return result.results[0]["out"].reshape(1, S, D)
```
